# Optimizing a Trainium2 kernel written in Bass

```python
import jax
import jax.numpy as jnp
from jax import lax
import numpy as np

D_MODEL = 1024
BATCH = 1
SEQ = 256
DEPTH = 2
DEC_BATCH = 8
DEC_SEQ = 1
PAST_LEN = 2048
PAGE_SIZE = 128

F32 = jnp.float32
N_EVEN = (DEPTH + 1) // 2
N_ODD = DEPTH // 2

SSD_D_INNER = D_MODEL
SSD_HEAD_DIM = 64
SSD_HEADS = SSD_D_INNER // SSD_HEAD_DIM
SSD_GROUPS = 2
SSD_STATE = 128
SSD_CONV = 4
SSD_CONV_CH = SSD_D_INNER + 2 * SSD_GROUPS * SSD_STATE
RET_HEADS = 8
RET_QK_DIM = 64
RET_V_DIM = 128
RET_QK_WIDTH = RET_HEADS * RET_QK_DIM
RET_V_WIDTH = RET_HEADS * RET_V_DIM
ROPE_BASE = 10000.0
EVEN_SPLITS = (SSD_D_INNER, SSD_CONV_CH, SSD_HEADS, RET_QK_WIDTH, RET_QK_WIDTH, RET_V_WIDTH, RET_V_WIDTH)
EVEN_IN = sum(EVEN_SPLITS)
EVEN_MIX = SSD_D_INNER + RET_V_WIDTH
POOL_WIDTH = D_MODEL // 2
POOL_WINDOWS = (2, 4, 8, 16)
POOL_GROUPS = len(POOL_WINDOWS)
POOL_GROUP_DIM = POOL_WIDTH // POOL_GROUPS
POOL_STATE = max(POOL_WINDOWS) - 1
CONV_WIDTH = D_MODEL // 2
CONV_K = 31
ODD_IN = POOL_WIDTH + 2 * CONV_WIDTH
ODD_MIX = POOL_WIDTH + CONV_WIDTH
MEM_LEN = 256
X_HEADS = 4
X_HEAD_DIM = D_MODEL // X_HEADS
D_FF = 2816
N_EXPERTS = 8
TOP_K = 2
D_FF_EXPERT = 1792

CHUNK = 128
EPS = 1e-6

kernel_name = 'hybrid_ssd_retention_pool_conformer_decoder_step'

def rmsnorm(x, g):
    xf = x.astype(F32)
    y = xf * lax.rsqrt(jnp.mean(xf * xf, axis=-1, keepdims=True) + EPS)
    return (y * g.astype(F32)).astype(x.dtype)

def rms_only(x):
    return x * lax.rsqrt(jnp.mean(x * x, axis=-1, keepdims=True) + EPS)

def rotary(x, pos):
    half = x.shape[-1] // 2
    inv = ROPE_BASE ** (-jnp.arange(half, dtype=F32) / half)
    ang = pos[:, None] * inv[None, :]
    cos = jnp.cos(ang)[None, :, None, :]
    sin = jnp.sin(ang)[None, :, None, :]
    x1, x2 = x[..., :half], x[..., half:]
    return jnp.concatenate([x1 * cos - x2 * sin, x1 * sin + x2 * cos], axis=-1)

def retention_log_decay():
    return jnp.log1p(-jnp.exp2(-5.0 - jnp.arange(RET_HEADS, dtype=F32)))

def causal_dwconv(x_full, w, b):
    c = x_full.shape[-1]
    y = lax.conv_general_dilated(x_full, w[:, None, :].astype(x_full.dtype), (1,), 'VALID',
                                 dimension_numbers=('NWC', 'WIO', 'NWC'), feature_group_count=c)
    return y + b.astype(y.dtype)

def chunked_decay_scan(q, k, v, log_a, h0):
    bsz, seq, nh, dk = q.shape
    dv = v.shape[-1]
    cs = CHUNK if seq % CHUNK == 0 else seq
    nc = seq // cs
    q = q.astype(F32).reshape(bsz, nc, cs, nh, dk)
    k = k.astype(F32).reshape(bsz, nc, cs, nh, dk)
    v = v.astype(F32).reshape(bsz, nc, cs, nh, dv)
    acum = jnp.cumsum(log_a.astype(F32).reshape(bsz, nc, cs, nh), axis=2)
    idx = jnp.arange(cs)
    causal = (idx[:, None] >= idx[None, :])[None, None, :, :, None]
    diff = acum[:, :, :, None, :] - acum[:, :, None, :, :]
    decay = jnp.where(causal, jnp.exp(jnp.minimum(diff, 0.0)), 0.0)
    scores = jnp.einsum('bcihk,bcjhk->bcijh', q, k) * decay
    y_intra = jnp.einsum('bcijh,bcjhv->bcihv', scores, v)
    total = acum[:, :, -1]
    w_end = jnp.exp(total[:, :, None, :] - acum)
    chunk_kv = jnp.einsum('bcjh,bcjhk,bcjhv->bchkv', w_end, k, v)

    def step(h, inp):
        dec, kv = inp
        return jnp.exp(dec)[:, :, None, None] * h + kv, h

    h_last, h_start = lax.scan(step, h0.astype(F32),
                               (jnp.moveaxis(total, 1, 0), jnp.moveaxis(chunk_kv, 1, 0)))
    h_start = jnp.moveaxis(h_start, 0, 1)
    y_inter = jnp.einsum('bcihk,bchkv->bcihv', q, h_start) * jnp.exp(acum)[..., None]
    return (y_intra + y_inter).reshape(bsz, seq, nh, dv), h_last

def even_mixer(h, pos0, conv_st, ssm_st, ret_st, w_in, conv_w, conv_b, dt_bias, a_log, d_skip, gnorm, w_out):
    bsz, seq, _ = h.shape
    offs = [int(o) for o in np.cumsum(EVEN_SPLITS)[:-1]]
    z, xbc, dt, q, k, v, g = jnp.split(h @ w_in, offs, axis=-1)
    xbc_full = jnp.concatenate([conv_st.astype(xbc.dtype), xbc], axis=1)
    new_conv = xbc_full[:, -(SSD_CONV - 1):]
    xbc = jax.nn.silu(causal_dwconv(xbc_full, conv_w, conv_b).astype(F32))
    xs, bm, cm = jnp.split(xbc, [SSD_D_INNER, SSD_D_INNER + SSD_GROUPS * SSD_STATE], axis=-1)
    xs = xs.reshape(bsz, seq, SSD_HEADS, SSD_HEAD_DIM)
    rep = SSD_HEADS // SSD_GROUPS
    bm = jnp.repeat(bm.reshape(bsz, seq, SSD_GROUPS, SSD_STATE), rep, axis=2)
    cm = jnp.repeat(cm.reshape(bsz, seq, SSD_GROUPS, SSD_STATE), rep, axis=2)
    dt = jax.nn.softplus(dt.astype(F32) + dt_bias.astype(F32))
    a = -jnp.exp(a_log.astype(F32))
    y, new_ssm = chunked_decay_scan(cm, bm, xs * dt[..., None], dt * a, ssm_st)
    y = y + d_skip.astype(F32)[:, None] * xs
    y = y.reshape(bsz, seq, SSD_D_INNER) * jax.nn.silu(z.astype(F32))
    y = rms_only(y.reshape(bsz, seq, SSD_GROUPS, -1)).reshape(bsz, seq, SSD_D_INNER) * gnorm.astype(F32)
    pos = pos0 + jnp.arange(seq, dtype=F32)
    q = rotary(q.astype(F32).reshape(bsz, seq, RET_HEADS, RET_QK_DIM), pos)
    k = rotary(k.astype(F32).reshape(bsz, seq, RET_HEADS, RET_QK_DIM), pos) * (RET_QK_DIM ** -0.5)
    v = v.astype(F32).reshape(bsz, seq, RET_HEADS, RET_V_DIM)
    log_g = jnp.broadcast_to(retention_log_decay(), (bsz, seq, RET_HEADS))
    o, new_ret = chunked_decay_scan(q, k, v, log_g, ret_st)
    o = rms_only(o).reshape(bsz, seq, RET_V_WIDTH) * jax.nn.silu(g.astype(F32))
    mixed = jnp.concatenate([y, o], axis=-1).astype(h.dtype)
    return (mixed @ w_out, new_conv, new_ssm.astype(ssm_st.dtype), new_ret.astype(ret_st.dtype))

def odd_mixer(h, pos0, pool_st, conv_st, w_in, pool_w, pool_scale, cw, cb, cng, cnb, w_out):
    bsz, seq, _ = h.shape
    u, ga, gb = jnp.split(h @ w_in, [POOL_WIDTH, POOL_WIDTH + CONV_WIDTH], axis=-1)
    u_full = jnp.concatenate([pool_st.astype(u.dtype), u], axis=1)
    new_pool = u_full[:, -POOL_STATE:]
    uf = u_full.astype(F32)
    csum = jnp.concatenate([jnp.zeros_like(uf[:, :1]), jnp.cumsum(uf, axis=1)], axis=1)
    end = csum[:, POOL_STATE + 1:]
    pos = pos0 + jnp.arange(seq, dtype=F32)
    parts = []
    for gi, w in enumerate(POOL_WINDOWS):
        sl = slice(gi * POOL_GROUP_DIM, (gi + 1) * POOL_GROUP_DIM)
        start = csum[:, POOL_STATE + 1 - w:POOL_STATE + 1 - w + seq, sl]
        cnt = jnp.minimum(pos + 1.0, float(w))[None, :, None]
        parts.append((end[..., sl] - start) / cnt)
    pooled = jnp.concatenate(parts, axis=-1) - u.astype(F32)
    pooled = jnp.einsum('blgc,gcd->blgd', pooled.reshape(bsz, seq, POOL_GROUPS, POOL_GROUP_DIM),
                        pool_w.astype(F32)).reshape(bsz, seq, POOL_WIDTH) * pool_scale.astype(F32)
    glu = ga * jax.nn.sigmoid(gb)
    g_full = jnp.concatenate([conv_st.astype(glu.dtype), glu], axis=1)
    new_conv = g_full[:, -(CONV_K - 1):]
    c = causal_dwconv(g_full, cw, cb).astype(F32)
    mu = jnp.mean(c, axis=-1, keepdims=True)
    var = jnp.mean(jnp.square(c - mu), axis=-1, keepdims=True)
    c = jax.nn.silu((c - mu) * lax.rsqrt(var + EPS) * cng.astype(F32) + cnb.astype(F32))
    mixed = jnp.concatenate([pooled, c], axis=-1).astype(h.dtype)
    return (mixed @ w_out, new_pool, new_conv)

def mem_kv(mem, g, wk, wv):
    bsz, m_len, _ = mem.shape
    m = rmsnorm(mem, g)
    return ((m @ wk).reshape(bsz, m_len, X_HEADS, X_HEAD_DIM), (m @ wv).reshape(bsz, m_len, X_HEADS, X_HEAD_DIM))

def cross_attn(h, mk, mv, wq, wo):
    bsz, seq, _ = h.shape
    q = (h @ wq).reshape(bsz, seq, X_HEADS, X_HEAD_DIM).astype(F32)
    s = jnp.einsum('blhd,bmhd->bhlm', q, mk.astype(F32)) * (X_HEAD_DIM ** -0.5)
    p = jax.nn.softmax(s, axis=-1)
    o = jnp.einsum('bhlm,bmhd->blhd', p, mv.astype(F32)).reshape(bsz, seq, X_HEADS * X_HEAD_DIM)
    return o.astype(h.dtype) @ wo

def swiglu(h, w1, w3, w2):
    return (jax.nn.silu(h @ w1) * (h @ w3)) @ w2

def moe(h, rw, rb, w1, w3, w2):
    bsz, seq, d = h.shape
    t = h.reshape(-1, d)
    logits = t.astype(F32) @ rw.astype(F32) + rb.astype(F32)
    top_v, top_i = lax.top_k(logits, TOP_K)
    gates = jax.nn.softmax(top_v, axis=-1)
    combine = jnp.sum(jax.nn.one_hot(top_i, N_EXPERTS, dtype=F32) * gates[..., None], axis=1)
    out = jnp.zeros((t.shape[0], d), F32)
    for e in range(N_EXPERTS):
        out = out + combine[:, e:e + 1] * swiglu(t, w1[e], w3[e], w2[e]).astype(F32)
    return out.astype(h.dtype).reshape(bsz, seq, d)

def trunk(x, pos0, mem_k, mem_v, ssm, ssm_conv, ret, pool, conv, p):
    n_ssm, n_ssm_conv, n_ret, n_pool, n_conv = [], [], [], [], []
    for l in range(DEPTH):
        i = l // 2
        h = rmsnorm(x, p['norm_mix'][l])
        if l % 2 == 0:
            m, c_st, s_st, r_st = even_mixer(h, pos0, ssm_conv[i], ssm[i], ret[i], p['w_in_even'][i],
                                             p['ssd_conv_w'][i], p['ssd_conv_b'][i], p['ssd_dt_bias'][i],
                                             p['ssd_a_log'][i], p['ssd_d'][i], p['ssd_norm'][i], p['w_out_even'][i])
            n_ssm_conv.append(c_st)
            n_ssm.append(s_st)
            n_ret.append(r_st)
        else:
            m, pl_st, cv_st = odd_mixer(h, pos0, pool[i], conv[i], p['w_in_odd'][i], p['pool_w'][i],
                                        p['pool_scale'][i], p['conv_w'][i], p['conv_b'][i],
                                        p['conv_norm_g'][i], p['conv_norm_b'][i], p['w_out_odd'][i])
            n_pool.append(pl_st)
            n_conv.append(cv_st)
        x = x + m
        x = x + cross_attn(rmsnorm(x, p['norm_cross'][l]), mem_k[l], mem_v[l], p['xattn_q'][l], p['xattn_o'][l])
        h = rmsnorm(x, p['norm_ffn'][l])
        if l % 2 == 0:
            x = x + swiglu(h, p['ffn_w1'][i], p['ffn_w3'][i], p['ffn_w2'][i])
        else:
            x = x + moe(h, p['router_w'][i], p['router_b'][i], p['moe_w1'][i], p['moe_w3'][i], p['moe_w2'][i])
    y = rmsnorm(x, p['norm_final'])
    return (y, jnp.stack(n_ssm), jnp.stack(n_ssm_conv), jnp.stack(n_ret), jnp.stack(n_pool), jnp.stack(n_conv))

def setup_inputs(seed: int = 0) -> dict:
    key = jax.random.key(seed)
    keys = iter(jax.random.split(key, 64))

    def nrm(shape, scale=1.0):
        return jax.random.normal(next(keys), shape, F32) * scale

    def dense(shape, fan_in):
        return nrm(shape, fan_in ** -0.5)

    def gain(shape):
        return 1.0 + nrm(shape, 0.1)

    dt0 = jnp.exp(jax.random.uniform(next(keys), (N_EVEN, SSD_HEADS), F32) * (np.log(0.1) - np.log(0.001)) + np.log(0.001))
    return {
        'x_prompt': nrm((BATCH, SEQ, D_MODEL)),
        'x_sample': nrm((DEC_BATCH, DEC_SEQ, D_MODEL)),
        'state_ssm': nrm((N_EVEN, DEC_BATCH, SSD_HEADS, SSD_STATE, SSD_HEAD_DIM)),
        'state_ssm_conv': nrm((N_EVEN, DEC_BATCH, SSD_CONV - 1, SSD_CONV_CH)),
        'state_ret': nrm((N_EVEN, DEC_BATCH, RET_HEADS, RET_QK_DIM, RET_V_DIM)),
        'state_pool': nrm((N_ODD, DEC_BATCH, POOL_STATE, POOL_WIDTH)),
        'state_conv': nrm((N_ODD, DEC_BATCH, CONV_K - 1, CONV_WIDTH)),
        'cache_mem_k': nrm((DEPTH, DEC_BATCH, MEM_LEN, X_HEADS, X_HEAD_DIM)),
        'cache_mem_v': nrm((DEPTH, DEC_BATCH, MEM_LEN, X_HEADS, X_HEAD_DIM)),
        'mem_prompt': nrm((BATCH, MEM_LEN, D_MODEL)),
        'norm_mix': gain((DEPTH, D_MODEL)),
        'norm_cross': gain((DEPTH, D_MODEL)),
        'norm_ffn': gain((DEPTH, D_MODEL)),
        'norm_mem': gain((DEPTH, D_MODEL)),
        'norm_final': gain((D_MODEL,)),
        'w_in_even': dense((N_EVEN, D_MODEL, EVEN_IN), D_MODEL),
        'ssd_conv_w': dense((N_EVEN, SSD_CONV, SSD_CONV_CH), SSD_CONV),
        'ssd_conv_b': nrm((N_EVEN, SSD_CONV_CH), 0.02),
        'ssd_dt_bias': dt0 + jnp.log(-jnp.expm1(-dt0)),
        'ssd_a_log': jnp.log(jax.random.uniform(next(keys), (N_EVEN, SSD_HEADS), F32, 1.0, 16.0)),
        'ssd_d': gain((N_EVEN, SSD_HEADS)),
        'ssd_norm': gain((N_EVEN, SSD_D_INNER)),
        'w_out_even': dense((N_EVEN, EVEN_MIX, D_MODEL), EVEN_MIX),
        'ffn_w1': dense((N_EVEN, D_MODEL, D_FF), D_MODEL),
        'ffn_w3': dense((N_EVEN, D_MODEL, D_FF), D_MODEL),
        'ffn_w2': dense((N_EVEN, D_FF, D_MODEL), D_FF),
        'w_in_odd': dense((N_ODD, D_MODEL, ODD_IN), D_MODEL),
        'pool_w': dense((N_ODD, POOL_GROUPS, POOL_GROUP_DIM, POOL_GROUP_DIM), POOL_GROUP_DIM),
        'pool_scale': gain((N_ODD, POOL_WIDTH)),
        'conv_w': dense((N_ODD, CONV_K, CONV_WIDTH), CONV_K),
        'conv_b': nrm((N_ODD, CONV_WIDTH), 0.02),
        'conv_norm_g': gain((N_ODD, CONV_WIDTH)),
        'conv_norm_b': nrm((N_ODD, CONV_WIDTH), 0.02),
        'w_out_odd': dense((N_ODD, ODD_MIX, D_MODEL), ODD_MIX),
        'router_w': dense((N_ODD, D_MODEL, N_EXPERTS), D_MODEL),
        'router_b': nrm((N_ODD, N_EXPERTS), 0.01),
        'moe_w1': dense((N_ODD, N_EXPERTS, D_MODEL, D_FF_EXPERT), D_MODEL),
        'moe_w3': dense((N_ODD, N_EXPERTS, D_MODEL, D_FF_EXPERT), D_MODEL),
        'moe_w2': dense((N_ODD, N_EXPERTS, D_FF_EXPERT, D_MODEL), D_FF_EXPERT),
        'xattn_q': dense((DEPTH, D_MODEL, X_HEADS * X_HEAD_DIM), D_MODEL),
        'xattn_k': dense((DEPTH, D_MODEL, X_HEADS * X_HEAD_DIM), D_MODEL),
        'xattn_v': dense((DEPTH, D_MODEL, X_HEADS * X_HEAD_DIM), D_MODEL),
        'xattn_o': dense((DEPTH, X_HEADS * X_HEAD_DIM, D_MODEL), X_HEADS * X_HEAD_DIM),
    }

def reference(x_prompt, x_sample, state_ssm, state_ssm_conv, state_ret, state_pool, state_conv,
              cache_mem_k, cache_mem_v, mem_prompt,
              norm_mix, norm_cross, norm_ffn, norm_mem, norm_final,
              w_in_even, ssd_conv_w, ssd_conv_b, ssd_dt_bias, ssd_a_log, ssd_d, ssd_norm, w_out_even,
              ffn_w1, ffn_w3, ffn_w2,
              w_in_odd, pool_w, pool_scale, conv_w, conv_b, conv_norm_g, conv_norm_b, w_out_odd,
              router_w, router_b, moe_w1, moe_w3, moe_w2,
              xattn_q, xattn_k, xattn_v, xattn_o):
    p = dict(norm_mix=norm_mix, norm_cross=norm_cross, norm_ffn=norm_ffn, norm_final=norm_final,
             w_in_even=w_in_even, ssd_conv_w=ssd_conv_w, ssd_conv_b=ssd_conv_b, ssd_dt_bias=ssd_dt_bias,
             ssd_a_log=ssd_a_log, ssd_d=ssd_d, ssd_norm=ssd_norm, w_out_even=w_out_even,
             ffn_w1=ffn_w1, ffn_w3=ffn_w3, ffn_w2=ffn_w2,
             w_in_odd=w_in_odd, pool_w=pool_w, pool_scale=pool_scale, conv_w=conv_w, conv_b=conv_b,
             conv_norm_g=conv_norm_g, conv_norm_b=conv_norm_b, w_out_odd=w_out_odd,
             router_w=router_w, router_b=router_b, moe_w1=moe_w1, moe_w3=moe_w3, moe_w2=moe_w2,
             xattn_q=xattn_q, xattn_o=xattn_o)
    kv = [mem_kv(mem_prompt, norm_mem[l], xattn_k[l], xattn_v[l]) for l in range(DEPTH)]
    mem_k_prompt = jnp.stack([a for a, _ in kv])
    mem_v_prompt = jnp.stack([b for _, b in kv])
    dt_p = x_prompt.dtype
    y_prompt, ssm_p, ssm_conv_p, ret_p, pool_p, conv_p = trunk(
        x_prompt, 0, mem_k_prompt, mem_v_prompt,
        jnp.zeros((N_EVEN, BATCH, SSD_HEADS, SSD_STATE, SSD_HEAD_DIM), dt_p),
        jnp.zeros((N_EVEN, BATCH, SSD_CONV - 1, SSD_CONV_CH), dt_p),
        jnp.zeros((N_EVEN, BATCH, RET_HEADS, RET_QK_DIM, RET_V_DIM), dt_p),
        jnp.zeros((N_ODD, BATCH, POOL_STATE, POOL_WIDTH), dt_p),
        jnp.zeros((N_ODD, BATCH, CONV_K - 1, CONV_WIDTH), dt_p), p)
    y_sample, ssm_s, ssm_conv_s, ret_s, pool_s, conv_s = trunk(
        x_sample, PAST_LEN, cache_mem_k, cache_mem_v,
        state_ssm, state_ssm_conv, state_ret, state_pool, state_conv, p)
    return (y_prompt, y_sample, mem_k_prompt, mem_v_prompt,
            ssm_p, ssm_conv_p, ret_p, pool_p, conv_p,
            ssm_s, ssm_conv_s, ret_s, pool_s, conv_s)


_drawn_inputs = setup_inputs


def setup_inputs(seed=0):
    import zlib

    import numpy as np

    out = dict(_drawn_inputs(seed))
    spreads = {}
    factors = {'norm_cross': 3.376, 'conv_b': 2.808, 'conv_norm_b': 4.242, 'router_b': 6.816}
    for name, (base, spread) in spreads.items():
        noise = np.random.default_rng([zlib.crc32(name.encode()), seed]).standard_normal(out[name].shape)
        drawn = base * np.exp(spread * noise) if base else spread * noise
        out[name] = jnp.asarray(drawn.astype(out[name].dtype))
    for name, factor in factors.items():
        out[name] = (out[name] * factor).astype(out[name].dtype)
    return out
```

```python
from contextlib import ExitStack

import numpy as np

import concourse.bass as bass
from concourse import mybir

F32 = mybir.dt.float32
U32 = mybir.dt.uint32
ALU = mybir.AluOpType
ACT = mybir.ActivationFunctionType
AX = mybir.AxisListType.X

P = 128
DM = 1024
KT = DM // P
NP = 256
NB = 8
T = NP + NB
NC = NP // P
EPS = 1e-6
SH, SD, SG, SN = 16, 64, 2, 128
RH, RK, RV = 8, 64, 128
XT = 12
SCONV = 4
FF = 2816
NE, FE = 8, 1792
CAP = 96
ML, XH = 256, 4
WINDOWS = (2, 4, 8, 16)
PST = max(WINDOWS) - 1
CK = 31
OT = 4
PAST = 2048
ROPE_BASE = 10000.0

RING = 11
SLOT_K, SLOT_N = 8, 256
SLOT = SLOT_K * SLOT_N
BANKS = 8
FT, ET = FF // P, FE // P
KV_SLOTS = 4

PA = dict(mix=0, cross=16, ffn=32, mem=48, final=64, gnorm=72, scw=80)
PB = dict(scb=128, pscale=140, ccb=144, cng=148, cnb=152)
PC = dict(ccw=156)
COL = {**PA, **PB, **PC}
NPAR = 280

CONST = {}


def _add(name, a):
    CONST[name] = np.ascontiguousarray(a, np.float32)


def _constants():
    i = np.arange(P)
    _add("ident", np.eye(P))
    _add("ones", np.ones((P, P)))
    half = RK // 2
    rot = np.zeros((P, P))
    for d in range(P):
        if d % RK < half:
            rot[d + half, d] = -1.0
        else:
            rot[d - half, d] = 1.0
    _add("rot", rot)
    inv = np.float32(ROPE_BASE) ** (-np.arange(half, dtype=np.float32) / np.float32(half))
    pos = np.concatenate([np.arange(NP), np.full(NB, PAST)]).astype(np.float32)
    ang = (pos[None, :] * inv[i % half][:, None]).astype(np.float32)
    for n, s in (("q", 1.0), ("k", RK ** -0.5)):
        _add("cos" + n, np.cos(ang.astype(np.float64)) * s)
        _add("sin" + n, np.sin(ang.astype(np.float64)) * s)
    _add("causal", (i[None, :] >= i[:, None]) * 1.0)
    lg = np.log1p(-np.exp2(-5.0 - np.arange(RH)))
    d = i[None, :] - i[:, None]
    dec = np.where(d >= 0, np.exp(np.minimum(lg[:, None, None] * d, 0.0)), 0.0)
    order = [2 * hh + par for par in range(2) for hh in range(RH // 2)]
    _add("dret", dec[order].transpose(1, 0, 2).reshape(P, RH * P))
    _add("gq", np.exp(lg[order][None, :] * (i[:, None] + 1)))
    _add("wk", np.exp(lg[None, :] * (P - 1 - i[:, None])))
    par = i // RK
    hh = np.arange(RH // 2)
    _add("gchunk", np.exp(lg[2 * hh[None, :] + par[:, None]] * P))
    _add("gone", np.exp(lg[2 * hh[None, :] + par[:, None]]))
    _add("iota", np.tile(np.arange(CAP), (P, 1)))
    cnt = np.stack([1.0 / np.minimum(np.arange(PST + 1) + 1.0, w) for w in WINDOWS])
    _add("invcnt", np.tile(cnt.reshape(1, -1), (P, 1)))


_constants()
EVEN_CONST = ("rot", "cosq", "sinq", "cosk", "sink", "dret", "gq", "wk", "gchunk", "gone")
BASE_CONST = ("ident", "ones", "causal", "iota", "invcnt")
CONST_AT = {}
_off = 0
for _n in BASE_CONST + EVEN_CONST:
    CONST_AT[_n] = (_off, CONST[_n].shape[1])
    _off += CONST[_n].shape[1]
N_CONST = _off
N_BASE = sum(CONST[_n].shape[1] for _n in BASE_CONST)
CONST_ARRAY = np.concatenate([CONST[_n] for _n in BASE_CONST + EVEN_CONST], axis=1)


def weight_items(w):
    items = []

    def block(name, wm, n0, n, block_no, chunks):
        for kc, (k0, kn) in enumerate(chunks):
            items.append((name, block_no, kc, wm[k0 * P:(k0 + kn) * P, n0:n0 + n].rearrange("(t p) n -> p t n", p=P)))

    def whole(name, wm, n, chunks):
        for b in range(n // SLOT_N):
            block(name, wm, b * SLOT_N, SLOT_N, b, chunks)

    full = [(0, 8)]
    win = w["w_in_even"][0]
    cols = dict(z=0, xbc=1024, dt=2560, q=2576, k=3088, v=3600, g=4624)
    for name, nb in (("xbc", 6), ("dt", 1), ("z", 4), ("g", 4), ("q", 2), ("k", 2), ("v", 4)):
        for b in range(nb):
            n = SH if name == "dt" else SLOT_N
            block(name, win, cols[name] + b * SLOT_N, n, b, full)
    whole("wout0", w["w_out_even"][0], DM, [(0, 8), (8, 8)])

    def cross(l):
        whole(f"xk{l}", w["xattn_k"][l], DM, full)
        whole(f"xv{l}", w["xattn_v"][l], DM, full)
        whole(f"xq{l}", w["xattn_q"][l], DM, full)
        whole(f"xo{l}", w["xattn_o"][l], DM, full)

    cross(0)
    for b in range(FF // SLOT_N):
        block("f1", w["ffn_w1"][0], b * SLOT_N, SLOT_N, b, full)
        block("f3", w["ffn_w3"][0], b * SLOT_N, SLOT_N, b, full)
    whole("f2", w["ffn_w2"][0], DM, [(0, 8), (8, 8), (16, 6)])
    whole("win1", w["w_in_odd"][0], 1536, full)
    whole("wout1", w["w_out_odd"][0], DM, full)
    cross(1)
    return items


def psum_groups():
    g = [("params",), ("cst",)]
    g += [("xT", t) for t in range(KT)]

    def lin(name, n):
        return [(name, t) for t in range(n)]

    g += [("ss", 0)] + lin("xbc", 12) + [("dt", 0)] + lin("z", 8) + lin("g", 8) + lin("q", 4) + lin("k", 4) + lin("v", 8)
    g += [("tail0", j) for j in range(3)]
    g += [("dtT",), ("dbc",), ("Btok",)] + [("xtok", c, j) for c in range(NC) for j in range(2)] + [("CB",)]
    for c in range(NC):
        for gr in range(SG):
            g += [("bc", c, gr, j) for j in range(2)] + [("y", c, gr)]
            if c:
                g += [("yi", gr)]
            g += [("kv", c, gr)]
    g += [("yT", t) for t in range(KT)]
    g += [("eab",), ("xstok", 0), ("xstok", 1)]
    for b in range(NB):
        g += [("xb", b, 0), ("xb", b, 1)]
        if b:
            g += [("ys", b - 1)]
    g += [("ys", NB - 1)]
    g += [("yss", 0), ("yss", 1)]
    g += [("rot", i) for i in range(8)]
    g += [("ktok", c) for c in range(NC)] + [("vtok", c, j) for c in range(NC) for j in range(2)]
    for c in range(NC):
        g += [("rs", c, p) for p in range(2)] + [("ro", c, p) for p in range(2)]
        if c:
            g += [("ri", p) for p in range(2)]
        g += [("rkv", c)]
    g += [("oT", h) for h in range(RH)]
    g += [("vstok", 0), ("vstok", 1)]
    for b in range(NB):
        g += [("vb", b)]
        if b:
            g += [("os", b - 1, p) for p in range(2)]
    g += [("os", NB - 1, p) for p in range(2)]
    g += [("oss", h) for h in range(RH)]
    g += lin("wout0", KT)

    def cross(l):
        r = [("mT", l, j) for j in range(4)] + [("ss", 1 + 4 * l)]
        r += [(f"xk{l}", b, m) for b in range(4) for m in range(2)]
        r += [("KT", l, j) for j in range(4)]
        r += [(f"xv{l}", b, m) for b in range(4) for m in range(2)]
        r += [("ss", 2 + 4 * l)] + lin(f"xq{l}", KT)
        r += [("qs", l, 0), ("qs", l, 1)]
        r += [("S", l, lt, hp) for lt in range(2) for hp in range(2)]
        r += [("PT", l, lt, hp) for lt in range(2) for hp in range(2)]
        r += [("ao", l, t) for t in range(KT)]
        r += [("qb", l, b, j) for b in range(NB) for j in range(2)]
        r += [("sT", l), ("pT", l), ("aos", l)] + lin(f"xo{l}", KT)
        return r

    g += cross(0)
    g += [("ss", 3)]
    for b in range(FF // SLOT_N):
        g += [("f1", 2 * b), ("f1", 2 * b + 1), ("f3", 2 * b), ("f3", 2 * b + 1)]
    g += lin("f2", KT)
    g += [("ost", j) for j in range(3)]
    g += [("ss", 4)] + lin("win1", 12) + [("tail1",), ("tail2",)] + [("pw", i) for i in range(4)] + [("mu",), ("var",)]
    g += lin("wout1", KT)
    g += cross(1)
    g += [("ss", 7), ("logit",), ("rank",)] + [("htok", c, j) for c in range(3) for j in range(2)]
    g += [("selT0",), ("gat0", 0), ("gat0", 1)]
    g += [("idle", i) for i in range(-len(g) % BANKS)]
    return g


def trunk_kernel(nc, w, consts, outs):
    (y_p, y_s, mk_p, mv_p, ssm_p, ssmc_p, ret_p, pool_p, conv_p, ssm_s, ssmc_s, ret_s, pool_s, conv_s) = outs
    items = weight_items(w)
    item_at = {(n, b, kc): i for i, (n, b, kc, _) in enumerate(items)}
    groups = psum_groups()
    G = {k: i for i, k in enumerate(groups)}
    assert len(G) == len(groups)

    ctx = ExitStack()
    with ctx:
        sems = {}

        def sem(name):
            if name not in sems:
                sems[name] = ctx.enter_context(nc.semaphore(name))
            return sems[name]

        def sb(name, shape, dt=F32):
            return ctx.enter_context(nc.sbuf_tensor(name, shape, dt))

        ring = sb("ring", [P, RING, SLOT])
        xT = sb("xT", [P, KT, T])
        hT = sb("hT", [P, KT, T])
        par = sb("par", [P, NPAR])
        cbase = sb("cbase", [P, N_BASE])
        rstd = sb("rstd", [P, T])
        eps = sb("eps", [P, 1])
        small = sb("small", [P, 160])
        arena_n = 25160
        arena = sb("arena", [P, arena_n])
        psum = ctx.enter_context(nc.psum_tensor("psum", [P, BANKS, 512], F32))
        bank_full = [sem(f"bank_full{b}") for b in range(BANKS)]
        bank_free = [sem(f"bank_free{b}") for b in range(BANKS)]
        slot_full = [sem(f"slot_full{s}") for s in range(RING)]
        chunk_used = sem("chunk_used")
        eu, ed, eh = sem("expert_up"), sem("expert_down"), sem("expert_half")
        base_full = [16 * sum(i % RING == s for i in range(len(items))) for s in range(RING)]

        class Region:

            def __init__(self, at=0):
                self.at = at

            def take(self, *shape):
                n = int(np.prod(shape))
                v = view(self.at, *shape)
                self.at += n
                assert self.at <= arena_n, self.at
                return v

        def view(at, *shape):
            n = int(np.prod(shape))
            v = arena[:, at:at + n]
            if len(shape) == 2:
                v = v.rearrange("p (a b) -> p a b", a=shape[0])
            if len(shape) == 3:
                v = v.rearrange("p (a b c) -> p a b c", a=shape[0], b=shape[1])
            return v

        def const(name):
            at, n = CONST_AT[name]
            if name in BASE_CONST:
                return cbase[:, at:at + n]
            return E_const[:, at - N_BASE:at - N_BASE + n]

        R = Region()
        E_const = R.take(N_CONST - N_BASE)
        zg = R.take(16, T)
        xr_at = R.at
        xr = R.take(XT, SCONV - 1 + NP)
        xrs = R.take(XT, NB, SCONV)
        xc = R.take(XT, T)
        qk = R.take(8, T)
        vT = R.take(RH, T)
        xdt = R.take(NC, DM)
        btok_at = R.at
        Btok = R.take(NC, SG * SN)
        SM = R.take(SG * NC, P)
        xdtw_at = R.at
        xdtw = R.take(DM)
        rs2 = view(R.at, 2, T)
        S = R.take(2, 512)
        hst = R.take(SG, 512)
        dtT = R.take(T)
        acT = R.take(T)
        ytok = view(xr_at, NC, DM)
        hb = view(xr_at, 3, DM)
        rb = view(xr_at, 4, 512)
        sqb = view(xr_at, KT, T)
        dtmp = view(xdtw_at, 5, T)
        xstok = view(xdtw_at, DM)
        vstok = view(btok_at, DM)
        vtok = xdt
        ktok = view(xdtw_at, NC, 512)
        otok = hT[:, :, :].rearrange("p a b -> p (a b)")[:, 0:NC * DM].rearrange("p (a b) -> p a b", a=NC)
        tailtok = hT[:, :, :].rearrange("p a b -> p (a b)")[0:11, 0:1536]
        oTt = xc[:, 0:RH, :]
        rst = hst
        tailT0 = R.take(XT, 11)
        tk = R.take(2, 2, SH)
        tot = R.take(NC, SH)
        wend = R.take(NC, SH)
        eac = R.take(SH)
        etot = R.take(SH)
        eab = R.take(NB, SH)
        eaD = R.take(NB, SH)
        ea = R.take(NB)
        dtst = R.take(SH)
        ysum = R.take(KT)
        cst_keep = R.take(XT * NB * (SCONV - 1))
        Dcol = R.take(KT)
        stage_x = view(xr_at, 2, DM)
        stage_s = view(xr_at + 2 * DM, DM)
        stage_c = view(btok_at, 1536)
        R = Region()
        mT = R.take(KT, ML)
        KTt = R.take(KT, ML)
        Vt = R.take(2, DM)
        Kt = R.take(2, DM)
        pr_at = R.at
        Pr = R.take(4, 2, ML)
        PTt = R.take(XH, 2, NP)
        qT = R.take(KT, T)
        oT = R.take(KT, T)
        kv = R.take(KV_SLOTS, 2, DM)
        qstok = view(0, DM)
        sS = R.take(2, NB * XH)
        Ps = R.take(2 * P)
        pTs = R.take(2, NB * XH)
        memtok = view(pr_at, 2, DM)
        memsq = view(pr_at + 2 * DM, KT, ML)
        R = Region()
        hid = R.take(FT, T)
        sil = R.take(2, T)
        up = R.take(OT, PST + NP)
        us = R.take(OT, NB, PST + 1)
        gp = R.take(OT, CK - 1 + NP)
        gs = R.take(OT, NB, CK)
        ga = R.take(OT, T)
        mixo = R.take(2 * OT, T)
        w2t = R.take(PST + NP)
        w4t = R.take(PST + NP)
        pooled = R.take(OT, T)
        csq = R.take(OT, T)
        tl1 = R.take(OT, 23)
        tl2 = R.take(OT, 38)
        st_pool = R.take(512)
        st_conv = R.take(2, 512)
        tok1 = R.take(512)
        tok2 = R.take(512)
        pw = R.take(OT, P)
        prods = R.take(NB, CK)
        R = Region()
        ehid = R.take(ET, CAP)
        esil = R.take(2, CAP)
        hg = R.take(2, KT, CAP)
        htok = R.take(3, DM)
        sel = R.take(3, CAP)
        selg = R.take(3, CAP)
        selT = R.take(2, T)
        ys = R.take(DM)
        rwt = R.take(KT, NE)
        rbt = R.take(NE)
        lg = R.take(3, NE)
        mx = R.take(3, NE)
        idxf = R.take(3, NE)
        comb = R.take(3, NE)
        picked = R.take(3, NE)
        slot = R.take(3, NE)
        gt = R.take(3, 4)
        cnts = R.take(4)
        fin = R.take(3, DM)
        idx = sb("idx", [P, 3, NE], U32)
        rounds = sb("rounds", [P, 2], mybir.dt.int32)

        a_log_t, dt_bias_t, D_row, ea_t = small[0:SH, 0:1], small[0:SH, 1:2], small[0:1, 2:2 + SH], small[0:SH, 20:21]
        nmx, rsum = small[:, 24:32], small[:, 32:40]
        nms, rss = small[0:32, 40:41], small[0:32, 41:42]

        def bank(key):
            return psum[:, G[key] % BANKS, :]

        def full(eng, key):
            eng.wait_ge(bank_full[G[key] % BANKS], G[key] // BANKS + 1)

        def taken(eng, key):
            eng.wait_ge(bank_free[G[key] % BANKS], G[key] // BANKS + 1)

        def gain(name, t):
            return par[:, COL[name] + t:COL[name] + t + 1]

        def slot_left(eng, i):
            name, b, kc, _ = items[i]
            if (name, b, kc + 1) in item_at:
                eng.wait_ge(chunk_used, sum((n, bb, k + 1) in item_at for n, bb, k, _ in items[:i + 1]))
            elif (name, b, 1) in G:
                full(eng, (name, b, 1))
            else:
                full(eng, (name, b if name == "dt" else 2 * b + 1))

        def ssm_stored(eng):
            for j in range(3):
                eng.wait_ge(sem(f"h_out{j}"), 16 * len(range(j, NB, 3)))
            eng.wait_ge(sem("ssm_p_out"), 16)

        def even_stored(eng):
            ssm_stored(eng)
            for j in range(4):
                eng.wait_ge(sem(f"r_out{j}"), 32 * len(range(j, NB, 4)))
            eng.wait_ge(sem("tail0_out"), 32)

        last_in_slot = [max(i for i in range(len(items)) if i % RING == s) for s in range(RING)]
        block = ctx.enter_context(nc.Block())

        def slot_view(i, k, n):
            return ring[:, i % RING, 0:k * n].rearrange("p (k n) -> p k n", k=k)

        @block.sync
        def _(sp):
            for i, (name, b, kc, src) in enumerate(items):
                if i >= RING:
                    slot_left(sp, i - RING)
                k, n = src.shape[1], src.shape[2]
                sp.dma_start(slot_view(i, k, n), src).then_inc(slot_full[i % RING], 16)
            ups = [w[n][0].rearrange("e (t p) n -> p e t n", p=P) for n in ("moe_w1", "moe_w3")]
            down = w["moe_w2"][0].rearrange("e (t p) n -> p e t n", p=P)

            def expert_load(e, j):
                pick = slice(e, e + 1) if isinstance(e, int) else bass.ds(e, 1)
                if j < 14:
                    src, k = ups[j % 2][:, pick, :, (j // 2) * 256:(j // 2 + 1) * 256], 8
                else:
                    q = j - 14
                    src, k = down[:, pick, 7 * (q % 2):7 * (q % 2) + 7, (q // 2) * 256:(q // 2 + 1) * 256], 7
                sp.dma_start(slot_view(j, k, 256), src.rearrange("p e t n -> p (e t) n")).then_inc(slot_full[j % RING], 16)

            def expert_left(n, j):
                if j < 14:
                    sp.wait_ge(eu, n * (2 * ET) + 2 * (j + 1))
                else:
                    sp.wait_ge(eh if j % 2 == 0 else ed, n * 4 + ((j - 14) // 2 + 1))

            for j in range(RING):
                slot_left(sp, last_in_slot[j])
                expert_load(0, j)
            sp.wait_ge(sem("rounds_known"), 1)
            steps = sp.value_load(rounds[0:1, 1:2], min_val=NE - 1, max_val=3 * NE - 1)
            with sp.Fori(0, steps) as n:
                e, e_next = n & (NE - 1), (n + 1) & (NE - 1)
                sp.wait_ge(eu, e + e_next + 1)
                for j in range(RING, 2 * RING):
                    if j != 14:
                        expert_left(n, j - RING + (j == 13))
                    expert_load(e, j)
                for j in range(RING):
                    expert_left(n, j + RING)
                    expert_load(e_next, j)
            for j in range(RING, 2 * RING):
                expert_left(steps, j - RING)
                expert_load(NE - 1, j)

        @block.gpsimd
        def _(pool):
            def load(dst, src, s):
                pool.dma_start(dst, src).then_inc(sem(s), 16)

            stored = [0]

            def store(dst, src):
                pool.dma_start(dst, src).then_inc(sem("stored"), 16)
                stored[0] += 16

            load(cbase[:], consts[:, 0:N_BASE], "consts_in")
            nc.gpsimd.memset(eps[:], EPS).then_inc(sem("eps_set"), 1)
            load(stage_x[:, 0, :], w["x_prompt"][0, 0:P, :], "x_in")
            load(stage_x[:, 1, :], w["x_prompt"][0, P:NP, :], "x_in")
            load(stage_s[0:NB, :], w["x_sample"].rearrange("b s d -> (b s) d"), "x_in")
            prow = zg[:, 0:3, 0:P]

            def rows(name, src, at, n):
                g = 0 if at < 128 else (1 if at < 156 else 2)
                base = (0, 128, 156)[g]
                load(prow[at - base:at - base + n, g, :], src, "params_in")

            def flat(a):
                return a.rearrange("l (t p) -> (l t) p", p=P)

            rows("mix", flat(w["norm_mix"]), PA["mix"], 16)
            rows("cross", flat(w["norm_cross"]), PA["cross"], 16)
            rows("ffn", flat(w["norm_ffn"]), PA["ffn"], 16)
            rows("mem", flat(w["norm_mem"]), PA["mem"], 16)
            rows("final", w["norm_final"].rearrange("(t p) -> t p", p=P), PA["final"], 8)
            rows("gnorm", flat(w["ssd_norm"]), PA["gnorm"], 8)
            rows("scw", w["ssd_conv_w"][0].rearrange("k (t p) -> (k t) p", p=P), PA["scw"], 48)
            rows("scb", flat(w["ssd_conv_b"]), PB["scb"], 12)
            rows("pscale", flat(w["pool_scale"]), PB["pscale"], 4)
            rows("ccb", flat(w["conv_b"]), PB["ccb"], 4)
            rows("cng", flat(w["conv_norm_g"]), PB["cng"], 4)
            rows("cnb", flat(w["conv_norm_b"]), PB["cnb"], 4)
            rows("ccw", w["conv_w"][0].rearrange("k (t p) -> (k t) p", p=P), PC["ccw"], 124)
            load(stage_c[0:24, :], w["state_ssm_conv"][0].rearrange("b s c -> (b s) c"), "cst_in")
            load(a_log_t, w["ssd_a_log"].rearrange("l h -> h l"), "small_in")
            load(dt_bias_t, w["ssd_dt_bias"].rearrange("l h -> h l"), "small_in")
            load(D_row, w["ssd_d"], "small_in")
            load(E_const, consts[:, N_BASE:N_CONST], "econst_in")
            store(ssmc_s[0, :, 0:SCONV - 2, :], w["state_ssm_conv"][0, :, 1:SCONV - 1, :])
            store(pool_s[0, :, 0:PST - 1, :], w["state_pool"][0, :, 1:PST, :])
            store(conv_s[0, :, 0:CK - 2, :], w["state_conv"][0, :, 1:CK - 1, :])

            taken(pool, ("xbc", XT - 1))
            nc.gpsimd.tensor_copy(tailT0[:, :, 0:3], xr[:, :, NP:NP + 3])
            nc.gpsimd.tensor_copy(tailT0[:, :, 3:11], xrs[:, :, :, SCONV - 1]).then_inc(sem("tail0_ready"), 1)
            taken(pool, ("tail0", 2))
            pool.dma_start(ssmc_p[0, 0], tailtok[0:3, :]).then_inc(sem("tail0_out"), 16)
            pool.dma_start(ssmc_s[0, :, SCONV - 2, :], tailtok[3:11, :]).then_inc(sem("tail0_out"), 16)

            taken(pool, ("yT", KT - 1))
            hsem = [sem(f"h_in{j}") for j in range(3)]
            ssm_v = w["state_ssm"][0].rearrange("b h k v -> b k h v")
            ssm_o = ssm_s[0].rearrange("b h k v -> b k h v")
            hdone = [sem(f"h_out{j}") for j in range(3)]

            def hload(b):
                if b >= 3:
                    pool.wait_ge(hdone[b % 3], 16 * (b // 3))
                    full(pool, ("ys", b - 3))
                pool.dma_start(hb[:, b % 3, :].rearrange("p (h v) -> p h v", h=SH), ssm_v[b]).then_inc(hsem[b % 3], 16)

            hload(0)
            hload(1)
            taken(pool, ("eab",))
            for b in range(NB):
                pool.wait_ge(hsem[b % 3], 16 * (b // 3 + 1))
                hv = hb[:, b % 3, :].rearrange("p (h v) -> p h v", h=SH)
                nc.gpsimd.tensor_tensor(hv, hv, eab[:, b, :].unsqueeze(2).to_broadcast([P, SH, SD]), ALU.mult)\
                    .then_inc(sem("h_decayed"), 1)
                if b + 2 < NB:
                    hload(b + 2)
                taken(pool, ("xb", b, 1))
                pool.dma_start(ssm_o[b], hv).then_inc(hdone[b % 3], 16)
            for g in range(SG):
                taken(pool, ("kv", 1, g))
            pool.dma_start(ssm_p[0, 0].rearrange("h k v -> k h v"), hst[:, :, :].rearrange("p g (h v) -> p (g h) v", v=SD))\
                .then_inc(sem("ssm_p_out"), 16)
            taken(pool, ("yss", 1))
            rsem = [sem(f"r_in{j}") for j in range(4)]
            rdone = [sem(f"r_out{j}") for j in range(4)]
            ret_v = w["state_ret"][0].rearrange("b (c r) k v -> b r k c v", r=2)
            ret_o = ret_s[0].rearrange("b (c r) k v -> b r k c v", r=2)

            def rload(b):
                if b >= 4:
                    pool.wait_ge(rdone[b % 4], 32 * (b // 4))
                    full(pool, ("os", b - 4, 1))
                for r in range(2):
                    pool.dma_start(rb[64 * r:64 * r + 64, b % 4, :].rearrange("p (c v) -> p c v", v=RV), ret_v[b, r])\
                        .then_inc(rsem[b % 4], 16)

            rload(0)
            rload(1)
            for b in range(NB):
                pool.wait_ge(rsem[b % 4], 32 * (b // 4 + 1))
                rv = rb[:, b % 4, :].rearrange("p (c v) -> p c v", v=RV)
                nc.gpsimd.tensor_tensor(rv, rv, const("gone").unsqueeze(2).to_broadcast([P, RH // 2, RV]), ALU.mult)\
                    .then_inc(sem("r_decayed"), 1)
                if b + 2 < NB:
                    rload(b + 2)
                taken(pool, ("vb", b))
                for r in range(2):
                    pool.dma_start(ret_o[b, r], rb[64 * r:64 * r + 64, b % 4, :].rearrange("p (c v) -> p c v", v=RV))\
                        .then_inc(rdone[b % 4], 16)
            taken(pool, ("rkv", 1))
            ret_po = ret_p[0, 0].rearrange("(c r) k v -> r k c v", r=2)
            for r in range(2):
                pool.dma_start(ret_po[r], rst[64 * r:64 * r + 64, 0, :].rearrange("p (c v) -> p c v", v=RV))\
                    .then_inc(sem("ret_p_out"), 16)
            even_stored(pool)
            pool.wait_ge(sem("ret_p_out"), 32)

            def cross(l):
                load(memtok[:, 0, :], w["mem_prompt"][0, 0:P, :], "mem_in")
                load(memtok[:, 1, :], w["mem_prompt"][0, P:ML, :], "mem_in")
                ksem = [sem(f"kv_in{j}") for j in range(KV_SLOTS)]
                caches = [w["cache_mem_k"], w["cache_mem_v"]]

                def kvload(n):
                    src = caches[n // NB][l, n % NB].rearrange("(m p) h d -> p m (h d)", p=P)
                    pool.dma_start(kv[:, n % KV_SLOTS, :, :], src).then_inc(ksem[n % KV_SLOTS], 16)

                for n in range(KV_SLOTS):
                    kvload(n)
                taken(pool, (f"xk{l}", 3, 1))
                pool.dma_start(mk_p[l, 0].rearrange("(m p) h d -> p m (h d)", p=P), Kt[:, :, :]).then_inc(sem("kst"), 16)
                taken(pool, (f"xv{l}", 3, 1))
                pool.dma_start(mv_p[l, 0].rearrange("(m p) h d -> p m (h d)", p=P), Vt[:, :, :]).then_inc(sem("vst"), 16)
                for n in range(KV_SLOTS, 2 * NB):
                    old = n - KV_SLOTS
                    if old < NB:
                        taken(pool, ("qb", l, old, 1))
                    else:
                        pool.wait_ge(sem("v_used"), (NB - 1) * l + old - NB + 1)
                    kvload(n)

            taken(pool, ("wout0", KT - 1))
            cross(0)
            taken(pool, ("xo0", KT - 1))
            pool.wait_ge(sem("kst"), 16)
            pool.wait_ge(sem("vst"), 16)
            load(st_pool[0:120, :], w["state_pool"][0].rearrange("b s c -> (b s) c"), "ost_in")
            for j in range(2):
                load(st_conv[0:120, j, :], w["state_conv"][0, 4 * j:4 * j + 4].rearrange("b s c -> (b s) c"), "ost_in")
            load(pw[:, :, :], w["pool_w"][0].rearrange("g c d -> c g d"), "pw_in")
            pool.wait_ge(sem("odd_raw"), 4)
            nc.gpsimd.tensor_copy(tl1[:, :, 0:15], up[:, :, NP:NP + 15])
            nc.gpsimd.tensor_copy(tl1[:, :, 15:23], us[:, :, :, PST])
            nc.gpsimd.tensor_copy(tl2[:, :, 0:30], gp[:, :, NP:NP + 30])
            nc.gpsimd.tensor_copy(tl2[:, :, 30:38], gs[:, :, :, CK - 1]).then_inc(sem("tail1_ready"), 1)
            taken(pool, ("tail2",))
            for dst, src in ((pool_p[0, 0], tok1[0:15, :]), (pool_s[0, :, PST - 1, :], tok1[15:23, :]),
                             (conv_p[0, 0], tok2[0:30, :]), (conv_s[0, :, CK - 2, :], tok2[30:38, :])):
                pool.dma_start(dst, src).then_inc(sem("odd_out"), 16)
            pool.wait_ge(sem("odd_out"), 64)
            taken(pool, ("wout1", KT - 1))
            cross(1)
            taken(pool, ("xo1", KT - 1))
            pool.wait_ge(sem("kst"), 32)
            pool.wait_ge(sem("vst"), 32)
            load(rwt[:, :, :], w["router_w"][0].rearrange("(t p) e -> p t e", p=P), "router_in")
            load(rbt[0:1, :], w["router_b"], "router_in")
            pool.wait_ge(sem("fin_tok"), 3)
            for c in range(NC):
                store(y_p[0, c * P:(c + 1) * P, :], fin[:, c, :])
            store(y_s.rearrange("b s d -> (b s) d"), fin[0:NB, 2, :])
            pool.wait_ge(sem("stored"), stored[0])

        @block.tensor
        def _(pe):
            mm, tr = nc.tensor.matmul, nc.tensor.transpose
            ident, ones = const("ident"), const("ones")
            made = [0]

            def begin(key):
                g = G[key]
                assert g == made[0], (key, g, made[0])
                made[0] += 1
                if g >= BANKS:
                    pe.wait_ge(bank_free[g % BANKS], g // BANKS)
                return psum[:, g % BANKS, :]

            def end(key, ins):
                ins.then_inc(bank_full[G[key] % BANKS], 1)

            def arrived(i):
                pe.wait_ge(slot_full[i % RING], 16 * (i // RING + 1))

            def linear(name, nb, chunks, rhs, width=256, tiles=2):
                for b in range(nb):
                    outs_ = [begin((name, tiles * b + m)) for m in range(tiles)]
                    base = 0
                    for kc, kn in enumerate(chunks):
                        i = item_at[(name, b, kc)]
                        arrived(i)
                        wv = slot_view(i, kn, width)
                        mw = min(P, width)
                        for m in range(tiles):
                            for k in range(kn):
                                ins = mm(outs_[m][0:mw, 0:T], wv[:, k, m * mw:(m + 1) * mw], rhs(base + k),
                                         start=(base + k == 0), stop=(kc == len(chunks) - 1 and k == kn - 1),
                                         skip_group_check=True)
                            if kc == len(chunks) - 1 and m < tiles - 1:
                                end((name, tiles * b + m), ins)
                        if kc < len(chunks) - 1:
                            ins.then_inc(chunk_used, 1)
                        base += kn
                    end((name, tiles * b + tiles - 1), ins)

            def sumsq(key, src, n, width):
                o = begin(key)
                for k in range(n):
                    ins = mm(o[:, 0:width], ones, src(k), start=(k == 0), stop=(k == n - 1))
                end(key, ins)

            pe.wait_ge(sem("consts_in"), 16)
            pe.wait_ge(sem("params_in"), 16 * 13)
            prow = zg[:, 0:3, 0:P]
            o = begin(("params",))
            for g, (at, n) in enumerate(((0, 128), (128, 28), (156, 124))):
                ins = tr(o[:, at:at + n], prow[0:n, g, :], ident[0:n, 0:n])
            end(("params",), ins)
            pe.wait_ge(sem("cst_in"), 16)
            o = begin(("cst",))
            for t in range(XT):
                ins = tr(o[:, 24 * t:24 * t + 24], stage_c[0:24, t * P:(t + 1) * P], ident[0:24, 0:24])
            end(("cst",), ins)
            pe.wait_ge(sem("x_in"), 48)
            for t in range(KT):
                o = begin(("xT", t))
                for c in range(NC):
                    tr(o[:, c * P:(c + 1) * P], stage_x[:, c, t * P:(t + 1) * P], ident)
                end(("xT", t), tr(o[:, NP:T], stage_s[0:NB, t * P:(t + 1) * P], ident[0:NB, 0:NB]))

            def normed(n):
                pe.wait_ge(sem("sq_ready"), n + 1)
                sumsq(("ss", n), lambda k: hT[:, k, :], KT, T)
                pe.wait_ge(sem("h_ready"), n + 1)

            normed(0)
            h_in = lambda k: hT[:, k, :]
            linear("xbc", 6, [8], h_in)
            linear("dt", 1, [8], h_in, width=SH, tiles=1)
            for name, nb in (("z", 4), ("g", 4), ("q", 2), ("k", 2), ("v", 4)):
                linear(name, nb, [8], h_in)

            pe.wait_ge(sem("tail0_ready"), 1)
            for j in range(3):
                o = begin(("tail0", j))
                for t in range(4):
                    ins = tr(o[0:11, t * P:(t + 1) * P], tailT0[:, 4 * j + t, :], ident)
                end(("tail0", j), ins)

            pe.wait_ge(sem("dt_ready"), 1)
            o = begin(("dtT",))
            for n, src in enumerate((dtT, acT)):
                for c in range(NC):
                    tr(o[:, (2 * n + c) * SH:(2 * n + c + 1) * SH], src[0:SH, c * P:(c + 1) * P], ident[0:SH, 0:SH])
            end(("dtT",), tr(o[0:NB, 4 * SH:5 * SH], dtT[0:SH, NP:T], ident[0:SH, 0:SH]))
            pe.wait_ge(sem("small_in"), 48)
            o = begin(("dbc",))
            end(("dbc",), mm(o[:, 0:SH], ones[0:1, :], D_row, start=True, stop=True))
            pe.wait_ge(sem("xc_ready"), XT)
            o = begin(("Btok",))
            for c in range(NC):
                for g in range(SG):
                    ins = tr(o[:, (2 * c + g) * P:(2 * c + g + 1) * P], xc[:, 8 + g, c * P:(c + 1) * P], ident)
            end(("Btok",), ins)
            for c in range(NC):
                for j in range(2):
                    o = begin(("xtok", c, j))
                    for t in range(4):
                        ins = tr(o[:, t * P:(t + 1) * P], xc[:, 4 * j + t, c * P:(c + 1) * P], ident)
                    end(("xtok", c, j), ins)
            o = begin(("CB",))
            for g in range(SG):
                for c in range(NC):
                    ins = mm(o[:, (2 * g + c) * P:(2 * g + c + 1) * P], xc[:, 8 + g, c * P:(c + 1) * P],
                             xc[:, 10 + g, c * P:(c + 1) * P], start=True, stop=True)
            end(("CB",), ins)
            n = 0
            for c in range(NC):
                for g in range(SG):
                    for j in range(2):
                        o = begin(("bc", c, g, j))
                        for q in range(4):
                            h = 8 * g + 4 * j + q
                            ins = mm(o[:, q * P:(q + 1) * P], ident[0:SH, h:h + 1].to_broadcast([SH, P]),
                                     acT[0:SH, c * P:(c + 1) * P], start=True, stop=True)
                        end(("bc", c, g, j), ins)
                    o = begin(("y", c, g))
                    taken(pe, ("xtok", c, g))
                    for j in range(2):
                        n += 1
                        pe.wait_ge(sem("s_ready"), n)
                        for q in range(4):
                            hl = 4 * j + q
                            ins = mm(o[:, hl * SD:(hl + 1) * SD], S[:, j, q * P:(q + 1) * P],
                                     xdt[:, c, (8 * g + hl) * SD:(8 * g + hl + 1) * SD], start=True, stop=True)
                    end(("y", c, g), ins)
                    if c:
                        o = begin(("yi", g))
                        taken(pe, ("kv", 0, g))
                        end(("yi", g), mm(o, xc[:, 10 + g, P:NP], hst[:, g, :], start=True, stop=True))
                    o = begin(("kv", c, g))
                    pe.wait_ge(sem("xdtw_ready"), 2 * c + g + 1)
                    taken(pe, ("Btok",))
                    end(("kv", c, g), mm(o, Btok[:, c, g * P:(g + 1) * P], xdtw[:, g * 512:(g + 1) * 512], start=True, stop=True))
            for c in range(NC):
                for g in range(SG):
                    taken(pe, ("y", c, g))
            for t in range(KT):
                o = begin(("yT", t))
                for c in range(NC):
                    ins = tr(o[:, c * P:(c + 1) * P], ytok[:, c, t * P:(t + 1) * P], ident)
                end(("yT", t), ins)
            pe.wait_ge(sem("ead_ready"), 1)
            o = begin(("eab",))
            end(("eab",), mm(o[:, 0:NB * SH], ones[0:SH, :], eaD[0:SH, :, :].rearrange("p b h -> p (b h)"), start=True, stop=True))
            for j in range(2):
                o = begin(("xstok", j))
                for t in range(4):
                    ins = tr(o[0:NB, t * P:(t + 1) * P], xc[:, 4 * j + t, NP:T], ident)
                end(("xstok", j), ins)

            def sample_y(b):
                o = begin(("ys", b))
                taken(pe, ("xb", b, 1))
                for t in range(KT):
                    ins = mm(o[:, t:t + 1], hb[:, b % 3, t * P:(t + 1) * P], xc[:, 10 + t // 4, NP + b:NP + b + 1],
                             start=True, stop=True)
                end(("ys", b), ins)

            taken(pe, ("xstok", 1))
            taken(pe, ("xstok", 0))
            for b in range(NB):
                for g in range(SG):
                    o = begin(("xb", b, g))
                    end(("xb", b, g), mm(o, ident[0:NB, b:b + 1].to_broadcast([NB, P]), xstok[0:NB, g * 512:(g + 1) * 512],
                                         start=True, stop=True))
                if b:
                    sample_y(b - 1)
            sample_y(NB - 1)
            pe.wait_ge(sem("ysq_ready"), 1)
            for g in range(SG):
                sumsq(("yss", g), lambda k: sqb[:, 4 * g + k, :], 4, T)

            pe.wait_ge(sem("econst_in"), 16)
            for i in range(8):
                o = begin(("rot", i))
                taken(pe, (("q", i) if i < 4 else ("k", i - 4)))
                end(("rot", i), mm(o[:, 0:T], const("rot"), qk[:, i, :], start=True, stop=True))
            pe.wait_ge(sem("rot_done"), 8)
            for c in range(NC):
                o = begin(("ktok", c))
                for t in range(4):
                    ins = tr(o[:, t * P:(t + 1) * P], qk[:, 4 + t, c * P:(c + 1) * P], ident)
                end(("ktok", c), ins)
            for t in range(RH):
                taken(pe, ("v", t))
            for c in range(NC):
                for j in range(2):
                    o = begin(("vtok", c, j))
                    for t in range(4):
                        ins = tr(o[:, t * P:(t + 1) * P], vT[:, 4 * j + t, c * P:(c + 1) * P], ident)
                    end(("vtok", c, j), ins)
            for c in range(NC):
                for p in range(2):
                    o = begin(("rs", c, p))
                    for hh in range(4):
                        ins = mm(o[:, hh * P:(hh + 1) * P], qk[64 * p:64 * p + 64, 4 + hh, c * P:(c + 1) * P],
                                 qk[64 * p:64 * p + 64, hh, c * P:(c + 1) * P], start=True, stop=True)
                    end(("rs", c, p), ins)
                for j in range(2):
                    taken(pe, ("vtok", c, j))
                for p in range(2):
                    o = begin(("ro", c, p))
                    taken(pe, ("rs", c, p))
                    for hh in range(4):
                        h = 2 * hh + p
                        ins = mm(o[:, hh * P:(hh + 1) * P], S[:, p, hh * P:(hh + 1) * P], vtok[:, c, h * RV:(h + 1) * RV],
                                 start=True, stop=True)
                    end(("ro", c, p), ins)
                if c:
                    taken(pe, ("rkv", 0))
                    for p in range(2):
                        o = begin(("ri", p))
                        for hh in range(4):
                            ins = mm(o[:, hh * P:(hh + 1) * P], qk[64 * p:64 * p + 64, hh, P:NP],
                                     rst[64 * p:64 * p + 64, 0, hh * P:(hh + 1) * P], start=True, stop=True)
                        end(("ri", p), ins)
                o = begin(("rkv", c))
                taken(pe, ("ktok", c))
                for hh in range(4):
                    for p in range(2):
                        h = 2 * hh + p
                        ins = mm(o[64 * p:64 * p + 64, hh * P:(hh + 1) * P], ktok[:, c, h * RK:(h + 1) * RK],
                                 vtok[:, c, h * RV:(h + 1) * RV], start=True, stop=True)
                end(("rkv", c), ins)
            for c in range(NC):
                for p in range(2):
                    taken(pe, ("ro", c, p))
            for h in range(RH):
                o = begin(("oT", h))
                at = ((h % 2) * 4 + h // 2) * P
                for c in range(NC):
                    ins = tr(o[:, c * P:(c + 1) * P], otok[:, c, at:at + P], ident)
                end(("oT", h), ins)
            for j in range(2):
                o = begin(("vstok", j))
                for t in range(4):
                    ins = tr(o[0:NB, t * P:(t + 1) * P], vT[:, 4 * j + t, NP:T], ident)
                end(("vstok", j), ins)

            def sample_o(b):
                taken(pe, ("vb", b))
                for p in range(2):
                    o = begin(("os", b, p))
                    for hh in range(4):
                        ins = mm(o[:, hh:hh + 1], rb[64 * p:64 * p + 64, b % 4, hh * P:(hh + 1) * P],
                                 qk[64 * p:64 * p + 64, hh, NP + b:NP + b + 1], start=True, stop=True)
                    end(("os", b, p), ins)

            taken(pe, ("vstok", 1))
            taken(pe, ("vstok", 0))
            vs4 = vstok[0:NB, :].rearrange("p (c r v) -> p c r v", r=2, v=RV)
            for b in range(NB):
                o = begin(("vb", b))
                for p in range(2):
                    ins = mm(o[64 * p:64 * p + 64, :], ident[0:NB, b:b + 1].to_broadcast([NB, 64]), vs4[:, :, p, :],
                             start=True, stop=True)
                end(("vb", b), ins)
                if b:
                    sample_o(b - 1)
            sample_o(NB - 1)
            pe.wait_ge(sem("osq_ready"), 1)
            for h in range(RH):
                sumsq(("oss", h), lambda k: sqb[:, h, :], 1, T)
            pe.wait_ge(sem("mixed_ready"), 1)
            linear("wout0", 4, [8, 8], lambda k: zg[:, k, :])

            def cross(l):
                pe.wait_ge(sem("mem_in"), 32 * (l + 1))
                for j in range(4):
                    o = begin(("mT", l, j))
                    for t in range(2):
                        for m in range(2):
                            ins = tr(o[:, (2 * t + m) * P:(2 * t + m + 1) * P], memtok[:, m, (2 * j + t) * P:(2 * j + t + 1) * P], ident)
                    end(("mT", l, j), ins)
                n = 1 + 4 * l
                pe.wait_ge(sem("sq_ready"), n + 1)
                sumsq(("ss", n), lambda k: memsq[:, k, :], KT, ML)
                pe.wait_ge(sem("h_ready"), n + 1)

                def tokmajor(name):
                    for b in range(4):
                        i = item_at[(name, b, 0)]
                        arrived(i)
                        wv = slot_view(i, 8, 256)
                        for m in range(2):
                            o = begin((name, b, m))
                            for k in range(KT):
                                ins = mm(o[:, 0:256], mT[:, k, m * P:(m + 1) * P], wv[:, k, :], start=(k == 0), stop=(k == KT - 1))
                            end((name, b, m), ins)

                tokmajor(f"xk{l}")
                taken(pe, (f"xk{l}", 3, 1))
                for j in range(4):
                    o = begin(("KT", l, j))
                    for t in range(2):
                        for m in range(2):
                            ins = tr(o[:, (2 * t + m) * P:(2 * t + m + 1) * P], Kt[:, m, (2 * j + t) * P:(2 * j + t + 1) * P], ident)
                    end(("KT", l, j), ins)
                tokmajor(f"xv{l}")
                normed(2 + 4 * l)
                linear(f"xq{l}", 4, [8], h_in)
                taken(pe, (f"xq{l}", KT - 1))
                for j in range(2):
                    o = begin(("qs", l, j))
                    for t in range(4):
                        ins = tr(o[0:NB, t * P:(t + 1) * P], qT[:, 4 * j + t, NP:T], ident)
                    end(("qs", l, j), ins)
                for j in range(4):
                    taken(pe, ("KT", l, j))
                for lt in range(2):
                    for hp in range(2):
                        o = begin(("S", l, lt, hp))
                        for q in range(2):
                            h = 2 * hp + q
                            for d in range(2):
                                ins = mm(o[:, q * ML:(q + 1) * ML], qT[:, 2 * h + d, lt * P:(lt + 1) * P], KTt[:, 2 * h + d, :],
                                         start=(d == 0), stop=(d == 1))
                        end(("S", l, lt, hp), ins)
                n = 0
                for lt in range(2):
                    for hp in range(2):
                        o = begin(("PT", l, lt, hp))
                        n += 1
                        pe.wait_ge(sem("p_ready"), 4 * l + n)
                        for q in range(2):
                            for m in range(2):
                                ins = tr(o[:, (2 * q + m) * P:(2 * q + m + 1) * P], Pr[:, 2 * lt + hp, q, m * P:(m + 1) * P], ident)
                        end(("PT", l, lt, hp), ins)
                taken(pe, (f"xv{l}", 3, 1))
                for lt in range(2):
                    for hp in range(2):
                        taken(pe, ("PT", l, lt, hp))
                for t in range(KT):
                    o = begin(("ao", l, t))
                    for m in range(2):
                        ins = mm(o[:, 0:NP], Vt[:, m, t * P:(t + 1) * P], PTt[:, t // 2, m, :], start=(m == 0), stop=(m == 1))
                    end(("ao", l, t), ins)
                taken(pe, ("qs", l, 0))
                taken(pe, ("qs", l, 1))
                for b in range(NB):
                    for j in range(2):
                        o = begin(("qb", l, b, j))
                        end(("qb", l, b, j), mm(o, ident[0:NB, b:b + 1].to_broadcast([NB, P]), qstok[0:NB, j * 512:(j + 1) * 512],
                                                start=True, stop=True))
                o = begin(("sT", l))
                taken(pe, ("qb", l, NB - 1, 1))
                for m in range(2):
                    ins = tr(o[0:32, m * P:(m + 1) * P], sS[:, m, :], ident)
                end(("sT", l), ins)
                o = begin(("pT", l))
                pe.wait_ge(sem("ps_ready"), l + 1)
                for m in range(2):
                    ins = tr(o[:, m * 32:(m + 1) * 32], Ps[0:32, m * P:(m + 1) * P], ident[0:32, 0:32])
                end(("pT", l), ins)
                o = begin(("aos", l))
                taken(pe, ("pT", l))
                for b in range(NB):
                    n = NB + b
                    pe.wait_ge(sem(f"kv_in{n % KV_SLOTS}"), 16 * (4 * l + n // KV_SLOTS + 1))
                    for t in range(KT):
                        for m in range(2):
                            ins = mm(o[:, t * NB + b:t * NB + b + 1], kv[:, n % KV_SLOTS, m, t * P:(t + 1) * P],
                                     pTs[:, m, b * XH + t // 2:b * XH + t // 2 + 1], start=(m == 0), stop=(m == 1))
                    if b < NB - 1:
                        ins.then_inc(sem("v_used"), 1)
                end(("aos", l), ins)
                taken(pe, ("aos", l))
                for t in range(KT):
                    taken(pe, ("ao", l, t))
                linear(f"xo{l}", 4, [8], lambda k: oT[:, k, :])

            cross(0)
            normed(3)
            for b in range(FF // SLOT_N):
                for name in ("f1", "f3"):
                    i = item_at[(name, b, 0)]
                    arrived(i)
                    wv = slot_view(i, 8, 256)
                    for m in range(2):
                        o = begin((name, 2 * b + m))
                        for k in range(KT):
                            ins = mm(o[:, 0:T], wv[:, k, m * P:(m + 1) * P], hT[:, k, :], start=(k == 0), stop=(k == KT - 1))
                        end((name, 2 * b + m), ins)
            for t in range(FT):
                taken(pe, ("f3", t))
            linear("f2", 4, [8, 8, 6], lambda k: hid[:, k, :])

            pe.wait_ge(sem("ost_in"), 48)
            for j in range(3):
                o = begin(("ost", j))
                src = st_pool if j == 0 else st_conv[:, j - 1, :]
                for t in range(4):
                    ins = tr(o[:, t * 120:(t + 1) * 120], src[0:120, t * P:(t + 1) * P], ident[0:120, 0:120])
                end(("ost", j), ins)
            normed(4)
            linear("win1", 6, [8], h_in)
            pe.wait_ge(sem("tail1_ready"), 1)
            for key, src, n in ((("tail1",), tl1, 23), (("tail2",), tl2, 38)):
                o = begin(key)
                for t in range(4):
                    ins = tr(o[0:n, t * P:(t + 1) * P], src[:, t, :], ident)
                end(key, ins)
            pe.wait_ge(sem("pw_in"), 16)
            pe.wait_ge(sem("pooled"), 4)
            for g in range(OT):
                o = begin(("pw", g))
                end(("pw", g), mm(o[:, 0:T], pw[:, g, :], pooled[:, g, :], start=True, stop=True))
            pe.wait_ge(sem("conv_done"), 4)
            sumsq(("mu",), lambda k: mixo[:, OT + k, :], OT, T)
            pe.wait_ge(sem("csq_ready"), 1)
            sumsq(("var",), lambda k: csq[:, k, :], OT, T)
            pe.wait_ge(sem("conv_act"), 4)
            for g in range(OT):
                taken(pe, ("pw", g))
            linear("wout1", 4, [8], lambda k: mixo[:, k, :])
            cross(1)

            normed(7)
            pe.wait_ge(sem("router_in"), 32)
            o = begin(("logit",))
            for c in range(3):
                n = P if c < 2 else NB
                for k in range(KT):
                    mm(o[0:n, c * NE:(c + 1) * NE], hT[:, k, c * P:c * P + n], rwt[:, k, :], start=(k == 0), stop=False)
                ins = mm(o[0:n, c * NE:(c + 1) * NE], ones[0:1, 0:n], rbt[0:1, :], start=False, stop=True)
            end(("logit",), ins)
            o = begin(("rank",))
            pe.wait_ge(sem("picked_ready"), 1)
            for c in range(3):
                n = P if c < 2 else NB
                for b in range(c):
                    mm(o[0:n, c * NE:(c + 1) * NE], ones[:, 0:n], picked[:, b, :], start=(b == 0), stop=False)
                mm(o[0:n, c * NE:(c + 1) * NE], const("causal")[0:n, 0:n], picked[0:n, c, :], start=(c == 0), stop=True)
            for c in range(3):
                n = P if c < 2 else NB
                ins = mm(o[:, 3 * NE:4 * NE], ones[0:n, :], picked[0:n, c, :], start=(c == 0), stop=(c == 2))
            end(("rank",), ins)
            for c in range(3):
                n = P if c < 2 else NB
                for j in range(2):
                    o = begin(("htok", c, j))
                    for t in range(4):
                        ins = tr(o[0:n, t * P:(t + 1) * P], hT[:, 4 * j + t, c * P:c * P + n], ident)
                    end(("htok", c, j), ins)

            def turn_gates(o):
                for c in range(3):
                    n = P if c < 2 else NB
                    ins = tr(o[0:CAP, c * P:c * P + n], selg[0:n, c, :], ident[0:n, 0:n])
                return ins

            def gather(o, j):
                for t in range(4):
                    for c in range(3):
                        n = P if c < 2 else NB
                        ins = mm(o[:, t * CAP:(t + 1) * CAP], htok[0:n, c, (4 * j + t) * P:(4 * j + t + 1) * P], sel[0:n, c, :],
                                 start=(c == 0), stop=(c == 2))
                return ins

            o = begin(("selT0",))
            pe.wait_ge(sem("sel_ready"), 1)
            end(("selT0",), turn_gates(o))
            taken(pe, ("htok", 2, 1))
            for j in range(2):
                o = begin(("gat0", j))
                end(("gat0", j), gather(o, j))
            for j in range(2):
                taken(pe, ("gat0", j))
            taken(pe, ("selT0",))
            pe.wait_ge(sem("rounds_known"), 1)
            pairs = pe.value_load(rounds[0:1, 0:1], min_val=NE // 2, max_val=3 * NE // 2)
            side_full = [sem("side_full6"), sem("side_full7")]
            side_taken = [sem("side_taken6"), sem("side_taken7")]
            PER = (6, 5)

            def side(n, b, k):
                pe.wait_ge(side_taken[b], n * PER[b] + (k + 1))
                return psum[:, 6 + b, :]

            def scatter(n, h):
                pe.wait_ge(sem("ys_ready"), n * 2 + 1)
                for t in range(KT):
                    o = side(n, t % 2, t // 2)
                    mm(o[:, 0:T], ys[0:CAP, t * P:(t + 1) * P], selT[0:CAP, 1 - h, :], start=True, stop=True)\
                        .then_inc(side_full[t % 2], 1)

            with pe.Fori(0, pairs) as pair:
                for h in range(2):
                    n = pair * 2 + h
                    for j in range(ET // 2):
                        for g in range(2):
                            it = 2 * j + g
                            s, r = it % RING, it // RING
                            pe.wait_ge(slot_full[s], n * 32 + (base_full[s] + 16 * (r + 1)))
                            wv = slot_view(s, 8, 256)
                            for m in range(2):
                                pe.wait_ge(sem("gate_taken" if g == 0 else "up_taken"), n * ET + (max(2 * j + m - 1, 0) + 1))
                                for k in range(KT):
                                    ins = mm(psum[:, 2 * g + m, 0:CAP], wv[:, k, m * P:(m + 1) * P], hg[:, h, k, :],
                                             start=(k == 0), stop=(k == KT - 1))
                                ins.then_inc(eu, 1)
                    scatter(n, h)
                    o = side(n, 0, 4)
                    pe.wait_ge(sem("sel_ready"), n + 2)
                    turn_gates(o).then_inc(side_full[0], 1)
                    gather(side(n, 1, 4), 0).then_inc(side_full[1], 1)
                    gather(side(n, 0, 5), 1).then_inc(side_full[0], 1)
                    pe.wait_ge(sem("up_taken"), n * ET + (ET + 1))
                    pe.wait_ge(sem("ys_ready"), n * 2 + 1)
                    for d in range(4):
                        for kc in range(2):
                            it = 14 + 2 * d + kc
                            s, r = it % RING, it // RING
                            pe.wait_ge(slot_full[s], n * 32 + (base_full[s] + 16 * (r + 1)))
                            wv = slot_view(s, 7, 256)
                            for k in range(7):
                                ins = mm(psum[0:CAP, 4 + d // 2, (d % 2) * 256:(d % 2 + 1) * 256], ehid[:, 7 * kc + k, :], wv[:, k, :],
                                         start=(kc == 0 and k == 0), stop=(kc == 1 and k == 6))
                            ins.then_inc(eh if kc == 0 else ed, 1)
                    pe.wait_ge(sem("gate_taken"), n * ET + (ET + 1))
                    pe.wait_ge(side_taken[0], n * PER[0] + 7)
                    pe.wait_ge(side_taken[1], n * PER[1] + 6)
            scatter(pe.snap(pairs * 2), 0)
            pe.wait_ge(sem("sq_ready"), 9)
            for k in range(KT):
                ins = mm(psum[:, 0, 0:T], ones, hT[:, k, :], start=(k == 0), stop=(k == KT - 1))
            ins.then_inc(sem("final_ss"), 1)
            pe.wait_ge(sem("h_ready"), 9)
            for c in range(3):
                n = P if c < 2 else NB
                for j in range(2):
                    for t in range(4):
                        ins = tr(psum[0:n, 1 + 2 * c + j, t * P:(t + 1) * P], hT[:, 4 * j + t, c * P:c * P + n], ident)
                ins.then_inc(sem("final_tok"), 1)


        @block.scalar
        def _(act):
            af = nc.scalar.activation

            def free(key, ins):
                ins.then_inc(bank_free[G[key] % BANKS], 1)

            act.wait_ge(sem("eps_set"), 1)

            def norm(n, width=T):
                full(act, ("ss", n))
                free(("ss", n), af(rstd[:, 0:width], bank(("ss", n))[:, 0:width], ACT.Sqrt, scale=1.0 / DM, bias=eps[:, 0:1]))

            norm(0)
            taken(act, ("params",))
            for t in range(XT):
                taken(act, ("xbc", t))
                af(xc[:, t, 0:NP], xr[:, t, 0:NP], ACT.Identity, scale=gain("scw", t), bias=gain("scb", t))\
                    .then_inc(sem("tap0"), 1)
            for name, at in (("z", 0), ("g", 8)):
                for t in range(8):
                    full(act, (name, t))
                    free((name, t), af(zg[:, at + t, :], bank((name, t))[:, 0:T], ACT.Silu))
            act.wait_ge(sem("conv0"), 1)
            for t in range(XT):
                af(xc[:, t, :], xc[:, t, :], ACT.Silu).then_inc(sem("xc_ready"), 1)
            for j in range(3):
                full(act, ("tail0", j))
                free(("tail0", j), af(tailtok[:, j * 512:(j + 1) * 512], bank(("tail0", j))[0:11, :], ACT.Copy))
            act.wait_ge(sem("u_ready"), 1)
            act.wait_ge(sem("small_in"), 48)
            af(ea_t, a_log_t, ACT.Exp)
            af(dtmp[0:SH, 2, :], dtmp[0:SH, 1, :], ACT.Exp).then_inc(sem("e_ready"), 1)
            act.wait_ge(sem("w_ready"), 1)
            af(dtmp[0:SH, 4, :], dtmp[0:SH, 3, :], ACT.Ln).then_inc(sem("ln_ready"), 1)
            act.wait_ge(sem("dt_ready"), 1)
            af(ea[0:SH, :], acT[0:SH, NP:T], ACT.Exp).then_inc(sem("ea_ready"), 1)
            taken(act, ("dtT",))
            af(eac, tk[:, 1, 1, :], ACT.Exp).then_inc(sem("eac_ready"), 1)
            n = 0
            for c in range(NC):
                for g in range(SG):
                    for j in range(2):
                        n += 1
                        act.wait_ge(sem("diff_ready"), n)
                        af(S[:, j, :], S[:, j, :], ACT.Exp).then_inc(sem("decay_ready"), 1)
                    act.wait_ge(sem("wdiff_ready"), 2 * c + g + 1)
                    w8 = wend[:, c, 8 * g:8 * g + 8]
                    af(w8, w8, ACT.Exp).then_inc(sem("wend_ready"), 1)
            taken(act, ("bc", 1, 1, 1))
            af(etot, tot[:, 1, :], ACT.Exp).then_inc(sem("etot_ready"), 1)
            for g in range(SG):
                full(act, ("yss", g))
                free(("yss", g), af(rs2[:, g, :], bank(("yss", g))[:, 0:T], ACT.Sqrt, scale=1.0 / 512, bias=eps[:, 0:1]))
            for h in range(RH):
                full(act, ("oss", h))
                free(("oss", h), af(sqb[:, h, :], bank(("oss", h))[:, 0:T], ACT.Sqrt, scale=1.0 / RV, bias=eps[:, 0:1]))

            def cross(l):
                norm(1 + 4 * l, ML)
                for b in range(4):
                    for m in range(2):
                        key = (f"xv{l}", b, m)
                        full(act, key)
                        free(key, af(Vt[:, m, b * 256:(b + 1) * 256], bank(key)[:, 0:256], ACT.Copy))
                norm(2 + 4 * l)
                n = 0
                for lt in range(2):
                    for hp in range(2):
                        key = ("S", l, lt, hp)
                        n += 1
                        act.wait_ge(sem("mx_ready"), 4 * l + n)
                        for q in range(2):
                            c = 4 * lt + 2 * hp + q
                            ins = af(Pr[:, 2 * lt + hp, q, :], bank(key)[:, q * ML:(q + 1) * ML], ACT.Exp, scale=1.0 / 16,
                                     bias=nmx[:, c:c + 1], accum_out=rsum[:, c:c + 1])
                        free(key, ins)
                for t in range(KT):
                    key = ("ao", l, t)
                    full(act, key)
                    free(key, af(oT[:, t, 0:NP], bank(key)[:, 0:NP], ACT.Copy))
                act.wait_ge(sem("smx_ready"), l + 1)
                free(("sT", l), af(Ps[0:32, :], bank(("sT", l))[0:32, 0:ML], ACT.Exp, scale=1.0 / 16, bias=nms, accum_out=rss))

            cross(0)
            norm(3)
            for t in range(FT):
                if t >= 2:
                    taken(act, ("f3", t - 2))
                full(act, ("f1", t))
                free(("f1", t), af(sil[:, t % 2, :], bank(("f1", t))[:, 0:T], ACT.Silu))
            norm(4)
            for t in range(OT):
                key = ("win1", 8 + t)
                full(act, key)
                free(key, af(csq[:, t, :], bank(key)[:, 0:T], ACT.Sigmoid))
            for t in range(OT):
                act.wait_ge(sem("odd_raw"), t + 1)
                af(mixo[:, OT + t, 0:NP], gp[:, t, 0:NP], ACT.Identity, scale=gain("ccw", t), bias=gain("ccb", t))\
                    .then_inc(sem("ctap0"), 1)
            full(act, ("var",))
            free(("var",), af(rstd[:], bank(("var",))[:, 0:T], ACT.Sqrt, scale=1.0 / 512, bias=eps[:, 0:1]))
            for t in range(OT):
                act.wait_ge(sem("cnorm"), t + 1)
                af(mixo[:, OT + t, :], mixo[:, OT + t, :], ACT.Silu, scale=gain("cng", t), bias=gain("cnb", t))\
                    .then_inc(sem("conv_act"), 1)
            cross(1)
            norm(7)
            for c in range(3):
                n = P if c < 2 else NB
                act.wait_ge(sem("gap_ready"), c + 1)
                af(gt[0:n, c, 1:2], gt[0:n, c, 0:1], ACT.Exp).then_inc(sem("gap_exp"), 1)
            act.sem_inc(sem("gate_taken"), 1)
            act.wait_ge(sem("rounds_known"), 1)
            pairs = act.value_load(rounds[0:1, 0:1], min_val=NE // 2, max_val=3 * NE // 2)
            side_full = [sem("side_full6"), sem("side_full7")]
            side_taken = [sem("side_taken6"), sem("side_taken7")]
            with act.Fori(0, pairs) as pair:
                for h in range(2):
                    n = pair * 2 + h
                    for f in range(ET):
                        act.wait_ge(eu, n * (2 * ET) + (4 * (f // 2) + f % 2 + 1))
                        act.wait_ge(sem("up_taken"), n * ET + (max(f - 1, 0) + 1))
                        af(esil[:, f % 2, :], psum[:, f % 2, 0:CAP], ACT.Silu).then_inc(sem("gate_taken"), 1)
                    act.wait_ge(side_full[0], n * 6 + 5)
                    af(selT[0:CAP, 1 - h, :], psum[0:CAP, 6, 0:T], ACT.Copy).then_inc(side_taken[0], 1)
                    act.wait_ge(side_full[1], n * 5 + 5)
                    af(hg[:, 1 - h, 0:4, :], psum[:, 7, 0:4 * CAP].rearrange("p (t s) -> p t s", t=4), ACT.Copy).then_inc(side_taken[1], 1)
                    act.wait_ge(side_full[0], n * 6 + 6)
                    af(hg[:, 1 - h, 4:8, :], psum[:, 6, 0:4 * CAP].rearrange("p (t s) -> p t s", t=4), ACT.Copy).then_inc(side_taken[0], 1)
                    for j in range(2):
                        act.wait_ge(ed, n * 4 + (2 * j + 2))
                        af(ys[0:CAP, j * 512:(j + 1) * 512], psum[0:CAP, 4 + j, :], ACT.Copy).then_inc(sem("ys_ready"), 1)
            act.wait_ge(sem("final_ss"), 1)
            af(rstd[:], psum[:, 0, 0:T], ACT.Sqrt, scale=1.0 / DM, bias=eps[:, 0:1]).then_inc(sem("final_root"), 1)

        @block.vector
        def _(dve):
            v = nc.vector
            chain = [0]

            def step(ins):
                chain[0] += 1
                ins.then_inc(sem("dve_chain"), 1)
                dve.wait_ge(sem("dve_chain"), chain[0])

            def free(key, ins, wait=False):
                ins.then_inc(bank_free[G[key] % BANKS], 1)
                if wait:
                    taken(dve, key)

            def norm(n, name, t0, x, h, sq, width=T, root=None):
                v.tensor_tensor(sq, x, x, ALU.mult).then_inc(sem("sq_ready"), 1)
                if root is None:
                    taken(dve, ("ss", n))
                else:
                    dve.wait_ge(root, 1)
                step(v.reciprocal(rstd[:, 0:width], rstd[:, 0:width]))
                for t in range(KT):
                    ins = v.scalar_tensor_tensor(out=h[:, t, :], in0=x[:, t, :], scalar=gain(name, t0 + t), in1=rstd[:, 0:width],
                                                 op0=ALU.mult, op1=ALU.mult)
                ins.then_inc(sem("h_ready"), 1)

            def x_norm(n, name, t0):
                norm(n, name, t0, xT[:, :, :], hT, hT[:, :, :])

            def add_x(name):
                for t in range(KT):
                    full(dve, (name, t))
                    free((name, t), v.tensor_tensor(xT[:, t, :], xT[:, t, :], bank((name, t))[:, 0:T], ALU.add), wait=(t == KT - 1))

            full(dve, ("params",))
            free(("params",), v.tensor_copy(par[:], bank(("params",))[:, 0:NPAR]), wait=True)
            full(dve, ("cst",))
            free(("cst",), v.tensor_copy(cst_keep, bank(("cst",))[:, 0:24 * XT]))
            for t in range(KT):
                full(dve, ("xT", t))
                free(("xT", t), v.tensor_copy(xT[:, t, :], bank(("xT", t))[:, 0:T]), wait=(t == KT - 1))
            x_norm(0, "mix", 0)
            step(v.memset(xr[:, :, 0:SCONV - 1], 0.0))
            v.tensor_copy(xrs[:, :, :, 0:SCONV - 1], cst_keep.rearrange("p (t b s) -> p t b s", t=XT, s=SCONV - 1))
            for t in range(XT):
                full(dve, ("xbc", t))
                v.tensor_copy(xrs[:, t, :, SCONV - 1], bank(("xbc", t))[:, NP:T])
                free(("xbc", t), v.tensor_copy(xr[:, t, SCONV - 1:], bank(("xbc", t))[:, 0:NP]), wait=True)
            full(dve, ("dt", 0))
            dve.wait_ge(sem("small_in"), 48)
            u, na, ex, wv, ln = (dtmp[0:SH, i, :] for i in range(5))
            free(("dt", 0), v.tensor_scalar(u, bank(("dt", 0))[0:SH, 0:T], dt_bias_t, None, ALU.add), wait=True)
            v.scalar_tensor_tensor(out=na, in0=u, scalar=-1.0, in1=u, op0=ALU.mult, op1=ALU.min).then_inc(sem("u_ready"), 1)
            for t in range(XT):
                dve.wait_ge(sem("tap0"), t + 1)
                for k in range(1, SCONV):
                    step(v.scalar_tensor_tensor(out=xc[:, t, 0:NP], in0=xr[:, t, k:k + NP], scalar=gain("scw", k * XT + t),
                                                in1=xc[:, t, 0:NP], op0=ALU.mult, op1=ALU.add))
            sx = xc[:, :, NP:T]
            wk_ = lambda k: par[:, COL["scw"] + k * XT:COL["scw"] + (k + 1) * XT].unsqueeze(2).to_broadcast([P, XT, NB])
            bias_ = par[:, COL["scb"]:COL["scb"] + XT].unsqueeze(2).to_broadcast([P, XT, NB])
            tmp = cst_keep[:, 0:XT * NB].rearrange("p (t b) -> p t b", t=XT)
            step(v.tensor_tensor(sx, xrs[:, :, :, 0], wk_(0), ALU.mult))
            step(v.tensor_tensor(sx, sx, bias_, ALU.add))
            for k in range(1, SCONV):
                step(v.tensor_tensor(tmp, xrs[:, :, :, k], wk_(k), ALU.mult))
                if k < SCONV - 1:
                    step(v.tensor_tensor(sx, sx, tmp, ALU.add))
            v.tensor_tensor(sx, sx, tmp, ALU.add).then_inc(sem("conv0"), 1)
            for name, at in (("q", 0), ("k", 4)):
                for t in range(4):
                    full(dve, (name, t))
                    free((name, t), v.tensor_copy(qk[:, at + t, :], bank((name, t))[:, 0:T]))
            for t in range(RH):
                full(dve, ("v", t))
                free(("v", t), v.tensor_copy(vT[:, t, :], bank(("v", t))[:, 0:T]))
            dve.wait_ge(sem("e_ready"), 1)
            v.tensor_scalar(wv, ex, 1.0, None, ALU.add).then_inc(sem("w_ready"), 1)
            dve.wait_ge(sem("w_ready"), 1)
            step(v.tensor_scalar(na, wv, -1.0, None, ALU.add))
            dve.wait_ge(sem("ln_ready"), 1)
            step(v.tensor_scalar(wv, na, 0.0, None, ALU.is_equal))
            step(v.tensor_tensor(na, na, wv, ALU.add))
            step(v.reciprocal(na, na))
            step(v.tensor_tensor(ln, ln, na, ALU.mult))
            step(v.tensor_tensor(ln, ln, wv, ALU.add))
            step(v.tensor_tensor(ln, ln, ex, ALU.mult))
            step(v.scalar_tensor_tensor(out=dtT[0:SH, :], in0=u, scalar=0.0, in1=ln, op0=ALU.max, op1=ALU.add))
            step(v.tensor_scalar(na, dtT[0:SH, :], ea_t, -1.0, ALU.mult, ALU.mult))
            for c in range(NC):
                v.tensor_tensor_scan(acT[0:SH, c * P:(c + 1) * P], const("ones")[0:SH, :], na[:, c * P:(c + 1) * P], 0.0,
                                     ALU.mult, ALU.add)
            v.tensor_copy(acT[0:SH, NP:T], na[:, NP:T]).then_inc(sem("dt_ready"), 1)
            full(dve, ("dtT",))
            v.tensor_copy(tk[:, :, :, :].rearrange("p a c h -> p (a c h)"), bank(("dtT",))[:, 0:4 * SH])
            free(("dtT",), v.tensor_copy(dtst[0:NB, :], bank(("dtT",))[0:NB, 4 * SH:5 * SH]), wait=True)
            full(dve, ("dbc",))
            db = bank(("dbc",))
            v.tensor_copy(Dcol[0:64, :], db[0:64, 0:SH:2])
            free(("dbc",), v.tensor_copy(Dcol[64:P, :], db[64:P, 1:SH:2]), wait=True)
            full(dve, ("Btok",))
            free(("Btok",), v.tensor_copy(Btok[:, :, :].rearrange("p c n -> p (c n)"), bank(("Btok",))))

            def heads(ap, n=8):
                return ap.rearrange("p (h v) -> p h v", h=n)

            def per_head(ap, width):
                return ap.unsqueeze(2).to_broadcast([ap.shape[0], ap.shape[1], width])

            for c in range(NC):
                for j in range(2):
                    key = ("xtok", c, j)
                    full(dve, key)
                    free(key, v.tensor_tensor(heads(xdt[:, c, j * 512:(j + 1) * 512]), heads(bank(key)),
                                              per_head(tk[:, 0, c, 8 * j:8 * j + 8], SD), ALU.mult), wait=True)
            full(dve, ("CB",))
            dve.wait_ge(sem("econst_in"), 16)
            free(("CB",), v.tensor_tensor(SM[:, :, :], bank(("CB",)).rearrange("p (a i) -> p a i", i=P),
                                          const("causal").unsqueeze(1).to_broadcast([P, SG * NC, P]), ALU.mult), wait=True)
            dve.wait_ge(sem("eac_ready"), 1)
            n = 0
            for c in range(NC):
                for g in range(SG):
                    for j in range(2):
                        key = ("bc", c, g, j)
                        full(dve, key)
                        h0 = 8 * g + 4 * j
                        for q in range(4):
                            ins = v.tensor_scalar(S[:, j, q * P:(q + 1) * P], bank(key)[:, q * P:(q + 1) * P],
                                                  tk[:, 1, c, h0 + q:h0 + q + 1], 0.0, ALU.subtract, ALU.min)
                        ins.then_inc(sem("diff_ready"), 1)
                        free(key, v.tensor_copy(tot[:, c, h0:h0 + 4], bank(key)[:, P - 1:512:P]), wait=True)
                    hs = slice(8 * g, 8 * g + 8)
                    v.tensor_tensor(wend[:, c, hs], tot[:, c, hs], tk[:, 1, c, hs], ALU.subtract).then_inc(sem("wdiff_ready"), 1)
                    for j in range(2):
                        n += 1
                        dve.wait_ge(sem("decay_ready"), n)
                        sv = S[:, j, :].rearrange("p (q i) -> p q i", q=4)
                        v.tensor_tensor(sv, sv, SM[:, 2 * g + c, :].unsqueeze(1).to_broadcast([P, 4, P]), ALU.mult)\
                            .then_inc(sem("s_ready"), 1)
                    dve.wait_ge(sem("wend_ready"), 2 * c + g + 1)
                    v.tensor_tensor(heads(xdtw[:, g * 512:(g + 1) * 512]), heads(xdt[:, c, g * 512:(g + 1) * 512]),
                                    per_head(wend[:, c, hs], SD), ALU.mult).then_inc(sem("xdtw_ready"), 1)
                    key, yv = ("y", c, g), ytok[:, c, g * 512:(g + 1) * 512]
                    full(dve, key)
                    if c == 0:
                        free(key, v.tensor_copy(yv, bank(key)))
                        full(dve, ("kv", 0, g))
                        free(("kv", 0, g), v.tensor_copy(hst[:, g, :], bank(("kv", 0, g))))
                    else:
                        full(dve, ("yi", g))
                        free(("yi", g), v.tensor_tensor(heads(yv), heads(bank(("yi", g))), per_head(eac[:, hs], SD), ALU.mult), wait=True)
                        free(key, v.tensor_tensor(yv, yv, bank(key), ALU.add))
            dve.wait_ge(sem("etot_ready"), 1)
            for g in range(SG):
                hv = heads(hst[:, g, :])
                step(v.tensor_tensor(hv, hv, per_head(etot[:, 8 * g:8 * g + 8], SD), ALU.mult))
                full(dve, ("kv", 1, g))
                free(("kv", 1, g), v.tensor_tensor(hst[:, g, :], hst[:, g, :], bank(("kv", 1, g)), ALU.add))
            for t in range(KT):
                key = ("yT", t)
                full(dve, key)
                free(key, v.scalar_tensor_tensor(out=xc[:, t, 0:NP], in0=xc[:, t, 0:NP], scalar=Dcol[:, t:t + 1],
                                                 in1=bank(key)[:, 0:NP], op0=ALU.mult, op1=ALU.add), wait=(t == KT - 1))
            dve.wait_ge(sem("ea_ready"), 1)
            idn = const("ident")[0:SH, 0:SH].unsqueeze(1).to_broadcast([SH, NB, SH])
            v.tensor_tensor(eaD[0:SH, :, :], idn, ea[0:SH, :].unsqueeze(2).to_broadcast([SH, NB, SH]), ALU.mult)\
                .then_inc(sem("ead_ready"), 1)
            full(dve, ("eab",))
            free(("eab",), v.tensor_copy(eab[:, :, :].rearrange("p b h -> p (b h)"), bank(("eab",))[:, 0:NB * SH]))
            for j in range(2):
                key = ("xstok", j)
                full(dve, key)
                free(key, v.tensor_tensor(heads(xstok[0:NB, j * 512:(j + 1) * 512]), heads(bank(key)[0:NB, :]),
                                          per_head(dtst[0:NB, 8 * j:8 * j + 8], SD), ALU.mult))

            def sample_y(b):
                key = ("ys", b)
                full(dve, key)
                step(v.tensor_tensor(ysum, xc[:, 0:KT, NP + b], Dcol[:, :], ALU.mult))
                free(key, v.tensor_tensor(xc[:, 0:KT, NP + b], ysum, bank(key)[:, 0:KT], ALU.add), wait=True)

            for b in range(NB):
                dve.wait_ge(sem("h_decayed"), b + 1)
                for g in range(SG):
                    key = ("xb", b, g)
                    full(dve, key)
                    hv = hb[:, b % 3, g * 512:(g + 1) * 512]
                    ins = v.scalar_tensor_tensor(out=hv, in0=bank(key), scalar=xc[:, 8 + g, NP + b:NP + b + 1], in1=hv,
                                                 op0=ALU.mult, op1=ALU.add)
                    free(key, ins)
                if b:
                    sample_y(b - 1)
            sample_y(NB - 1)
            zy = zg[:, 0:KT, :]
            step(v.tensor_tensor(zy, zy, xc[:, 0:KT, :], ALU.mult))
            ssm_stored(dve)
            v.tensor_tensor(sqb[:, :, :], zy, zy, ALU.mult).then_inc(sem("ysq_ready"), 1)
            for g in range(SG):
                taken(dve, ("yss", g))
                step(v.reciprocal(rs2[:, g, :], rs2[:, g, :]))
                for t in range(4 * g, 4 * g + 4):
                    ins = v.scalar_tensor_tensor(out=zg[:, t, :], in0=zg[:, t, :], scalar=gain("gnorm", t), in1=rs2[:, g, :],
                                                 op0=ALU.mult, op1=ALU.mult)
            step(ins)
            for i in range(8):
                kind = "q" if i < 4 else "k"
                full(dve, ("rot", i))
                v.tensor_tensor(rs2[:, 0, :], qk[:, i, :], const("cos" + kind), ALU.mult)
                free(("rot", i), v.tensor_tensor(rs2[:, 1, :], bank(("rot", i))[:, 0:T], const("sin" + kind), ALU.mult), wait=True)
                v.tensor_tensor(qk[:, i, :], rs2[:, 0, :], rs2[:, 1, :], ALU.add).then_inc(sem("rot_done"), 1)
                dve.wait_ge(sem("rot_done"), i + 1)
            for c in range(NC):
                key = ("ktok", c)
                full(dve, key)
                free(key, v.tensor_tensor(heads(ktok[:, c, :]), heads(bank(key)), per_head(const("wk"), RK), ALU.mult))
            for c in range(NC):
                for j in range(2):
                    key = ("vtok", c, j)
                    full(dve, key)
                    free(key, v.tensor_copy(vtok[:, c, j * 512:(j + 1) * 512], bank(key)))
            dve.wait_ge(sem("tail0_out"), 32)
            for c in range(NC):
                for p in range(2):
                    key = ("rs", c, p)
                    full(dve, key)
                    free(key, v.tensor_tensor(S[:, p, :], bank(key), const("dret")[:, p * 512:(p + 1) * 512], ALU.mult))
                for p in range(2):
                    key, ov = ("ro", c, p), otok[:, c, p * 512:(p + 1) * 512]
                    if c == 0:
                        full(dve, key)
                        free(key, v.tensor_copy(ov, bank(key)))
                    else:
                        full(dve, ("ri", p))
                        free(("ri", p), v.tensor_tensor(heads(ov, 4), heads(bank(("ri", p)), 4),
                                                        per_head(const("gq")[:, 4 * p:4 * p + 4], RV), ALU.mult), wait=True)
                        free(key, v.tensor_tensor(ov, ov, bank(key), ALU.add))
                key = ("rkv", c)
                full(dve, key)
                rv = rst[:, 0, :]
                if c == 0:
                    free(key, v.tensor_copy(rv, bank(key)), wait=True)
                else:
                    for hh in range(4):
                        hv = rv[:, hh * RV:(hh + 1) * RV]
                        ins = v.scalar_tensor_tensor(out=hv, in0=hv, scalar=const("gchunk")[:, hh:hh + 1],
                                                     in1=bank(key)[:, hh * RV:(hh + 1) * RV], op0=ALU.mult, op1=ALU.add)
                    free(key, ins)
            for h in range(RH):
                full(dve, ("oT", h))
                free(("oT", h), v.tensor_copy(oTt[:, h, 0:NP], bank(("oT", h))[:, 0:NP]))
            for j in range(2):
                full(dve, ("vstok", j))
                free(("vstok", j), v.tensor_copy(vstok[0:NB, j * 512:(j + 1) * 512], bank(("vstok", j))[0:NB, :]))

            def sample_o(b):
                for p in range(2):
                    full(dve, ("os", b, p))
                    free(("os", b, p), v.tensor_copy(oTt[:, p:RH:2, NP + b], bank(("os", b, p))[:, 0:4]), wait=(b == NB - 1))

            for b in range(NB):
                key = ("vb", b)
                full(dve, key)
                dve.wait_ge(sem("r_decayed"), b + 1)
                for hh in range(4):
                    hv = rb[:, b % 4, hh * RV:(hh + 1) * RV]
                    ins = v.scalar_tensor_tensor(out=hv, in0=bank(key)[:, hh * RV:(hh + 1) * RV], scalar=qk[:, 4 + hh, NP + b:NP + b + 1],
                                                 in1=hv, op0=ALU.mult, op1=ALU.add)
                free(key, ins)
                if b:
                    sample_o(b - 1)
            sample_o(NB - 1)
            even_stored(dve)
            v.tensor_tensor(sqb[:, :, :], oTt, oTt, ALU.mult).then_inc(sem("osq_ready"), 1)
            zo = zg[:, RH:2 * RH, :]
            step(v.tensor_tensor(zo, zo, oTt, ALU.mult))
            for h in range(RH):
                taken(dve, ("oss", h))
            step(v.reciprocal(sqb[:, :, :], sqb[:, :, :]))
            v.tensor_tensor(zo, zo, sqb[:, :, :], ALU.mult).then_inc(sem("mixed_ready"), 1)
            add_x("wout0")

            def cross(l):
                for j in range(4):
                    key = ("mT", l, j)
                    full(dve, key)
                    free(key, v.tensor_copy(mT[:, 2 * j:2 * j + 2, :].rearrange("p t m -> p (t m)"), bank(key)), wait=(j == 3))
                norm(1 + 4 * l, "mem", KT * l, mT[:, :, :], mT, memsq[:, :, :], width=ML)
                for b in range(4):
                    for m in range(2):
                        key = (f"xk{l}", b, m)
                        full(dve, key)
                        free(key, v.tensor_copy(Kt[:, m, b * 256:(b + 1) * 256], bank(key)[:, 0:256]))
                for j in range(4):
                    key = ("KT", l, j)
                    full(dve, key)
                    free(key, v.tensor_copy(KTt[:, 2 * j:2 * j + 2, :].rearrange("p t m -> p (t m)"), bank(key)))
                x_norm(2 + 4 * l, "cross", KT * l)
                for t in range(KT):
                    full(dve, (f"xq{l}", t))
                    free((f"xq{l}", t), v.tensor_copy(qT[:, t, :], bank((f"xq{l}", t))[:, 0:T]))
                for j in range(2):
                    full(dve, ("qs", l, j))
                    free(("qs", l, j), v.tensor_copy(qstok[0:NB, j * 512:(j + 1) * 512], bank(("qs", l, j))[0:NB, :]))
                for lt in range(2):
                    for hp in range(2):
                        key = ("S", l, lt, hp)
                        full(dve, key)
                        c = 4 * lt + 2 * hp
                        step(v.tensor_reduce(nmx[:, c:c + 2], bank(key).rearrange("p (q m) -> p q m", q=2), AX, ALU.max))
                        v.tensor_scalar(nmx[:, c:c + 2], nmx[:, c:c + 2], -1.0 / 16, None, ALU.mult).then_inc(sem("mx_ready"), 1)
                for lt in range(2):
                    for hp in range(2):
                        key = ("S", l, lt, hp)
                        taken(dve, key)
                        c = 4 * lt + 2 * hp
                        step(v.reciprocal(rsum[:, c:c + 2], rsum[:, c:c + 2]))
                        for q in range(2):
                            ins = v.tensor_scalar(Pr[:, 2 * lt + hp, q, :], Pr[:, 2 * lt + hp, q, :], rsum[:, c + q:c + q + 1], None, ALU.mult)
                        ins.then_inc(sem("p_ready"), 1)
                for lt in range(2):
                    for hp in range(2):
                        key = ("PT", l, lt, hp)
                        full(dve, key)
                        for q in range(2):
                            ins = v.tensor_copy(PTt[:, 2 * hp + q, :, lt * P:(lt + 1) * P],
                                                bank(key)[:, q * 256:(q + 1) * 256].rearrange("p (m i) -> p m i", m=2))
                        free(key, ins)
                for b in range(NB):
                    dve.wait_ge(sem(f"kv_in{b % KV_SLOTS}"), 16 * (4 * l + b // KV_SLOTS + 1))
                    for j in range(2):
                        key = ("qb", l, b, j)
                        full(dve, key)
                        for m in range(2):
                            for q in range(2):
                                h = 2 * j + q
                                kh = kv[:, b % KV_SLOTS, m, h * 256:(h + 1) * 256]
                                ins = v.tensor_tensor_reduce(kh, kh, bank(key)[:, q * 256:(q + 1) * 256], 1.0, 0.0, ALU.mult, ALU.add,
                                                             sS[:, m, b * XH + h:b * XH + h + 1])
                        free(key, ins)
                key = ("sT", l)
                full(dve, key)
                step(v.tensor_reduce(nms, bank(key)[0:32, 0:ML], AX, ALU.max))
                v.tensor_scalar(nms, nms, -1.0 / 16, None, ALU.mult).then_inc(sem("smx_ready"), 1)
                taken(dve, key)
                step(v.reciprocal(rss, rss))
                v.tensor_scalar(Ps[0:32, :], Ps[0:32, :], rss, None, ALU.mult).then_inc(sem("ps_ready"), 1)
                full(dve, ("pT", l))
                free(("pT", l), v.tensor_copy(pTs[:, :, :].rearrange("p m i -> p (m i)"), bank(("pT", l))[:, 0:64]))
                full(dve, ("aos", l))
                free(("aos", l), v.tensor_copy(oT[:, :, NP:T], bank(("aos", l))[:, 0:64].rearrange("p (t b) -> p t b", t=KT)))
                add_x(f"xo{l}")

            cross(0)
            x_norm(3, "ffn", 0)
            dve.wait_ge(sem("vst"), 16)
            for t in range(FT):
                full(dve, ("f3", t))
                taken(dve, ("f1", t))
                free(("f3", t), v.tensor_tensor(hid[:, t, :], sil[:, t % 2, :], bank(("f3", t))[:, 0:T], ALU.mult))
            add_x("f2")
            full(dve, ("ost", 0))
            v.memset(up[:, :, 0:PST], 0.0)
            v.memset(gp[:, :, 0:CK - 1], 0.0)
            for t in range(OT):
                ins = v.tensor_copy(us[:, t, :, 0:PST], bank(("ost", 0))[:, t * 120:(t + 1) * 120].rearrange("p (b s) -> p b s", s=PST))
            free(("ost", 0), ins)
            for j in (1, 2):
                key = ("ost", j)
                full(dve, key)
                for t in range(OT):
                    ins = v.tensor_copy(gs[:, t, 4 * j - 4:4 * j, 0:CK - 1],
                                        bank(key)[:, t * 120:(t + 1) * 120].rearrange("p (b s) -> p b s", s=CK - 1))
                free(key, ins)
            x_norm(4, "mix", KT)
            for t in range(8):
                key = ("win1", t)
                full(dve, key)
                if t < OT:
                    v.tensor_copy(us[:, t, :, PST], bank(key)[:, NP:T])
                    free(key, v.tensor_copy(up[:, t, PST:], bank(key)[:, 0:NP]), wait=True)
                else:
                    free(key, v.tensor_copy(ga[:, t - OT, :], bank(key)[:, 0:T]), wait=True)
            for t in range(OT):
                taken(dve, ("win1", 8 + t))
                v.tensor_tensor(gs[:, t, :, CK - 1], ga[:, t, NP:T], csq[:, t, NP:T], ALU.mult)
                v.tensor_tensor(gp[:, t, CK - 1:], ga[:, t, 0:NP], csq[:, t, 0:NP], ALU.mult).then_inc(sem("odd_raw"), 1)
            dve.wait_ge(sem("odd_raw"), 4)
            n_up = PST + NP
            for g, win in enumerate(WINDOWS):
                src, width, lo = up[:, g, :], 1, 0
                bufs = [w2t, w4t]
                while width < win:
                    dst = bufs[0]
                    step(v.tensor_tensor(dst[:, lo + width:n_up], src[:, lo + width:n_up], src[:, lo:n_up - width], ALU.add))
                    src, lo, width = dst, lo + width, 2 * width
                    bufs = bufs[::-1]
                u_ = up[:, g, PST:]
                step(v.scalar_tensor_tensor(out=pooled[:, g, 0:NP], in0=src[:, PST:], scalar=1.0 / win, in1=u_, op0=ALU.mult,
                                            op1=ALU.subtract))
                at = g * (PST + 1)
                step(v.tensor_tensor(prods[:, 0, 0:PST + 1], src[:, PST:2 * PST + 1], const("invcnt")[:, at:at + PST + 1], ALU.mult))
                step(v.tensor_tensor(pooled[:, g, 0:PST + 1], prods[:, 0, 0:PST + 1], u_[:, 0:PST + 1], ALU.subtract))
                step(v.tensor_reduce(prods[:, 1, 0:NB], us[:, g, :, PST + 1 - win:PST + 1], AX, ALU.add))
                v.scalar_tensor_tensor(out=pooled[:, g, NP:T], in0=prods[:, 1, 0:NB], scalar=1.0 / win, in1=us[:, g, :, PST],
                                       op0=ALU.mult, op1=ALU.subtract).then_inc(sem("pooled"), 1)
                dve.wait_ge(sem("pooled"), g + 1)
            for j, (key, dst, n) in enumerate(((("tail1",), tok1, 23), (("tail2",), tok2, 38))):
                full(dve, key)
                free(key, v.tensor_copy(dst[0:n, :], bank(key)[0:n, :]))
            for g in range(OT):
                key = ("pw", g)
                full(dve, key)
                free(key, v.tensor_scalar(mixo[:, g, :], bank(key)[:, 0:T], gain("pscale", g), None, ALU.mult))
            for t in range(OT):
                cw = par[:, COL["ccw"] + t:COL["ccw"] + 4 * CK:4]
                step(v.tensor_tensor(prods[:, :, :], gs[:, t, :, :], cw.unsqueeze(1).to_broadcast([P, NB, CK]), ALU.mult))
                step(v.tensor_reduce(mixo[:, OT + t, NP:T], prods[:, :, :], AX, ALU.add))
                step(v.tensor_scalar(mixo[:, OT + t, NP:T], mixo[:, OT + t, NP:T], gain("ccb", t), None, ALU.add))
                dve.wait_ge(sem("ctap0"), t + 1)
                for k in range(1, CK):
                    ins = v.scalar_tensor_tensor(out=mixo[:, OT + t, 0:NP], in0=gp[:, t, k:k + NP], scalar=gain("ccw", 4 * k + t),
                                                 in1=mixo[:, OT + t, 0:NP], op0=ALU.mult, op1=ALU.add)
                    if k < CK - 1:
                        step(ins)
                ins.then_inc(sem("conv_done"), 1)
                dve.wait_ge(sem("conv_done"), t + 1)
            full(dve, ("mu",))
            for t in range(OT):
                ins = v.scalar_tensor_tensor(out=mixo[:, OT + t, :], in0=bank(("mu",))[:, 0:T], scalar=-1.0 / 512, in1=mixo[:, OT + t, :],
                                             op0=ALU.mult, op1=ALU.add)
            free(("mu",), ins, wait=True)
            v.tensor_tensor(csq[:, :, :], mixo[:, OT:, :], mixo[:, OT:, :], ALU.mult).then_inc(sem("csq_ready"), 1)
            taken(dve, ("var",))
            step(v.reciprocal(rstd[:], rstd[:]))
            for t in range(OT):
                v.tensor_tensor(mixo[:, OT + t, :], mixo[:, OT + t, :], rstd[:], ALU.mult).then_inc(sem("cnorm"), 1)
            add_x("wout1")
            cross(1)

            x_norm(7, "ffn", KT)
            full(dve, ("logit",))
            step(v.memset(comb[:, 2, :], 0.0))
            step(v.memset(slot[:, 2, :], -1.0))
            for c in range(3):
                n = P if c < 2 else NB
                ins = v.tensor_copy(lg[0:n, c, :], bank(("logit",))[0:n, c * NE:(c + 1) * NE])
            free(("logit",), ins, wait=True)
            for c in range(3):
                n = P if c < 2 else NB
                step(v.max(mx[0:n, c, :], lg[0:n, c, :]))
                step(v.max_index(idx[0:n, c, :], mx[0:n, c, :], lg[0:n, c, :]))
                step(v.tensor_copy(idxf[0:n, c, :], idx[0:n, c, :]))
                v.tensor_tensor(gt[0:n, c, 0:1], mx[0:n, c, 1:2], mx[0:n, c, 0:1], ALU.subtract).then_inc(sem("gap_ready"), 1)
            for c in range(3):
                n = P if c < 2 else NB
                dve.wait_ge(sem("gap_exp"), c + 1)
                step(v.tensor_scalar(gt[0:n, c, 2:3], gt[0:n, c, 1:2], 1.0, None, ALU.add))
                step(v.reciprocal(gt[0:n, c, 2:3], gt[0:n, c, 2:3]))
                step(v.tensor_tensor(gt[0:n, c, 3:4], gt[0:n, c, 1:2], gt[0:n, c, 2:3], ALU.mult))
                iota = const("iota")[0:n, 0:NE]
                step(v.tensor_scalar(picked[0:n, c, :], iota, idxf[0:n, c, 0:1], None, ALU.is_equal))
                step(v.tensor_scalar(lg[0:n, c, :], iota, idxf[0:n, c, 1:2], None, ALU.is_equal))
                step(v.tensor_scalar(comb[0:n, c, :], picked[0:n, c, :], gt[0:n, c, 2:3], None, ALU.mult))
                step(v.scalar_tensor_tensor(out=comb[0:n, c, :], in0=lg[0:n, c, :], scalar=gt[0:n, c, 3:4], in1=comb[0:n, c, :],
                                            op0=ALU.mult, op1=ALU.add))
                step(v.tensor_tensor(picked[0:n, c, :], picked[0:n, c, :], lg[0:n, c, :], ALU.add))
            v.memset(ys[0:CAP, :], 0.0)
            v.memset(selT[0:CAP, 1, :], 0.0).then_inc(sem("picked_ready"), 1)
            full(dve, ("rank",))
            rank = bank(("rank",))
            for c in range(3):
                n = P if c < 2 else NB
                step(v.tensor_tensor(slot[0:n, c, :], rank[0:n, c * NE:(c + 1) * NE], picked[0:n, c, :], ALU.mult))
                step(v.tensor_scalar(slot[0:n, c, :], slot[0:n, c, :], -1.0, None, ALU.add))
            step(v.tensor_reduce(cnts[:, 0:1], rank[:, 3 * NE:4 * NE], AX, ALU.max))
            free(("rank",), v.tensor_scalar(cnts[:, 1:2], cnts[:, 0:1], float(CAP), float(NE // 2), ALU.is_gt, ALU.mult), wait=True)
            step(v.tensor_scalar(cnts[:, 2:3], cnts[:, 0:1], float(2 * CAP), float(NE // 2), ALU.is_gt, ALU.mult))
            step(v.scalar_tensor_tensor(out=cnts[:, 3:4], in0=cnts[:, 1:2], scalar=float(NE // 2), in1=cnts[:, 2:3],
                                        op0=ALU.add, op1=ALU.add))
            step(v.tensor_scalar(cnts[:, 2:3], cnts[:, 3:4], 2.0, -1.0, ALU.mult, ALU.add))
            v.tensor_copy(rounds[:, 0:1], cnts[:, 3:4])
            v.tensor_copy(rounds[:, 1:2], cnts[:, 2:3]).then_inc(sem("rounds_known"), 1)
            iota3 = const("iota").unsqueeze(1).to_broadcast([P, 3, CAP])

            def choose(e, link):
                at = slot[:, :, bass.ds(e, 1)] if not isinstance(e, int) else slot[:, :, e:e + 1]
                gate = comb[:, :, bass.ds(e, 1)] if not isinstance(e, int) else comb[:, :, e:e + 1]
                link(v.tensor_tensor(sel[:, :, :], iota3, at.to_broadcast([P, 3, CAP]), ALU.is_equal))
                link(v.tensor_scalar(at, at, -float(CAP), None, ALU.add))
                v.tensor_tensor(selg[:, :, :], sel[:, :, :], gate.to_broadcast([P, 3, CAP]), ALU.mult).then_inc(sem("sel_ready"), 1)

            choose(0, step)
            for c in range(3):
                n = P if c < 2 else NB
                for j in range(2):
                    key = ("htok", c, j)
                    full(dve, key)
                    free(key, v.tensor_copy(htok[0:n, c, j * 512:(j + 1) * 512], bank(key)[0:n, :]))
            full(dve, ("selT0",))
            free(("selT0",), v.tensor_copy(selT[0:CAP, 0, :], bank(("selT0",))[0:CAP, 0:T]))
            for j in range(2):
                key = ("gat0", j)
                full(dve, key)
                free(key, v.tensor_copy(hg[:, 0, 4 * j:4 * j + 4, :], bank(key)[:, 0:4 * CAP].rearrange("p (t s) -> p t s", t=4)))
            side_full = [sem("side_full6"), sem("side_full7")]
            side_taken = [sem("side_taken6"), sem("side_taken7")]
            for name in ("up_taken", "ys_ready", "side_taken6", "side_taken7"):
                dve.sem_inc(sem(name), 1)
            dve.wait_ge(sem("rounds_known"), 1)
            pairs = dve.value_load(rounds[0:1, 0:1], min_val=NE // 2, max_val=3 * NE // 2)

            def scatter_add(n):
                for t in range(KT):
                    b = t % 2
                    dve.wait_ge(side_full[b], n * (6, 5)[b] + (t // 2 + 1))
                    v.tensor_tensor(xT[:, t, :], xT[:, t, :], psum[:, 6 + b, 0:T], ALU.add).then_inc(side_taken[b], 1)

            with dve.Fori(0, pairs) as pair:
                for h in range(2):
                    n = pair * 2 + h
                    links = [0]

                    def link(ins):
                        links[0] += 1
                        ins.then_inc(sem("choose_chain"), 1)
                        dve.wait_ge(sem("choose_chain"), n * 2 + links[0])

                    dve.wait_ge(side_taken[0], n * 6 + 1)
                    choose((n + 1) & (NE - 1), link)
                    for f in range(ET):
                        dve.wait_ge(eu, n * (2 * ET) + (4 * (f // 2) + 2 + f % 2 + 1))
                        dve.wait_ge(sem("gate_taken"), n * ET + (f + 2))
                        v.tensor_tensor(ehid[:, f, :], esil[:, f % 2, :], psum[:, 2 + f % 2, 0:CAP], ALU.mult).then_inc(sem("up_taken"), 1)
                    scatter_add(n)
            scatter_add(dve.snap(pairs * 2))
            dve.wait_ge(side_taken[1], pairs * 10 + 5)
            norm(8, "final", 0, xT[:, :, :], hT, hT[:, :, :], root=sem("final_root"))
            for c in range(3):
                n = P if c < 2 else NB
                dve.wait_ge(sem("final_tok"), c + 1)
                v.tensor_copy(fin[0:n, c, :], psum[0:n, 1 + 2 * c:3 + 2 * c, :].rearrange("p a b -> p (a b)")).then_inc(sem("fin_tok"), 1)


_INS = ["x_prompt", "x_sample", "state_ssm", "state_ssm_conv", "state_ret", "state_pool", "state_conv",
        "cache_mem_k", "cache_mem_v", "mem_prompt", "norm_mix", "norm_cross", "norm_ffn", "norm_mem", "norm_final",
        "w_in_even", "ssd_conv_w", "ssd_conv_b", "ssd_dt_bias", "ssd_a_log", "ssd_d", "ssd_norm", "w_out_even",
        "ffn_w1", "ffn_w3", "ffn_w2", "w_in_odd", "pool_w", "pool_scale", "conv_w", "conv_b", "conv_norm_g",
        "conv_norm_b", "w_out_odd", "router_w", "router_b", "moe_w1", "moe_w3", "moe_w2",
        "xattn_q", "xattn_k", "xattn_v", "xattn_o"]
_OUTS = [(1, NP, DM), (NB, 1, DM), (2, 1, ML, XH, 256), (2, 1, ML, XH, 256),
         (1, 1, SH, SN, SD), (1, 1, SCONV - 1, 1536), (1, 1, RH, RK, RV), (1, 1, PST, 512), (1, 1, CK - 1, 512),
         (1, NB, SH, SN, SD), (1, NB, SCONV - 1, 1536), (1, NB, RH, RK, RV), (1, NB, PST, 512), (1, NB, CK - 1, 512)]


def kernel(**inputs):
    import numpy as _np
    import concourse.bacc as _bacc
    from concourse.bass_utils import run_bass_kernel_spmd as _run

    nc = _bacc.Bacc("TRN2", target_bir_lowering=False, num_devices=1)
    arrays, w = {}, {}
    for name in _INS:
        a = _np.ascontiguousarray(inputs[name])
        arrays[f"in_{name}_dram"] = a
        w[name] = nc.dram_tensor(f"in_{name}_dram", a.shape, F32, kind="ExternalInput").ap()
    arrays["in_consts_dram"] = CONST_ARRAY
    consts = nc.dram_tensor("in_consts_dram", CONST_ARRAY.shape, F32, kind="ExternalInput").ap()
    outs = [nc.dram_tensor(f"out_{i}_dram", shape, F32, kind="ExternalOutput").ap() for i, shape in enumerate(_OUTS)]
    trunk_kernel(nc, w, consts, outs)
    r = _run(nc, [arrays], core_ids=[0])
    return tuple(r.results[0][f"out_{i}_dram"] for i in range(len(_OUTS)))
```

```python
from contextlib import ExitStack

import numpy as np

import concourse.bass as bass
from concourse import mybir

F32 = mybir.dt.float32
U32 = mybir.dt.uint32
ALU = mybir.AluOpType
ACT = mybir.ActivationFunctionType
AX = mybir.AxisListType.X

P = 128
DM = 1024
KT = DM // P
NP = 256
NB = 8
T = NP + NB
NC = NP // P
EPS = 1e-6
SH, SD, SG, SN = 16, 64, 2, 128
RH, RK, RV = 8, 64, 128
XT = 12
SCONV = 4
FF = 2816
NE, FE = 8, 1792
CAP = 96
ML, XH = 256, 4
WINDOWS = (2, 4, 8, 16)
PST = max(WINDOWS) - 1
CK = 31
OT = 4
PAST = 2048
ROPE_BASE = 10000.0

RING = 11
TRUNK_RING = 6
SLOT_K, SLOT_N = 8, 256
SLOT = SLOT_K * SLOT_N
BANKS = 8
FT, ET = FF // P, FE // P
KV_SLOTS = RING - TRUNK_RING

PA = dict(mix=0, cross=16, ffn=32, mem=48, final=64, gnorm=72, scw=80)
PB = dict(scb=128, pscale=140, ccb=144, cng=148, cnb=152)
PC = dict(ccw=156)
COL = {**PA, **PB, **PC}
NPAR = 280

CONST = {}


def _add(name, a):
    CONST[name] = np.ascontiguousarray(a, np.float32)


def _constants():
    i = np.arange(P)
    _add("ident", np.eye(P))
    _add("ones", np.ones((P, P)))
    half = RK // 2
    rot = np.zeros((P, P))
    for d in range(P):
        if d % RK < half:
            rot[d + half, d] = -1.0
        else:
            rot[d - half, d] = 1.0
    _add("rot", rot)
    inv = np.float32(ROPE_BASE) ** (-np.arange(half, dtype=np.float32) / np.float32(half))
    pos = np.concatenate([np.arange(NP), np.full(NB, PAST)]).astype(np.float32)
    ang = (pos[None, :] * inv[i % half][:, None]).astype(np.float32)
    for n, s in (("q", 1.0), ("k", RK ** -0.5)):
        _add("cos" + n, np.cos(ang.astype(np.float64)) * s)
        _add("sin" + n, np.sin(ang.astype(np.float64)) * s)
    _add("causal", (i[None, :] >= i[:, None]) * 1.0)
    lg = np.log1p(-np.exp2(-5.0 - np.arange(RH)))
    d = i[None, :] - i[:, None]
    dec = np.where(d >= 0, np.exp(np.minimum(lg[:, None, None] * d, 0.0)), 0.0)
    order = [2 * hh + par for par in range(2) for hh in range(RH // 2)]
    _add("dret", dec[order].transpose(1, 0, 2).reshape(P, RH * P))
    _add("gq", np.exp(lg[order][None, :] * (i[:, None] + 1)))
    _add("wk", np.exp(lg[None, :] * (P - 1 - i[:, None])))
    par = i // RK
    hh = np.arange(RH // 2)
    _add("gchunk", np.exp(lg[2 * hh[None, :] + par[:, None]] * P))
    _add("gone", np.exp(lg[2 * hh[None, :] + par[:, None]]))
    _add("iota", np.tile(np.arange(CAP), (P, 1)))
    cnt = np.stack([1.0 / np.minimum(np.arange(PST + 1) + 1.0, w) for w in WINDOWS])
    _add("invcnt", np.tile(cnt.reshape(1, -1), (P, 1)))


_constants()
EVEN_CONST = ("rot", "cosq", "sinq", "cosk", "sink", "dret", "gq", "wk", "gchunk", "gone")
BASE_CONST = ("ident", "ones", "causal", "iota", "invcnt")
CONST_AT = {}
_off = 0
for _n in BASE_CONST + EVEN_CONST:
    CONST_AT[_n] = (_off, CONST[_n].shape[1])
    _off += CONST[_n].shape[1]
N_CONST = _off
N_BASE = sum(CONST[_n].shape[1] for _n in BASE_CONST)
CONST_ARRAY = np.concatenate([CONST[_n] for _n in BASE_CONST + EVEN_CONST], axis=1)


def weight_items(w):
    items = []

    def block(name, wm, n0, n, block_no, chunks):
        for kc, (k0, kn) in enumerate(chunks):
            items.append((name, block_no, kc, wm[k0 * P:(k0 + kn) * P, n0:n0 + n].rearrange("(t p) n -> p t n", p=P)))

    def whole(name, wm, n, chunks):
        for b in range(n // SLOT_N):
            block(name, wm, b * SLOT_N, SLOT_N, b, chunks)

    full = [(0, 8)]
    win = w["w_in_even"][0]
    cols = dict(z=0, xbc=1024, dt=2560, q=2576, k=3088, v=3600, g=4624)
    for name, nb in (("xbc", 6), ("dt", 1), ("q", 2), ("k", 2), ("v", 4), ("z", 4), ("g", 4)):
        for b in range(nb):
            n = SH if name == "dt" else SLOT_N
            block(name, win, cols[name] + b * SLOT_N, n, b, full)
    whole("wout0", w["w_out_even"][0], DM, [(0, 8), (8, 8)])

    def memory(l):
        whole(f"xk{l}", w["xattn_k"][l], DM, full)
        whole(f"xv{l}", w["xattn_v"][l], DM, full)

    def cross(l):
        whole(f"xq{l}", w["xattn_q"][l], DM, full)
        whole(f"xo{l}", w["xattn_o"][l], DM, full)

    memory(0)
    cross(0)
    for b in range(FF // SLOT_N):
        block("f1", w["ffn_w1"][0], b * SLOT_N, SLOT_N, b, full)
        block("f3", w["ffn_w3"][0], b * SLOT_N, SLOT_N, b, full)
    whole("f2", w["ffn_w2"][0], DM, [(0, 8), (8, 8), (16, 6)])
    whole("win1", w["w_in_odd"][0], 1536, full)
    memory(1)
    whole("wout1", w["w_out_odd"][0], DM, full)
    cross(1)
    return items


def ssd_sample(b):
    return [("xb", b, 0), ("xb", b, 1)] + ([("ys", b - 1)] if b else [])


def ret_sample(b):
    return [("vb", b)] + ([("os", b - 1, p) for p in range(2)] if b else [])


MEM_NORM, CROSS_NORM, ODD_NORM = (1, 4), (2, 6), 5


def memory_rows(l):
    return [("mT", l, j) for j in range(4)] + [("ss", MEM_NORM[l])]


def psum_groups():
    g = [("xT", t) for t in range(KT)] + [("params",), ("cst",)]

    def lin(name, n):
        return [(name, t) for t in range(n)]

    g += [("ss", 0)] + lin("xbc", 12) + [("dt", 0)] + lin("q", 4) + [("tail0", j) for j in range(3)] + lin("k", 4) + lin("v", 8)
    g += [("dtT",), ("dbc",), ("Btok",)] + [("xtok", c, j) for c in range(NC) for j in range(2)] + [("CB",)]
    g += [("xstok", 0), ("xstok", 1), ("eab",), ("bc", 0, 0, 0), ("bc", 0, 0, 1)]
    for s in range(NC * SG):
        if s < 3:
            g += [("bc", (s + 1) // SG, (s + 1) % SG, j) for j in range(2)]
        g += ssd_sample(2 * s)
        g += [("y", s // SG, s % SG)] + ([("yi", s % SG)] if s >= SG else []) + [("kv", s // SG, s % SG)]
        g += [("z", 2 * s), ("z", 2 * s + 1)]
        g += ssd_sample(2 * s + 1)
    g += [("ys", NB - 1)]
    g += [("yT", t) for t in range(KT)]
    g += [("g", 0), ("g", 1), ("yss", 0), ("yss", 1)]
    g += [("rot", i) for i in range(8)]
    g += [("vstok", 0), ("vstok", 1), ("g", 2), ("g", 3)]
    g += [("ktok", c) for c in range(NC)] + [("vtok", c, j) for c in range(NC) for j in range(2)]
    for c in range(NC):
        g += [("rs", c, p) for p in range(2)]
        g += ret_sample(2 * c)
        g += [("g", 4 + 2 * c), ("g", 5 + 2 * c)]
        g += [("ro", c, p) for p in range(2)]
        if c:
            g += [("ri", p) for p in range(2)]
        g += [("rkv", c)]
        g += ret_sample(2 * c + 1)
    for b in range(4, NB):
        g += ret_sample(b)
    g += [("os", NB - 1, p) for p in range(2)]
    g += [("oT", h) for h in range(RH)] + [("oss",)]
    g += memory_rows(0)
    g += lin("wout0", KT)

    def mem_k(l):
        return [(f"xk{l}", b, m) for b in range(4) for m in range(2)] + [("KT", l, j) for j in range(4)]

    def mem_v(l):
        return [(f"xv{l}", b, m) for b in range(4) for m in range(2)]

    def cross(l):
        r = [("ss", CROSS_NORM[l])] + lin(f"xq{l}", KT)
        r += [("qs", l, 0), ("qs", l, 1)]
        r += [("S", l, lt, hp) for lt in range(2) for hp in range(2)]
        r += [("PT", l, lt, hp) for lt in range(2) for hp in range(2)]
        r += [("ao", l, t) for t in range(KT)]
        r += [("qb", l, b, j) for b in range(NB) for j in range(2)]
        r += [("sT", l), ("pT", l), ("aos", l)] + lin(f"xo{l}", KT)
        return r

    g += mem_k(0) + mem_v(0) + cross(0)
    g += [("ss", 3)]
    for b in range(FF // SLOT_N):
        g += [("f1", 2 * b), ("f1", 2 * b + 1), ("f3", 2 * b), ("f3", 2 * b + 1)]
    g += memory_rows(1)
    g += lin("f2", KT)
    g += [("ost", j) for j in range(3)]
    g += [("ss", ODD_NORM)] + lin("win1", 12) + [("tail1",), ("tail2",)]
    g += mem_k(1) + [("pw", i) for i in range(4)] + mem_v(1) + [("mu",), ("var",)]
    g += lin("wout1", KT)
    g += cross(1)
    g += [("ss", 7), ("logit",), ("rank",)] + [("htok", c, j) for c in range(3) for j in range(2)]
    g += [("selT0",), ("gat0", 0), ("gat0", 1)]
    g += [("idle", i) for i in range(-len(g) % BANKS)]
    return g


def trunk_kernel(nc, w, consts, outs):
    (y_p, y_s, mk_p, mv_p, ssm_p, ssmc_p, ret_p, pool_p, conv_p, ssm_s, ssmc_s, ret_s, pool_s, conv_s) = outs
    items = weight_items(w)
    item_at = {(n, b, kc): i for i, (n, b, kc, _) in enumerate(items)}
    groups = psum_groups()
    G = {k: i for i, k in enumerate(groups)}
    assert len(G) == len(groups)

    ctx = ExitStack()
    with ctx:
        sems = {}

        def sem(name):
            if name not in sems:
                sems[name] = ctx.enter_context(nc.semaphore(name))
            return sems[name]

        def sb(name, shape, dt=F32):
            return ctx.enter_context(nc.sbuf_tensor(name, shape, dt))

        ring = sb("ring", [P, RING, SLOT])
        xT = sb("xT", [P, KT, T])
        hT = sb("hT", [P, KT, T])
        par = sb("par", [P, NPAR])
        cbase = sb("cbase", [P, N_BASE])
        rstd = sb("rstd", [P, T])
        eps = sb("eps", [P, 1])
        small = sb("small", [P, 160])
        arena_n = 25160
        arena = sb("arena", [P, arena_n])
        psum = ctx.enter_context(nc.psum_tensor("psum", [P, BANKS, 512], F32))
        bank_full = [sem(f"bank_full{b}") for b in range(BANKS)]
        bank_free = [sem(f"bank_free{b}") for b in range(BANKS)]
        slot_full = [sem(f"slot_full{s}") for s in range(RING)]
        chunk_used = sem("chunk_used")
        eu, ed, eh = sem("expert_up"), sem("expert_down"), sem("expert_half")
        base_full = [16 * sum(i % TRUNK_RING == s for i in range(len(items))) if s < TRUNK_RING else 0 for s in range(RING)]

        class Region:

            def __init__(self, at=0):
                self.at = at

            def take(self, *shape):
                n = int(np.prod(shape))
                v = view(self.at, *shape)
                self.at += n
                assert self.at <= arena_n, self.at
                return v

        def view(at, *shape):
            n = int(np.prod(shape))
            v = arena[:, at:at + n]
            if len(shape) == 2:
                v = v.rearrange("p (a b) -> p a b", a=shape[0])
            if len(shape) == 3:
                v = v.rearrange("p (a b c) -> p a b c", a=shape[0], b=shape[1])
            return v

        def const(name):
            at, n = CONST_AT[name]
            if name in BASE_CONST:
                return cbase[:, at:at + n]
            return E_const[:, at - N_BASE:at - N_BASE + n]

        X = ring[:, TRUNK_RING:, :].rearrange("p a b -> p (a b)")
        x_taken = [0]

        def take_x(*shape):
            n, at = int(np.prod(shape)), x_taken[0]
            x_taken[0] += n
            assert x_taken[0] <= (RING - TRUNK_RING) * SLOT
            v = X[:, at:at + n]
            if len(shape) == 2:
                v = v.rearrange("p (a b) -> p a b", a=shape[0])
            return v

        R = Region()
        E_const = R.take(N_CONST - N_BASE)
        zg = R.take(16, T)
        xr_at = R.at
        xr = R.take(XT, SCONV - 1 + NP)
        xrs = R.take(XT, NB, SCONV)
        xc = R.take(XT, T)
        qk = R.take(8, T)
        vT = R.take(RH, T)
        xdt = R.take(NC, DM)
        btok_at = R.at
        Btok = R.take(NC, SG * SN)
        SM = R.take(SG * NC, P)
        xdtw_at = R.at
        xdtw = R.take(DM)
        rs2 = view(R.at, 2, T)
        R.take(1024)
        hst = R.take(SG, 512)
        dtT = R.take(T)
        acT = R.take(T)
        ytok = view(xr_at, NC, DM)
        hb = take_x(3, DM)
        rb = take_x(4, 512)
        S = take_x(4, 512)
        otok = take_x(NC, DM)
        xstok = take_x(DM)
        sqb = view(xr_at, KT, T)
        dtmp = view(xdtw_at, 5, T)
        vstok = view(btok_at, DM)
        vtok = xdt
        ktok = view(xdtw_at, NC, 512)
        tailtok = xdt[:, :, :].rearrange("p a b -> p (a b)")[0:11, 0:1536]
        oTt = xc[:, 0:RH, :]
        rst = hst
        tailT0 = R.take(XT, 11)
        tk = R.take(2, 2, SH)
        tot = R.take(NC, SH)
        wend = R.take(NC, SH)
        eac = R.take(SH)
        etot = R.take(SH)
        eab = R.take(NB, SH)
        eaD = R.take(NB, SH)
        ea = R.take(NB)
        dtst = R.take(SH)
        ysum = R.take(KT)
        oms = R.take(NC, RH)
        ogs = view(xdtw_at, RH, NB)
        junk = view(xdtw_at + 1024 + 2 * T, P)
        cst_keep = R.take(XT * NB * (SCONV - 1))
        Dcol = R.take(KT)
        stage_x = view(xr_at, 2, DM)
        stage_s = view(xr_at + 2 * DM, DM)
        stage_c = view(btok_at, 1536)
        R = Region()
        KTt = R.take(KT, ML)
        Vt = R.take(2, DM)
        Kt = R.take(2, DM)
        R.at = max(xr_at, (FT + 2) * T)
        memtok = R.take(2, DM)
        mT_at = R.at
        mT = R.take(KT, ML)
        odd_at = R.at + KT * ML
        memsq = view(R.at, KT, ML)
        Pr = R.take(4, 2, ML)
        PTt = R.take(XH, 2, NP)
        qT = R.take(KT, T)
        oT = R.take(KT, T)
        qstok = view(mT_at, DM)
        sS = R.take(2, NB * XH)
        Ps = R.take(2 * P)
        pTs = R.take(2, NB * XH)
        kv = X[:, 0:KV_SLOTS * 2 * DM].rearrange("p (s m d) -> p s m d", s=KV_SLOTS, m=2)
        R = Region()
        hid = R.take(FT, T)
        sil = R.take(2, T)
        R = Region(odd_at)
        up = R.take(OT, PST + NP)
        us = R.take(OT, NB, PST + 1)
        gp = R.take(OT, CK - 1 + NP)
        gs = R.take(OT, NB, CK)
        ga = R.take(OT, T)
        mixo = R.take(2 * OT, T)
        w2t = R.take(PST + NP)
        w4t = R.take(PST + NP)
        pooled = R.take(OT, T)
        csq = R.take(OT, T)
        tl1 = R.take(OT, 23)
        tl2 = R.take(OT, 38)
        st_pool = R.take(512)
        st_conv = R.take(2, 512)
        tok1, tok2 = st_conv[:, 0, :], st_conv[:, 1, :]
        pw = R.take(OT, P)
        prods = R.take(NB, CK)
        R = Region()
        ehid = R.take(ET, CAP)
        esil = R.take(2, CAP)
        hg = R.take(2, KT, CAP)
        htok = R.take(3, DM)
        sel = R.take(3, CAP)
        selg = R.take(3, CAP)
        selT = R.take(2, T)
        ys = R.take(DM)
        rwt = R.take(KT, NE)
        rbt = R.take(NE)
        lg = R.take(3, NE)
        mx = R.take(3, NE)
        idxf = R.take(3, NE)
        comb = R.take(3, NE)
        picked = R.take(3, NE)
        slot = R.take(3, NE)
        gt = R.take(3, 4)
        cnts = R.take(4)
        fin = R.take(3, DM)
        idx = sb("idx", [P, 3, NE], U32)
        rounds = sb("rounds", [P, 2], mybir.dt.int32)

        a_log_t, dt_bias_t, D_row, ea_t = small[0:SH, 0:1], small[0:SH, 1:2], small[0:1, 2:2 + SH], small[0:SH, 20:21]
        nmx, rsum = small[:, 24:32], small[:, 32:40]
        nms, rss = small[0:32, 40:41], small[0:32, 41:42]

        def bank(key):
            return psum[:, G[key] % BANKS, :]

        def full(eng, key):
            eng.wait_ge(bank_full[G[key] % BANKS], G[key] // BANKS + 1)

        def taken(eng, key):
            eng.wait_ge(bank_free[G[key] % BANKS], G[key] // BANKS + 1)

        def gain(name, t):
            return par[:, COL[name] + t:COL[name] + t + 1]

        def slot_left(eng, i):
            name, b, kc, _ = items[i]
            if (name, b, kc + 1) in item_at:
                eng.wait_ge(chunk_used, sum((n, bb, k + 1) in item_at for n, bb, k, _ in items[:i + 1]))
            elif (name, b, 1) in G:
                full(eng, (name, b, 1))
            else:
                full(eng, (name, b if name == "dt" else 2 * b + 1))

        def kv_in(eng, l, n):
            i = 2 * NB * l + n
            eng.wait_ge(sem(f"kv_in{i % KV_SLOTS}"), 16 * (i // KV_SLOTS + 1))
            return kv[:, i % KV_SLOTS, :, :]

        def even_stored(eng):
            for j in range(3):
                eng.wait_ge(sem(f"h_out{j}"), 16 * len(range(j, NB, 3)))
            for j in range(4):
                eng.wait_ge(sem(f"r_out{j}"), 32 * len(range(j, NB, 4)))
            eng.wait_ge(sem("tail0_out"), 32)

        last_in_slot = [max(i for i in range(len(items)) if i % TRUNK_RING == s) for s in range(TRUNK_RING)]
        block = ctx.enter_context(nc.Block())

        def slot_view(i, k, n):
            return ring[:, i % RING, 0:k * n].rearrange("p (k n) -> p k n", k=k)

        @block.sync
        def _(sp):
            for i, (name, b, kc, src) in enumerate(items):
                if i >= TRUNK_RING:
                    slot_left(sp, i - TRUNK_RING)
                k, n = src.shape[1], src.shape[2]
                sp.dma_start(slot_view(i % TRUNK_RING, k, n), src).then_inc(slot_full[i % TRUNK_RING], 16)
            ups = [w[n][0].rearrange("e (t p) n -> p e t n", p=P) for n in ("moe_w1", "moe_w3")]
            down = w["moe_w2"][0].rearrange("e (t p) n -> p e t n", p=P)

            def expert_load(e, j):
                pick = slice(e, e + 1) if isinstance(e, int) else bass.ds(e, 1)
                if j < 14:
                    src, k = ups[j % 2][:, pick, :, (j // 2) * 256:(j // 2 + 1) * 256], 8
                else:
                    q = j - 14
                    src, k = down[:, pick, 7 * (q % 2):7 * (q % 2) + 7, (q // 2) * 256:(q // 2 + 1) * 256], 7
                sp.dma_start(slot_view(j, k, 256), src.rearrange("p e t n -> p (e t) n")).then_inc(slot_full[j % RING], 16)

            def expert_left(n, j):
                if j < 14:
                    sp.wait_ge(eu, n * (2 * ET) + 2 * (j + 1))
                else:
                    sp.wait_ge(eh if j % 2 == 0 else ed, n * 4 + ((j - 14) // 2 + 1))

            full(sp, ("aos", 1))
            for j in range(TRUNK_RING, RING):
                expert_load(0, j)
            for j in range(TRUNK_RING):
                slot_left(sp, last_in_slot[j])
                expert_load(0, j)
            sp.wait_ge(sem("rounds_known"), 1)
            steps = sp.value_load(rounds[0:1, 1:2], min_val=NE - 1, max_val=3 * NE - 1)
            with sp.Fori(0, steps) as n:
                e, e_next = n & (NE - 1), (n + 1) & (NE - 1)
                sp.wait_ge(eu, e + e_next + 1)
                for j in range(RING, 2 * RING):
                    if j != 14:
                        expert_left(n, j - RING + (j == 13))
                    expert_load(e, j)
                for j in range(RING):
                    expert_left(n, j + RING)
                    expert_load(e_next, j)
            for j in range(RING, 2 * RING):
                expert_left(steps, j - RING)
                expert_load(NE - 1, j)

        @block.gpsimd
        def _(pool):
            def load(dst, src, s):
                pool.dma_start(dst, src).then_inc(sem(s), 16)

            stored = [0]

            def store(dst, src):
                pool.dma_start(dst, src).then_inc(sem("stored"), 16)
                stored[0] += 16

            load(cbase[:], consts[:, 0:N_BASE], "consts_in")
            nc.gpsimd.memset(eps[:], EPS).then_inc(sem("eps_set"), 1)
            prow = zg[:, 0:3, 0:P]

            def rows(name, src, at, n):
                g = 0 if at < 128 else (1 if at < 156 else 2)
                base = (0, 128, 156)[g]
                load(prow[at - base:at - base + n, g, :], src, "params_in")

            def flat(a):
                return a.rearrange("l (t p) -> (l t) p", p=P)

            rows("mix", flat(w["norm_mix"]), PA["mix"], 16)
            rows("cross", flat(w["norm_cross"]), PA["cross"], 16)
            rows("ffn", flat(w["norm_ffn"]), PA["ffn"], 16)
            rows("mem", flat(w["norm_mem"]), PA["mem"], 16)
            rows("final", w["norm_final"].rearrange("(t p) -> t p", p=P), PA["final"], 8)
            rows("gnorm", flat(w["ssd_norm"]), PA["gnorm"], 8)
            rows("scw", w["ssd_conv_w"][0].rearrange("k (t p) -> (k t) p", p=P), PA["scw"], 48)
            rows("scb", flat(w["ssd_conv_b"]), PB["scb"], 12)
            rows("pscale", flat(w["pool_scale"]), PB["pscale"], 4)
            rows("ccb", flat(w["conv_b"]), PB["ccb"], 4)
            rows("cng", flat(w["conv_norm_g"]), PB["cng"], 4)
            rows("cnb", flat(w["conv_norm_b"]), PB["cnb"], 4)
            rows("ccw", w["conv_w"][0].rearrange("k (t p) -> (k t) p", p=P), PC["ccw"], 124)
            load(stage_c[0:24, :], w["state_ssm_conv"][0].rearrange("b s c -> (b s) c"), "cst_in")
            load(a_log_t, w["ssd_a_log"].rearrange("l h -> h l"), "small_in")
            load(dt_bias_t, w["ssd_dt_bias"].rearrange("l h -> h l"), "small_in")
            load(D_row, w["ssd_d"], "small_in")
            load(E_const, consts[:, N_BASE:N_CONST], "econst_in")
            hsem = [sem(f"h_in{j}") for j in range(3)]
            ssm_v = w["state_ssm"][0].rearrange("b h k v -> b k h v")
            ssm_o = ssm_s[0].rearrange("b h k v -> b k h v")
            hdone = [sem(f"h_out{j}") for j in range(3)]
            rsem = [sem(f"r_in{j}") for j in range(4)]
            rdone = [sem(f"r_out{j}") for j in range(4)]
            ret_v = w["state_ret"][0].rearrange("b (c r) k v -> b r k c v", r=2)
            ret_o = ret_s[0].rearrange("b (c r) k v -> b r k c v", r=2)

            def hload(b):
                if b >= 3:
                    pool.wait_ge(hdone[b % 3], 16 * (b // 3))
                    full(pool, ("ys", b - 3))
                pool.dma_start(hb[:, b % 3, :].rearrange("p (h v) -> p h v", h=SH), ssm_v[b]).then_inc(hsem[b % 3], 16)

            def rload(b):
                if b >= 4:
                    pool.wait_ge(rdone[b % 4], 32 * (b // 4))
                    full(pool, ("os", b - 4, 1))
                for r in range(2):
                    pool.dma_start(rb[64 * r:64 * r + 64, b % 4, :].rearrange("p (c v) -> p c v", v=RV), ret_v[b, r])\
                        .then_inc(rsem[b % 4], 16)

            for b in range(3):
                hload(b)
            for b in range(4):
                rload(b)
            store(ssmc_s[0, :, 0:SCONV - 2, :], w["state_ssm_conv"][0, :, 1:SCONV - 1, :])
            store(pool_s[0, :, 0:PST - 1, :], w["state_pool"][0, :, 1:PST, :])
            store(conv_s[0, :, 0:CK - 2, :], w["state_conv"][0, :, 1:CK - 1, :])
            taken(pool, ("xbc", XT - 1))
            nc.gpsimd.tensor_copy(tailT0[:, :, 0:3], xr[:, :, NP:NP + 3])
            nc.gpsimd.tensor_copy(tailT0[:, :, 3:11], xrs[:, :, :, SCONV - 1]).then_inc(sem("tail0_ready"), 1)
            taken(pool, ("tail0", 2))
            pool.dma_start(ssmc_p[0, 0], tailtok[0:3, :]).then_inc(sem("tail0_out"), 16)
            pool.dma_start(ssmc_s[0, :, SCONV - 2, :], tailtok[3:11, :]).then_inc(sem("tail0_out"), 16)

            taken(pool, ("eab",))
            for b in range(NB):
                pool.wait_ge(hsem[b % 3], 16 * (b // 3 + 1))
                hv = hb[:, b % 3, :].rearrange("p (h v) -> p h v", h=SH)
                nc.gpsimd.tensor_tensor(hv, hv, eab[:, b, :].unsqueeze(2).to_broadcast([P, SH, SD]), ALU.mult)\
                    .then_inc(sem("h_decayed"), 1)
                if b and b + 2 < NB:
                    hload(b + 2)
                taken(pool, ("xb", b, 1))
                pool.dma_start(ssm_o[b], hv).then_inc(hdone[b % 3], 16)
            for g in range(SG):
                taken(pool, ("kv", 1, g))
            pool.dma_start(ssm_p[0, 0].rearrange("h k v -> k h v"), hst[:, :, :].rearrange("p g (h v) -> p (g h) v", v=SD))\
                .then_inc(sem("ssm_p_out"), 16)

            def memload():
                load(memtok[:, 0, :], w["mem_prompt"][0, 0:P, :], "mem_in")
                load(memtok[:, 1, :], w["mem_prompt"][0, P:ML, :], "mem_in")

            full(pool, ("yss", 1))
            memload()
            for b in range(NB):
                pool.wait_ge(rsem[b % 4], 32 * (b // 4 + 1))
                rv = rb[:, b % 4, :].rearrange("p (c v) -> p c v", v=RV)
                nc.gpsimd.tensor_tensor(rv, rv, const("gone").unsqueeze(2).to_broadcast([P, RH // 2, RV]), ALU.mult)\
                    .then_inc(sem("r_decayed"), 1)
                if b and b + 3 < NB:
                    rload(b + 3)
                taken(pool, ("vb", b))
                for r in range(2):
                    pool.dma_start(ret_o[b, r], rb[64 * r:64 * r + 64, b % 4, :].rearrange("p (c v) -> p c v", v=RV))\
                        .then_inc(rdone[b % 4], 16)
                if b == 3:
                    taken(pool, ("rkv", 1))
                    ret_po = ret_p[0, 0].rearrange("(c r) k v -> r k c v", r=2)
                    for r in range(2):
                        pool.dma_start(ret_po[r], rst[64 * r:64 * r + 64, 0, :].rearrange("p (c v) -> p c v", v=RV))\
                            .then_inc(sem("ret_p_out"), 16)
            even_stored(pool)
            pool.wait_ge(sem("ret_p_out"), 32)
            caches = [w["cache_mem_k"], w["cache_mem_v"]]

            def kvload(l, n):
                i = 2 * NB * l + n
                src = caches[n // NB][l, n % NB].rearrange("(m p) h d -> p m (h d)", p=P)
                pool.dma_start(kv[:, i % KV_SLOTS, :, :], src).then_inc(sem(f"kv_in{i % KV_SLOTS}"), 16)

            def memory_out(l):
                taken(pool, (f"xk{l}", 3, 1))
                pool.dma_start(mk_p[l, 0].rearrange("(m p) h d -> p m (h d)", p=P), Kt[:, :, :]).then_inc(sem("kst"), 16)
                taken(pool, (f"xv{l}", 3, 1))
                pool.dma_start(mv_p[l, 0].rearrange("(m p) h d -> p m (h d)", p=P), Vt[:, :, :]).then_inc(sem("vst"), 16)

            def more_kv(l):
                for n in range(KV_SLOTS, 2 * NB):
                    old = n - KV_SLOTS
                    if old < NB:
                        taken(pool, ("qb", l, old, 1))
                    else:
                        pool.wait_ge(sem("v_used"), (NB - 1) * l + old - NB + 1)
                    kvload(l, n)

            pool.wait_ge(sem("mixed_ready"), 1)
            for n in range(KV_SLOTS):
                kvload(0, n)
            memory_out(0)
            more_kv(0)
            taken(pool, ("xo0", KT - 1))
            memload()
            for n in range(KV_SLOTS):
                kvload(1, n)
            load(st_pool[0:120, :], w["state_pool"][0].rearrange("b s c -> (b s) c"), "ost_in")
            for j in range(2):
                load(st_conv[0:120, j, :], w["state_conv"][0, 4 * j:4 * j + 4].rearrange("b s c -> (b s) c"), "ost_in")
            load(pw[:, :, :], w["pool_w"][0].rearrange("g c d -> c g d"), "pw_in")
            pool.wait_ge(sem("odd_raw"), 4)
            nc.gpsimd.tensor_copy(tl1[:, :, 0:15], up[:, :, NP:NP + 15])
            nc.gpsimd.tensor_copy(tl1[:, :, 15:23], us[:, :, :, PST])
            nc.gpsimd.tensor_copy(tl2[:, :, 0:30], gp[:, :, NP:NP + 30])
            nc.gpsimd.tensor_copy(tl2[:, :, 30:38], gs[:, :, :, CK - 1]).then_inc(sem("tail1_ready"), 1)
            taken(pool, ("tail2",))
            for dst, src in ((pool_p[0, 0], tok1[0:15, :]), (pool_s[0, :, PST - 1, :], tok1[15:23, :]),
                             (conv_p[0, 0], tok2[0:30, :]), (conv_s[0, :, CK - 2, :], tok2[30:38, :])):
                pool.dma_start(dst, src).then_inc(sem("odd_out"), 16)
            memory_out(1)
            more_kv(1)
            taken(pool, ("xo1", KT - 1))
            pool.wait_ge(sem("kst"), 32)
            pool.wait_ge(sem("vst"), 32)
            load(rwt[:, :, :], w["router_w"][0].rearrange("(t p) e -> p t e", p=P), "router_in")
            load(rbt[0:1, :], w["router_b"], "router_in")
            pool.wait_ge(sem("fin_tok"), 3)
            for c in range(NC):
                store(y_p[0, c * P:(c + 1) * P, :], fin[:, c, :])
            store(y_s.rearrange("b s d -> (b s) d"), fin[0:NB, 2, :])
            pool.wait_ge(sem("stored"), stored[0])

        @block.tensor
        def _(pe):
            mm, tr = nc.tensor.matmul, nc.tensor.transpose
            ident, ones = const("ident"), const("ones")
            made = [0]

            def begin(key):
                g = G[key]
                assert g == made[0], (key, g, made[0])
                made[0] += 1
                if g >= BANKS:
                    pe.wait_ge(bank_free[g % BANKS], g // BANKS)
                return psum[:, g % BANKS, :]

            def end(key, ins):
                ins.then_inc(bank_full[G[key] % BANKS], 1)

            def arrived(i):
                pe.wait_ge(slot_full[i % TRUNK_RING], 16 * (i // TRUNK_RING + 1))

            def linear(name, nb, chunks, rhs, width=256, tiles=2, first=0):
                for b in range(first, first + nb):
                    outs_ = [begin((name, tiles * b + m)) for m in range(tiles)]
                    base = 0
                    for kc, kn in enumerate(chunks):
                        i = item_at[(name, b, kc)]
                        arrived(i)
                        wv = slot_view(i % TRUNK_RING, kn, width)
                        mw = min(P, width)
                        for m in range(tiles):
                            for k in range(kn):
                                ins = mm(outs_[m][0:mw, 0:T], wv[:, k, m * mw:(m + 1) * mw], rhs(base + k),
                                         start=(base + k == 0), stop=(kc == len(chunks) - 1 and k == kn - 1),
                                         skip_group_check=True)
                            if kc == len(chunks) - 1 and m < tiles - 1:
                                end((name, tiles * b + m), ins)
                        if kc < len(chunks) - 1:
                            ins.then_inc(chunk_used, 1)
                        base += kn
                    end((name, tiles * b + tiles - 1), ins)

            def sumsq(key, src, n, width):
                o = begin(key)
                for k in range(n):
                    ins = mm(o[:, 0:width], ones, src(k), start=(k == 0), stop=(k == n - 1))
                end(key, ins)

            pe.wait_ge(sem("consts_in"), 16)
            pe.wait_ge(sem("x_in"), 48)
            for t in range(KT):
                o = begin(("xT", t))
                for c in range(NC):
                    tr(o[:, c * P:(c + 1) * P], stage_x[:, c, t * P:(t + 1) * P], ident)
                end(("xT", t), tr(o[:, NP:T], stage_s[0:NB, t * P:(t + 1) * P], ident[0:NB, 0:NB]))
            pe.wait_ge(sem("params_in"), 16 * 13)
            prow = zg[:, 0:3, 0:P]
            o = begin(("params",))
            for g, (at, n) in enumerate(((0, 128), (128, 28), (156, 124))):
                ins = tr(o[:, at:at + n], prow[0:n, g, :], ident[0:n, 0:n])
            end(("params",), ins)
            pe.wait_ge(sem("cst_in"), 16)
            o = begin(("cst",))
            for t in range(XT):
                ins = tr(o[:, 24 * t:24 * t + 24], stage_c[0:24, t * P:(t + 1) * P], ident[0:24, 0:24])
            end(("cst",), ins)

            def normed(n):
                pe.wait_ge(sem("sq_ready"), n + 1)
                sumsq(("ss", n), lambda k: hT[:, k, :], KT, T)
                pe.wait_ge(sem("h_ready"), n + 1)

            normed(0)

            def h_in(k):
                return hT[:, k, :]

            linear("xbc", 6, [8], h_in)
            linear("dt", 1, [8], h_in, width=SH, tiles=1)
            linear("q", 2, [8], h_in)
            pe.wait_ge(sem("tail0_ready"), 1)
            for j in range(3):
                o = begin(("tail0", j))
                for t in range(4):
                    ins = tr(o[0:11, t * P:(t + 1) * P], tailT0[:, 4 * j + t, :], ident)
                end(("tail0", j), ins)
            linear("k", 2, [8], h_in)
            linear("v", 4, [8], h_in)

            pe.wait_ge(sem("dt_ready"), 1)
            o = begin(("dtT",))
            for n, src in enumerate((dtT, acT)):
                for c in range(NC):
                    tr(o[:, (2 * n + c) * SH:(2 * n + c + 1) * SH], src[0:SH, c * P:(c + 1) * P], ident[0:SH, 0:SH])
            end(("dtT",), tr(o[0:NB, 4 * SH:5 * SH], dtT[0:SH, NP:T], ident[0:SH, 0:SH]))
            pe.wait_ge(sem("small_in"), 48)
            o = begin(("dbc",))
            end(("dbc",), mm(o[:, 0:SH], ones[0:1, :], D_row, start=True, stop=True))
            pe.wait_ge(sem("xc_ready"), XT)
            o = begin(("Btok",))
            for c in range(NC):
                for g in range(SG):
                    ins = tr(o[:, (2 * c + g) * P:(2 * c + g + 1) * P], xc[:, 8 + g, c * P:(c + 1) * P], ident)
            end(("Btok",), ins)
            for c in range(NC):
                for j in range(2):
                    o = begin(("xtok", c, j))
                    for t in range(4):
                        ins = tr(o[:, t * P:(t + 1) * P], xc[:, 4 * j + t, c * P:(c + 1) * P], ident)
                    end(("xtok", c, j), ins)
            o = begin(("CB",))
            for g in range(SG):
                for c in range(NC):
                    ins = mm(o[:, (2 * g + c) * P:(2 * g + c + 1) * P], xc[:, 8 + g, c * P:(c + 1) * P],
                             xc[:, 10 + g, c * P:(c + 1) * P], start=True, stop=True)
            end(("CB",), ins)
            for j in range(2):
                o = begin(("xstok", j))
                for t in range(4):
                    ins = tr(o[0:NB, t * P:(t + 1) * P], xc[:, 4 * j + t, NP:T], ident)
                end(("xstok", j), ins)
            pe.wait_ge(sem("ead_ready"), 1)
            o = begin(("eab",))
            end(("eab",), mm(o[:, 0:NB * SH], ones[0:SH, :], eaD[0:SH, :, :].rearrange("p b h -> p (b h)"), start=True, stop=True))

            def decay_rows(s):
                c, g = s // SG, s % SG
                for j in range(2):
                    o = begin(("bc", c, g, j))
                    for q in range(4):
                        h = 8 * g + 4 * j + q
                        ins = mm(o[:, q * P:(q + 1) * P], ident[0:SH, h:h + 1].to_broadcast([SH, P]),
                                 acT[0:SH, c * P:(c + 1) * P], start=True, stop=True)
                    end(("bc", c, g, j), ins)

            def sample_y(b):
                o = begin(("ys", b))
                taken(pe, ("xb", b, 1))
                for t in range(KT):
                    ins = mm(o[:, t:t + 1], hb[:, b % 3, t * P:(t + 1) * P], xc[:, 10 + t // 4, NP + b:NP + b + 1],
                             start=True, stop=True)
                end(("ys", b), ins)

            def sample_x(b):
                if b == 0:
                    taken(pe, ("xstok", 0))
                    taken(pe, ("xstok", 1))
                for g in range(SG):
                    o = begin(("xb", b, g))
                    end(("xb", b, g), mm(o, ident[0:NB, b:b + 1].to_broadcast([NB, P]), xstok[0:NB, g * 512:(g + 1) * 512],
                                         start=True, stop=True))
                if b:
                    sample_y(b - 1)

            decay_rows(0)
            for s in range(NC * SG):
                c, g = s // SG, s % SG
                if s < NC * SG - 1:
                    decay_rows(s + 1)
                sample_x(2 * s)
                o = begin(("y", c, g))
                taken(pe, ("xtok", c, g))
                for j in range(2):
                    pe.wait_ge(sem("s_ready"), 2 * s + j + 1)
                    for q in range(4):
                        hl = 4 * j + q
                        ins = mm(o[:, hl * SD:(hl + 1) * SD], S[:, 2 * (s % 2) + j, q * P:(q + 1) * P],
                                 xdt[:, c, (8 * g + hl) * SD:(8 * g + hl + 1) * SD], start=True, stop=True)
                end(("y", c, g), ins)
                if c:
                    o = begin(("yi", g))
                    taken(pe, ("kv", 0, g))
                    end(("yi", g), mm(o, xc[:, 10 + g, P:NP], hst[:, g, :], start=True, stop=True))
                o = begin(("kv", c, g))
                pe.wait_ge(sem("xdtw_ready"), s + 1)
                if s == 0:
                    taken(pe, ("Btok",))
                end(("kv", c, g), mm(o, Btok[:, c, g * P:(g + 1) * P], xdtw[:, g * 512:(g + 1) * 512], start=True, stop=True))
                linear("z", 1, [8], h_in, first=s)
                sample_x(2 * s + 1)
            sample_y(NB - 1)
            for c in range(NC):
                for g in range(SG):
                    taken(pe, ("y", c, g))
            for t in range(KT):
                o = begin(("yT", t))
                for c in range(NC):
                    ins = tr(o[:, c * P:(c + 1) * P], ytok[:, c, t * P:(t + 1) * P], ident)
                end(("yT", t), ins)
            linear("g", 1, [8], h_in, first=0)
            pe.wait_ge(sem("ysq_ready"), 1)
            for g in range(SG):
                sumsq(("yss", g), lambda k: sqb[:, 4 * g + k, :], 4, T)

            pe.wait_ge(sem("econst_in"), 16)
            for i in range(8):
                o = begin(("rot", i))
                taken(pe, (("q", i) if i < 4 else ("k", i - 4)))
                end(("rot", i), mm(o[:, 0:T], const("rot"), qk[:, i, :], start=True, stop=True))
            for t in range(RH):
                taken(pe, ("v", t))
            for j in range(2):
                o = begin(("vstok", j))
                for t in range(4):
                    ins = tr(o[0:NB, t * P:(t + 1) * P], vT[:, 4 * j + t, NP:T], ident)
                end(("vstok", j), ins)
            linear("g", 1, [8], h_in, first=1)
            pe.wait_ge(sem("rot_done"), 8)
            for c in range(NC):
                o = begin(("ktok", c))
                for t in range(4):
                    ins = tr(o[:, t * P:(t + 1) * P], qk[:, 4 + t, c * P:(c + 1) * P], ident)
                end(("ktok", c), ins)
            for c in range(NC):
                for j in range(2):
                    o = begin(("vtok", c, j))
                    for t in range(4):
                        ins = tr(o[:, t * P:(t + 1) * P], vT[:, 4 * j + t, c * P:(c + 1) * P], ident)
                    end(("vtok", c, j), ins)

            def sample_o(b):
                taken(pe, ("vb", b))
                for p in range(2):
                    o = begin(("os", b, p))
                    for hh in range(4):
                        ins = mm(o[:, hh:hh + 1], rb[64 * p:64 * p + 64, b % 4, hh * P:(hh + 1) * P],
                                 qk[64 * p:64 * p + 64, hh, NP + b:NP + b + 1], start=True, stop=True)
                    end(("os", b, p), ins)

            vs4 = vstok[0:NB, :].rearrange("p (c r v) -> p c r v", r=2, v=RV)

            def sample_v(b):
                if b == 0:
                    taken(pe, ("vstok", 0))
                    taken(pe, ("vstok", 1))
                o = begin(("vb", b))
                for p in range(2):
                    ins = mm(o[64 * p:64 * p + 64, :], ident[0:NB, b:b + 1].to_broadcast([NB, 64]), vs4[:, :, p, :],
                             start=True, stop=True)
                end(("vb", b), ins)
                if b:
                    sample_o(b - 1)

            for c in range(NC):
                for p in range(2):
                    o = begin(("rs", c, p))
                    for hh in range(4):
                        ins = mm(o[:, hh * P:(hh + 1) * P], qk[64 * p:64 * p + 64, 4 + hh, c * P:(c + 1) * P],
                                 qk[64 * p:64 * p + 64, hh, c * P:(c + 1) * P], start=True, stop=True)
                    end(("rs", c, p), ins)
                sample_v(2 * c)
                linear("g", 1, [8], h_in, first=2 + c)
                for j in range(2):
                    taken(pe, ("vtok", c, j))
                for p in range(2):
                    o = begin(("ro", c, p))
                    taken(pe, ("rs", c, p))
                    for hh in range(4):
                        h = 2 * hh + p
                        ins = mm(o[:, hh * P:(hh + 1) * P], S[:, 2 * c + p, hh * P:(hh + 1) * P], vtok[:, c, h * RV:(h + 1) * RV],
                                 start=True, stop=True)
                    end(("ro", c, p), ins)
                if c:
                    taken(pe, ("rkv", 0))
                    for p in range(2):
                        o = begin(("ri", p))
                        for hh in range(4):
                            ins = mm(o[:, hh * P:(hh + 1) * P], qk[64 * p:64 * p + 64, hh, P:NP],
                                     rst[64 * p:64 * p + 64, 0, hh * P:(hh + 1) * P], start=True, stop=True)
                        end(("ri", p), ins)
                o = begin(("rkv", c))
                taken(pe, ("ktok", c))
                for hh in range(4):
                    for p in range(2):
                        h = 2 * hh + p
                        ins = mm(o[64 * p:64 * p + 64, hh * P:(hh + 1) * P], ktok[:, c, h * RK:(h + 1) * RK],
                                 vtok[:, c, h * RV:(h + 1) * RV], start=True, stop=True)
                end(("rkv", c), ins)
                sample_v(2 * c + 1)
            for b in range(4, NB):
                sample_v(b)
            sample_o(NB - 1)
            pe.wait_ge(sem("o_scaled"), NC)
            for h in range(RH):
                o = begin(("oT", h))
                at = ((h % 2) * 4 + h // 2) * P
                for c in range(NC):
                    ins = tr(o[:, c * P:(c + 1) * P], otok[:, c, at:at + P], ident)
                end(("oT", h), ins)
            o = begin(("oss",))
            pe.wait_ge(sem("osq_ready"), 1)
            end(("oss",), mm(o[:, 0:RH * NB], ones, ogs.rearrange("p h b -> p (h b)"), start=True, stop=True))

            def memory_rows(l):
                pe.wait_ge(sem("mem_in"), 32 * (l + 1))
                for j in range(4):
                    o = begin(("mT", l, j))
                    for t in range(2):
                        for m in range(2):
                            ins = tr(o[:, (2 * t + m) * P:(2 * t + m + 1) * P], memtok[:, m, (2 * j + t) * P:(2 * j + t + 1) * P], ident)
                    end(("mT", l, j), ins)
                n = MEM_NORM[l]
                pe.wait_ge(sem("sq_ready"), n + 1)
                sumsq(("ss", n), lambda k: memsq[:, k, :], KT, ML)

            def tokmajor(name):
                for b in range(4):
                    i = item_at[(name, b, 0)]
                    arrived(i)
                    wv = slot_view(i % TRUNK_RING, 8, 256)
                    for m in range(2):
                        o = begin((name, b, m))
                        for k in range(KT):
                            ins = mm(o[:, 0:256], mT[:, k, m * P:(m + 1) * P], wv[:, k, :], start=(k == 0), stop=(k == KT - 1))
                        end((name, b, m), ins)

            def memory_k(l):
                pe.wait_ge(sem("h_ready"), MEM_NORM[l] + 1)
                tokmajor(f"xk{l}")
                taken(pe, (f"xk{l}", 3, 1))
                for j in range(4):
                    o = begin(("KT", l, j))
                    for t in range(2):
                        for m in range(2):
                            ins = tr(o[:, (2 * t + m) * P:(2 * t + m + 1) * P], Kt[:, m, (2 * j + t) * P:(2 * j + t + 1) * P], ident)
                    end(("KT", l, j), ins)

            memory_rows(0)
            pe.wait_ge(sem("mixed_ready"), 1)
            linear("wout0", 4, [8, 8], lambda k: zg[:, k, :])

            def cross(l):
                normed(CROSS_NORM[l])
                linear(f"xq{l}", 4, [8], h_in)
                taken(pe, (f"xq{l}", KT - 1))
                for j in range(2):
                    o = begin(("qs", l, j))
                    for t in range(4):
                        ins = tr(o[0:NB, t * P:(t + 1) * P], qT[:, 4 * j + t, NP:T], ident)
                    end(("qs", l, j), ins)
                for j in range(4):
                    taken(pe, ("KT", l, j))
                for lt in range(2):
                    for hp in range(2):
                        o = begin(("S", l, lt, hp))
                        for q in range(2):
                            h = 2 * hp + q
                            for d in range(2):
                                ins = mm(o[:, q * ML:(q + 1) * ML], qT[:, 2 * h + d, lt * P:(lt + 1) * P], KTt[:, 2 * h + d, :],
                                         start=(d == 0), stop=(d == 1))
                        end(("S", l, lt, hp), ins)
                n = 0
                for lt in range(2):
                    for hp in range(2):
                        o = begin(("PT", l, lt, hp))
                        n += 1
                        pe.wait_ge(sem("p_ready"), 4 * l + n)
                        for q in range(2):
                            for m in range(2):
                                ins = tr(o[:, (2 * q + m) * P:(2 * q + m + 1) * P], Pr[:, 2 * lt + hp, q, m * P:(m + 1) * P], ident)
                        end(("PT", l, lt, hp), ins)
                taken(pe, (f"xv{l}", 3, 1))
                for lt in range(2):
                    for hp in range(2):
                        taken(pe, ("PT", l, lt, hp))
                for t in range(KT):
                    o = begin(("ao", l, t))
                    for m in range(2):
                        ins = mm(o[:, 0:NP], Vt[:, m, t * P:(t + 1) * P], PTt[:, t // 2, m, :], start=(m == 0), stop=(m == 1))
                    end(("ao", l, t), ins)
                taken(pe, ("qs", l, 0))
                taken(pe, ("qs", l, 1))
                for b in range(NB):
                    for j in range(2):
                        o = begin(("qb", l, b, j))
                        end(("qb", l, b, j), mm(o, ident[0:NB, b:b + 1].to_broadcast([NB, P]), qstok[0:NB, j * 512:(j + 1) * 512],
                                                start=True, stop=True))
                o = begin(("sT", l))
                taken(pe, ("qb", l, NB - 1, 1))
                for m in range(2):
                    ins = tr(o[0:32, m * P:(m + 1) * P], sS[:, m, :], ident)
                end(("sT", l), ins)
                o = begin(("pT", l))
                pe.wait_ge(sem("ps_ready"), l + 1)
                for m in range(2):
                    ins = tr(o[:, m * 32:(m + 1) * 32], Ps[0:32, m * P:(m + 1) * P], ident[0:32, 0:32])
                end(("pT", l), ins)
                o = begin(("aos", l))
                taken(pe, ("pT", l))
                for b in range(NB):
                    rows = kv_in(pe, l, NB + b)
                    for t in range(KT):
                        for m in range(2):
                            ins = mm(o[:, t * NB + b:t * NB + b + 1], rows[:, m, t * P:(t + 1) * P],
                                     pTs[:, m, b * XH + t // 2:b * XH + t // 2 + 1], start=(m == 0), stop=(m == 1))
                    if b < NB - 1:
                        ins.then_inc(sem("v_used"), 1)
                end(("aos", l), ins)
                taken(pe, ("aos", l))
                for t in range(KT):
                    taken(pe, ("ao", l, t))
                linear(f"xo{l}", 4, [8], lambda k: oT[:, k, :])

            memory_k(0)
            tokmajor("xv0")
            cross(0)
            normed(3)
            for b in range(FF // SLOT_N):
                for name in ("f1", "f3"):
                    i = item_at[(name, b, 0)]
                    arrived(i)
                    wv = slot_view(i % TRUNK_RING, 8, 256)
                    for m in range(2):
                        o = begin((name, 2 * b + m))
                        for k in range(KT):
                            ins = mm(o[:, 0:T], wv[:, k, m * P:(m + 1) * P], hT[:, k, :], start=(k == 0), stop=(k == KT - 1))
                        end((name, 2 * b + m), ins)
            memory_rows(1)
            for t in range(FT):
                taken(pe, ("f3", t))
            linear("f2", 4, [8, 8, 6], lambda k: hid[:, k, :])

            pe.wait_ge(sem("ost_in"), 48)
            for j in range(3):
                o = begin(("ost", j))
                src = st_pool if j == 0 else st_conv[:, j - 1, :]
                for t in range(4):
                    ins = tr(o[:, t * 120:(t + 1) * 120], src[0:120, t * P:(t + 1) * P], ident[0:120, 0:120])
                end(("ost", j), ins)
            normed(ODD_NORM)
            linear("win1", 6, [8], h_in)
            pe.wait_ge(sem("tail1_ready"), 1)
            for key, src, n in ((("tail1",), tl1, 23), (("tail2",), tl2, 38)):
                o = begin(key)
                for t in range(4):
                    ins = tr(o[0:n, t * P:(t + 1) * P], src[:, t, :], ident)
                end(key, ins)
            memory_k(1)
            pe.wait_ge(sem("pw_in"), 16)
            pe.wait_ge(sem("pooled"), 4)
            for g in range(OT):
                o = begin(("pw", g))
                end(("pw", g), mm(o[:, 0:T], pw[:, g, :], pooled[:, g, :], start=True, stop=True))
            tokmajor("xv1")
            pe.wait_ge(sem("conv_done"), 4)
            sumsq(("mu",), lambda k: mixo[:, OT + k, :], OT, T)
            pe.wait_ge(sem("csq_ready"), 1)
            sumsq(("var",), lambda k: csq[:, k, :], OT, T)
            pe.wait_ge(sem("conv_act"), 4)
            for g in range(OT):
                taken(pe, ("pw", g))
            linear("wout1", 4, [8], lambda k: mixo[:, k, :])
            cross(1)

            normed(7)
            pe.wait_ge(sem("router_in"), 32)
            o = begin(("logit",))
            for c in range(3):
                n = P if c < 2 else NB
                for k in range(KT):
                    mm(o[0:n, c * NE:(c + 1) * NE], hT[:, k, c * P:c * P + n], rwt[:, k, :], start=(k == 0), stop=False)
                ins = mm(o[0:n, c * NE:(c + 1) * NE], ones[0:1, 0:n], rbt[0:1, :], start=False, stop=True)
            end(("logit",), ins)
            o = begin(("rank",))
            pe.wait_ge(sem("picked_ready"), 1)
            for c in range(3):
                n = P if c < 2 else NB
                for b in range(c):
                    mm(o[0:n, c * NE:(c + 1) * NE], ones[:, 0:n], picked[:, b, :], start=(b == 0), stop=False)
                mm(o[0:n, c * NE:(c + 1) * NE], const("causal")[0:n, 0:n], picked[0:n, c, :], start=(c == 0), stop=True)
            for c in range(3):
                n = P if c < 2 else NB
                ins = mm(o[:, 3 * NE:4 * NE], ones[0:n, :], picked[0:n, c, :], start=(c == 0), stop=(c == 2))
            end(("rank",), ins)
            for c in range(3):
                n = P if c < 2 else NB
                for j in range(2):
                    o = begin(("htok", c, j))
                    for t in range(4):
                        ins = tr(o[0:n, t * P:(t + 1) * P], hT[:, 4 * j + t, c * P:c * P + n], ident)
                    end(("htok", c, j), ins)

            def turn_gates(o):
                for c in range(3):
                    n = P if c < 2 else NB
                    ins = tr(o[0:CAP, c * P:c * P + n], selg[0:n, c, :], ident[0:n, 0:n])
                return ins

            def gather(o, j):
                for t in range(4):
                    for c in range(3):
                        n = P if c < 2 else NB
                        ins = mm(o[:, t * CAP:(t + 1) * CAP], htok[0:n, c, (4 * j + t) * P:(4 * j + t + 1) * P], sel[0:n, c, :],
                                 start=(c == 0), stop=(c == 2))
                return ins

            o = begin(("selT0",))
            pe.wait_ge(sem("sel_ready"), 1)
            end(("selT0",), turn_gates(o))
            taken(pe, ("htok", 2, 1))
            for j in range(2):
                o = begin(("gat0", j))
                end(("gat0", j), gather(o, j))
            for j in range(2):
                taken(pe, ("gat0", j))
            taken(pe, ("selT0",))
            pe.wait_ge(sem("rounds_known"), 1)
            pairs = pe.value_load(rounds[0:1, 0:1], min_val=NE // 2, max_val=3 * NE // 2)
            side_full = [sem("side_full6"), sem("side_full7")]
            side_taken = [sem("side_taken6"), sem("side_taken7")]
            PER = (6, 5)

            def side(n, b, k):
                pe.wait_ge(side_taken[b], n * PER[b] + (k + 1))
                return psum[:, 6 + b, :]

            def scatter(n, h):
                pe.wait_ge(sem("ys_ready"), n * 2 + 1)
                for t in range(KT):
                    o = side(n, t % 2, t // 2)
                    mm(o[:, 0:T], ys[0:CAP, t * P:(t + 1) * P], selT[0:CAP, 1 - h, :], start=True, stop=True)\
                        .then_inc(side_full[t % 2], 1)

            with pe.Fori(0, pairs) as pair:
                for h in range(2):
                    n = pair * 2 + h
                    for j in range(ET // 2):
                        for g in range(2):
                            it = 2 * j + g
                            s, r = it % RING, it // RING
                            pe.wait_ge(slot_full[s], n * 32 + (base_full[s] + 16 * (r + 1)))
                            wv = slot_view(s, 8, 256)
                            for m in range(2):
                                pe.wait_ge(sem("gate_taken" if g == 0 else "up_taken"), n * ET + (max(2 * j + m - 1, 0) + 1))
                                for k in range(KT):
                                    ins = mm(psum[:, 2 * g + m, 0:CAP], wv[:, k, m * P:(m + 1) * P], hg[:, h, k, :],
                                             start=(k == 0), stop=(k == KT - 1))
                                ins.then_inc(eu, 1)
                    scatter(n, h)
                    o = side(n, 0, 4)
                    pe.wait_ge(sem("sel_ready"), n + 2)
                    turn_gates(o).then_inc(side_full[0], 1)
                    gather(side(n, 1, 4), 0).then_inc(side_full[1], 1)
                    gather(side(n, 0, 5), 1).then_inc(side_full[0], 1)
                    pe.wait_ge(sem("up_taken"), n * ET + (ET + 1))
                    pe.wait_ge(sem("ys_ready"), n * 2 + 1)
                    for d in range(4):
                        for kc in range(2):
                            it = 14 + 2 * d + kc
                            s, r = it % RING, it // RING
                            pe.wait_ge(slot_full[s], n * 32 + (base_full[s] + 16 * (r + 1)))
                            wv = slot_view(s, 7, 256)
                            for k in range(7):
                                ins = mm(psum[0:CAP, 4 + d // 2, (d % 2) * 256:(d % 2 + 1) * 256], ehid[:, 7 * kc + k, :], wv[:, k, :],
                                         start=(kc == 0 and k == 0), stop=(kc == 1 and k == 6))
                            ins.then_inc(eh if kc == 0 else ed, 1)
                    pe.wait_ge(sem("gate_taken"), n * ET + (ET + 1))
                    pe.wait_ge(side_taken[0], n * PER[0] + 7)
                    pe.wait_ge(side_taken[1], n * PER[1] + 6)
            scatter(pe.snap(pairs * 2), 0)
            pe.wait_ge(sem("sq_ready"), 9)
            for k in range(KT):
                ins = mm(psum[:, 0, 0:T], ones, hT[:, k, :], start=(k == 0), stop=(k == KT - 1))
            ins.then_inc(sem("final_ss"), 1)
            pe.wait_ge(sem("h_ready"), 9)
            for c in range(3):
                n = P if c < 2 else NB
                for j in range(2):
                    for t in range(4):
                        ins = tr(psum[0:n, 1 + 2 * c + j, t * P:(t + 1) * P], hT[:, 4 * j + t, c * P:c * P + n], ident)
                ins.then_inc(sem("final_tok"), 1)


        @block.scalar
        def _(act):
            af = nc.scalar.activation

            def free(key, ins):
                ins.then_inc(bank_free[G[key] % BANKS], 1)

            for dst, src in ((stage_x[:, 0, :], w["x_prompt"][0, 0:P, :]), (stage_x[:, 1, :], w["x_prompt"][0, P:NP, :]),
                             (stage_s[0:NB, :], w["x_sample"].rearrange("b s d -> (b s) d"))):
                act.dma_start(dst, src).then_inc(sem("x_in"), 16)
            act.wait_ge(sem("eps_set"), 1)

            def norm(n, width=T):
                full(act, ("ss", n))
                free(("ss", n), af(rstd[:, 0:width], bank(("ss", n))[:, 0:width], ACT.Sqrt, scale=1.0 / DM, bias=eps[:, 0:1]))

            norm(0)
            taken(act, ("params",))
            for t in range(XT):
                taken(act, ("xbc", t))
                af(xc[:, t, 0:NP], xr[:, t, 0:NP], ACT.Identity, scale=gain("scw", t), bias=gain("scb", t))\
                    .then_inc(sem("tap0"), 1)

            def gate_out(name, t):
                for i in (t, t + 1):
                    full(act, (name, i))
                    free((name, i), af(zg[:, (0 if name == "z" else 8) + i, :], bank((name, i))[:, 0:T], ACT.Copy))

            act.wait_ge(sem("conv0"), 1)
            for t in range(XT):
                af(xc[:, t, :], xc[:, t, :], ACT.Silu).then_inc(sem("xc_ready"), 1)
            for j in range(3):
                full(act, ("tail0", j))
                free(("tail0", j), af(tailtok[:, j * 512:(j + 1) * 512], bank(("tail0", j))[0:11, :], ACT.Copy))
            act.wait_ge(sem("u_ready"), 1)
            act.wait_ge(sem("small_in"), 48)
            af(ea_t, a_log_t, ACT.Exp)
            af(dtmp[0:SH, 2, :], dtmp[0:SH, 1, :], ACT.Exp).then_inc(sem("e_ready"), 1)
            act.wait_ge(sem("w_ready"), 1)
            af(dtmp[0:SH, 4, :], dtmp[0:SH, 3, :], ACT.Ln).then_inc(sem("ln_ready"), 1)
            act.wait_ge(sem("dt_ready"), 1)
            af(ea[0:SH, :], acT[0:SH, NP:T], ACT.Exp).then_inc(sem("ea_ready"), 1)
            taken(act, ("dtT",))
            af(eac, tk[:, 1, 1, :], ACT.Exp).then_inc(sem("eac_ready"), 1)

            def decays(s):
                c, g = s // SG, s % SG
                for j in range(2):
                    act.wait_ge(sem("diff_ready"), 2 * s + j + 1)
                    sv = S[:, 2 * (s % 2) + j, :]
                    af(sv, sv, ACT.Exp).then_inc(sem("decay_ready"), 1)
                act.wait_ge(sem("wdiff_ready"), s + 1)
                w8 = wend[:, c, 8 * g:8 * g + 8]
                af(w8, w8, ACT.Exp).then_inc(sem("wend_ready"), 1)

            decays(0)
            for s in range(NC * SG):
                if s < NC * SG - 1:
                    decays(s + 1)
                if s == NC * SG - 2:
                    af(etot, tot[:, 1, :], ACT.Exp).then_inc(sem("etot_ready"), 1)
                gate_out("z", 2 * s)
            taken(act, ("z", KT - 1))
            af(zg[:, 0:KT, :], zg[:, 0:KT, :], ACT.Silu).then_inc(sem("z_ready"), 1)
            gate_out("g", 0)
            for g in range(SG):
                full(act, ("yss", g))
                free(("yss", g), af(rs2[:, g, :], bank(("yss", g))[:, 0:T], ACT.Sqrt, scale=1.0 / 512, bias=eps[:, 0:1]))
            gate_out("g", 2)
            for c in range(NC):
                gate_out("g", 4 + 2 * c)
                if c:
                    taken(act, ("g", RH - 1))
                    af(zg[:, KT:, :], zg[:, KT:, :], ACT.Silu).then_inc(sem("g_ready"), 1)
                act.wait_ge(sem("o_rows"), c + 1)
                for h in range(RH):
                    af(junk, otok[:, c, h * P:(h + 1) * P], ACT.Square, accum_out=oms[:, c, h:h + 1]).then_inc(sem("o_squared"), 1)
                    act.wait_ge(sem("o_squared"), RH * c + h + 1)
                af(oms[:, c, :], oms[:, c, :], ACT.Sqrt, scale=1.0 / RV, bias=eps[:, 0:1]).then_inc(sem("o_root"), 1)
            full(act, ("oss",))
            free(("oss",), af(ogs.rearrange("p h b -> p (h b)"), bank(("oss",))[:, 0:RH * NB], ACT.Sqrt, scale=1.0 / RV, bias=eps[:, 0:1]))

            def memory(l):
                for name, dst in (("xk", Kt), ("xv", Vt)):
                    for b in range(4):
                        for m in range(2):
                            key = (f"{name}{l}", b, m)
                            full(act, key)
                            free(key, af(dst[:, m, b * 256:(b + 1) * 256], bank(key)[:, 0:256], ACT.Copy))
                    if name == "xk":
                        for j in range(4):
                            key = ("KT", l, j)
                            full(act, key)
                            free(key, af(KTt[:, 2 * j:2 * j + 2, :].rearrange("p t m -> p (t m)"), bank(key), ACT.Copy))

            def cross(l):
                norm(CROSS_NORM[l])
                n = 0
                for lt in range(2):
                    for hp in range(2):
                        key = ("S", l, lt, hp)
                        n += 1
                        act.wait_ge(sem("mx_ready"), 4 * l + n)
                        for q in range(2):
                            c = 4 * lt + 2 * hp + q
                            ins = af(Pr[:, 2 * lt + hp, q, :], bank(key)[:, q * ML:(q + 1) * ML], ACT.Exp, scale=1.0 / 16,
                                     bias=nmx[:, c:c + 1], accum_out=rsum[:, c:c + 1])
                        free(key, ins)
                for t in range(KT):
                    key = ("ao", l, t)
                    full(act, key)
                    free(key, af(oT[:, t, 0:NP], bank(key)[:, 0:NP], ACT.Copy))
                act.wait_ge(sem("smx_ready"), l + 1)
                free(("sT", l), af(Ps[0:32, :], bank(("sT", l))[0:32, 0:ML], ACT.Exp, scale=1.0 / 16, bias=nms, accum_out=rss))

            norm(MEM_NORM[0], ML)
            memory(0)
            cross(0)
            norm(3)
            for t in range(FT):
                if t >= 2:
                    taken(act, ("f3", t - 2))
                full(act, ("f1", t))
                free(("f1", t), af(sil[:, t % 2, :], bank(("f1", t))[:, 0:T], ACT.Silu))
            norm(MEM_NORM[1], ML)
            norm(ODD_NORM)
            for t in range(OT):
                key = ("win1", 8 + t)
                full(act, key)
                free(key, af(csq[:, t, :], bank(key)[:, 0:T], ACT.Sigmoid))
            for t in range(OT):
                act.wait_ge(sem("odd_raw"), t + 1)
                af(mixo[:, OT + t, 0:NP], gp[:, t, 0:NP], ACT.Identity, scale=gain("ccw", t), bias=gain("ccb", t))\
                    .then_inc(sem("ctap0"), 1)
            memory(1)
            full(act, ("var",))
            free(("var",), af(rstd[:], bank(("var",))[:, 0:T], ACT.Sqrt, scale=1.0 / 512, bias=eps[:, 0:1]))
            for t in range(OT):
                act.wait_ge(sem("cnorm"), t + 1)
                af(mixo[:, OT + t, :], mixo[:, OT + t, :], ACT.Silu, scale=gain("cng", t), bias=gain("cnb", t))\
                    .then_inc(sem("conv_act"), 1)
            cross(1)
            norm(7)
            for c in range(3):
                n = P if c < 2 else NB
                act.wait_ge(sem("gap_ready"), c + 1)
                af(gt[0:n, c, 1:2], gt[0:n, c, 0:1], ACT.Exp).then_inc(sem("gap_exp"), 1)
            act.sem_inc(sem("gate_taken"), 1)
            act.wait_ge(sem("rounds_known"), 1)
            pairs = act.value_load(rounds[0:1, 0:1], min_val=NE // 2, max_val=3 * NE // 2)
            side_full = [sem("side_full6"), sem("side_full7")]
            side_taken = [sem("side_taken6"), sem("side_taken7")]
            with act.Fori(0, pairs) as pair:
                for h in range(2):
                    n = pair * 2 + h
                    for f in range(ET):
                        act.wait_ge(eu, n * (2 * ET) + (4 * (f // 2) + f % 2 + 1))
                        act.wait_ge(sem("up_taken"), n * ET + (max(f - 1, 0) + 1))
                        af(esil[:, f % 2, :], psum[:, f % 2, 0:CAP], ACT.Silu).then_inc(sem("gate_taken"), 1)
                    act.wait_ge(side_full[0], n * 6 + 5)
                    af(selT[0:CAP, 1 - h, :], psum[0:CAP, 6, 0:T], ACT.Copy).then_inc(side_taken[0], 1)
                    act.wait_ge(side_full[1], n * 5 + 5)
                    af(hg[:, 1 - h, 0:4, :], psum[:, 7, 0:4 * CAP].rearrange("p (t s) -> p t s", t=4), ACT.Copy).then_inc(side_taken[1], 1)
                    act.wait_ge(side_full[0], n * 6 + 6)
                    af(hg[:, 1 - h, 4:8, :], psum[:, 6, 0:4 * CAP].rearrange("p (t s) -> p t s", t=4), ACT.Copy).then_inc(side_taken[0], 1)
                    for j in range(2):
                        act.wait_ge(ed, n * 4 + (2 * j + 2))
                        af(ys[0:CAP, j * 512:(j + 1) * 512], psum[0:CAP, 4 + j, :], ACT.Copy).then_inc(sem("ys_ready"), 1)
            act.wait_ge(sem("final_ss"), 1)
            af(rstd[:], psum[:, 0, 0:T], ACT.Sqrt, scale=1.0 / DM, bias=eps[:, 0:1]).then_inc(sem("final_root"), 1)

        @block.vector
        def _(dve):
            v = nc.vector
            chain = [0]

            def step(ins):
                chain[0] += 1
                ins.then_inc(sem("dve_chain"), 1)
                dve.wait_ge(sem("dve_chain"), chain[0])

            def free(key, ins, wait=False):
                ins.then_inc(bank_free[G[key] % BANKS], 1)
                if wait:
                    taken(dve, key)

            def norm(n, name, t0, x, h, sq, width=T, root=None):
                v.tensor_tensor(sq, x, x, ALU.mult).then_inc(sem("sq_ready"), 1)
                if root is None:
                    taken(dve, ("ss", n))
                else:
                    dve.wait_ge(root, 1)
                step(v.reciprocal(rstd[:, 0:width], rstd[:, 0:width]))
                for t in range(KT):
                    ins = v.scalar_tensor_tensor(out=h[:, t, :], in0=x[:, t, :], scalar=gain(name, t0 + t), in1=rstd[:, 0:width],
                                                 op0=ALU.mult, op1=ALU.mult)
                ins.then_inc(sem("h_ready"), 1)

            def x_norm(n, name, t0):
                norm(n, name, t0, xT[:, :, :], hT, hT[:, :, :])

            def add_x(name):
                for t in range(KT):
                    full(dve, (name, t))
                    free((name, t), v.tensor_tensor(xT[:, t, :], xT[:, t, :], bank((name, t))[:, 0:T], ALU.add), wait=(t == KT - 1))

            for t in range(KT):
                full(dve, ("xT", t))
                free(("xT", t), v.tensor_copy(xT[:, t, :], bank(("xT", t))[:, 0:T]), wait=(t == KT - 1))
            full(dve, ("params",))
            free(("params",), v.tensor_copy(par[:], bank(("params",))[:, 0:NPAR]), wait=True)
            full(dve, ("cst",))
            free(("cst",), v.tensor_copy(cst_keep, bank(("cst",))[:, 0:24 * XT]))
            x_norm(0, "mix", 0)
            step(v.memset(xr[:, :, 0:SCONV - 1], 0.0))
            v.tensor_copy(xrs[:, :, :, 0:SCONV - 1], cst_keep.rearrange("p (t b s) -> p t b s", t=XT, s=SCONV - 1))
            for t in range(XT):
                full(dve, ("xbc", t))
                v.tensor_copy(xrs[:, t, :, SCONV - 1], bank(("xbc", t))[:, NP:T])
                free(("xbc", t), v.tensor_copy(xr[:, t, SCONV - 1:], bank(("xbc", t))[:, 0:NP]), wait=True)
            full(dve, ("dt", 0))
            dve.wait_ge(sem("small_in"), 48)
            u, na, ex, wv, ln = (dtmp[0:SH, i, :] for i in range(5))
            free(("dt", 0), v.tensor_scalar(u, bank(("dt", 0))[0:SH, 0:T], dt_bias_t, None, ALU.add), wait=True)
            v.scalar_tensor_tensor(out=na, in0=u, scalar=-1.0, in1=u, op0=ALU.mult, op1=ALU.min).then_inc(sem("u_ready"), 1)
            for t in range(XT):
                dve.wait_ge(sem("tap0"), t + 1)
                for k in range(1, SCONV):
                    step(v.scalar_tensor_tensor(out=xc[:, t, 0:NP], in0=xr[:, t, k:k + NP], scalar=gain("scw", k * XT + t),
                                                in1=xc[:, t, 0:NP], op0=ALU.mult, op1=ALU.add))
            sx = xc[:, :, NP:T]
            wk_ = lambda k: par[:, COL["scw"] + k * XT:COL["scw"] + (k + 1) * XT].unsqueeze(2).to_broadcast([P, XT, NB])
            bias_ = par[:, COL["scb"]:COL["scb"] + XT].unsqueeze(2).to_broadcast([P, XT, NB])
            tmp = cst_keep[:, 0:XT * NB].rearrange("p (t b) -> p t b", t=XT)
            step(v.tensor_tensor(sx, xrs[:, :, :, 0], wk_(0), ALU.mult))
            step(v.tensor_tensor(sx, sx, bias_, ALU.add))
            for k in range(1, SCONV):
                step(v.tensor_tensor(tmp, xrs[:, :, :, k], wk_(k), ALU.mult))
                if k < SCONV - 1:
                    step(v.tensor_tensor(sx, sx, tmp, ALU.add))
            v.tensor_tensor(sx, sx, tmp, ALU.add).then_inc(sem("conv0"), 1)
            for name, at in (("q", 0), ("k", 4)):
                for t in range(4):
                    full(dve, (name, t))
                    free((name, t), v.tensor_copy(qk[:, at + t, :], bank((name, t))[:, 0:T]))
            dve.wait_ge(sem("e_ready"), 1)
            v.tensor_scalar(wv, ex, 1.0, None, ALU.add).then_inc(sem("w_ready"), 1)
            dve.wait_ge(sem("w_ready"), 1)
            step(v.tensor_scalar(na, wv, -1.0, None, ALU.add))
            dve.wait_ge(sem("ln_ready"), 1)
            step(v.tensor_scalar(wv, na, 0.0, None, ALU.is_equal))
            step(v.tensor_tensor(na, na, wv, ALU.add))
            step(v.reciprocal(na, na))
            step(v.tensor_tensor(ln, ln, na, ALU.mult))
            step(v.tensor_tensor(ln, ln, wv, ALU.add))
            step(v.tensor_tensor(ln, ln, ex, ALU.mult))
            step(v.scalar_tensor_tensor(out=dtT[0:SH, :], in0=u, scalar=0.0, in1=ln, op0=ALU.max, op1=ALU.add))
            step(v.tensor_scalar(na, dtT[0:SH, :], ea_t, -1.0, ALU.mult, ALU.mult))
            for c in range(NC):
                v.tensor_tensor_scan(acT[0:SH, c * P:(c + 1) * P], const("ones")[0:SH, :], na[:, c * P:(c + 1) * P], 0.0,
                                     ALU.mult, ALU.add)
            v.tensor_copy(acT[0:SH, NP:T], na[:, NP:T]).then_inc(sem("dt_ready"), 1)
            for t in range(RH):
                full(dve, ("v", t))
                free(("v", t), v.tensor_copy(vT[:, t, :], bank(("v", t))[:, 0:T]))
            full(dve, ("dtT",))
            v.tensor_copy(tk[:, :, :, :].rearrange("p a c h -> p (a c h)"), bank(("dtT",))[:, 0:4 * SH])
            free(("dtT",), v.tensor_copy(dtst[0:NB, :], bank(("dtT",))[0:NB, 4 * SH:5 * SH]), wait=True)
            full(dve, ("dbc",))
            db = bank(("dbc",))
            v.tensor_copy(Dcol[0:64, :], db[0:64, 0:SH:2])
            free(("dbc",), v.tensor_copy(Dcol[64:P, :], db[64:P, 1:SH:2]), wait=True)
            full(dve, ("Btok",))
            free(("Btok",), v.tensor_copy(Btok[:, :, :].rearrange("p c n -> p (c n)"), bank(("Btok",))))

            def heads(ap, n=8):
                return ap.rearrange("p (h v) -> p h v", h=n)

            def per_head(ap, width):
                return ap.unsqueeze(2).to_broadcast([ap.shape[0], ap.shape[1], width])

            dve.wait_ge(sem("tail0_out"), 32)
            for c in range(NC):
                for j in range(2):
                    key = ("xtok", c, j)
                    full(dve, key)
                    free(key, v.tensor_tensor(heads(xdt[:, c, j * 512:(j + 1) * 512]), heads(bank(key)),
                                              per_head(tk[:, 0, c, 8 * j:8 * j + 8], SD), ALU.mult), wait=True)
            full(dve, ("CB",))
            dve.wait_ge(sem("econst_in"), 16)
            free(("CB",), v.tensor_tensor(SM[:, :, :], bank(("CB",)).rearrange("p (a i) -> p a i", i=P),
                                          const("causal").unsqueeze(1).to_broadcast([P, SG * NC, P]), ALU.mult), wait=True)
            for j in range(2):
                key = ("xstok", j)
                full(dve, key)
                free(key, v.tensor_tensor(heads(xstok[0:NB, j * 512:(j + 1) * 512]), heads(bank(key)[0:NB, :]),
                                          per_head(dtst[0:NB, 8 * j:8 * j + 8], SD), ALU.mult))
            dve.wait_ge(sem("ea_ready"), 1)
            idn = const("ident")[0:SH, 0:SH].unsqueeze(1).to_broadcast([SH, NB, SH])
            v.tensor_tensor(eaD[0:SH, :, :], idn, ea[0:SH, :].unsqueeze(2).to_broadcast([SH, NB, SH]), ALU.mult)\
                .then_inc(sem("ead_ready"), 1)
            full(dve, ("eab",))
            free(("eab",), v.tensor_copy(eab[:, :, :].rearrange("p b h -> p (b h)"), bank(("eab",))[:, 0:NB * SH]))
            dve.wait_ge(sem("eac_ready"), 1)

            def decay_logs(s):
                c, g = s // SG, s % SG
                for j in range(2):
                    key = ("bc", c, g, j)
                    full(dve, key)
                    h0 = 8 * g + 4 * j
                    for q in range(4):
                        ins = v.tensor_scalar(S[:, 2 * (s % 2) + j, q * P:(q + 1) * P], bank(key)[:, q * P:(q + 1) * P],
                                              tk[:, 1, c, h0 + q:h0 + q + 1], 0.0, ALU.subtract, ALU.min)
                    ins.then_inc(sem("diff_ready"), 1)
                    free(key, v.tensor_copy(tot[:, c, h0:h0 + 4], bank(key)[:, P - 1:512:P]), wait=(j == 1))
                hs = slice(8 * g, 8 * g + 8)
                v.tensor_tensor(wend[:, c, hs], tot[:, c, hs], tk[:, 1, c, hs], ALU.subtract).then_inc(sem("wdiff_ready"), 1)

            def sample_y(b):
                key = ("ys", b)
                full(dve, key)
                step(v.tensor_tensor(ysum, xc[:, 0:KT, NP + b], Dcol[:, :], ALU.mult))
                free(key, v.tensor_tensor(xc[:, 0:KT, NP + b], ysum, bank(key)[:, 0:KT], ALU.add), wait=True)

            def sample_state(b):
                dve.wait_ge(sem("h_decayed"), b + 1)
                for g in range(SG):
                    key = ("xb", b, g)
                    full(dve, key)
                    hv = hb[:, b % 3, g * 512:(g + 1) * 512]
                    free(key, v.scalar_tensor_tensor(out=hv, in0=bank(key), scalar=xc[:, 8 + g, NP + b:NP + b + 1], in1=hv,
                                                     op0=ALU.mult, op1=ALU.add))
                if b:
                    sample_y(b - 1)

            decay_logs(0)
            for s in range(NC * SG):
                c, g = s // SG, s % SG
                hs = slice(8 * g, 8 * g + 8)
                if s < NC * SG - 1:
                    decay_logs(s + 1)
                for j in range(2):
                    dve.wait_ge(sem("decay_ready"), 2 * s + j + 1)
                    sv = S[:, 2 * (s % 2) + j, :].rearrange("p (q i) -> p q i", q=4)
                    v.tensor_tensor(sv, sv, SM[:, 2 * g + c, :].unsqueeze(1).to_broadcast([P, 4, P]), ALU.mult)\
                        .then_inc(sem("s_ready"), 1)
                dve.wait_ge(sem("wend_ready"), s + 1)
                v.tensor_tensor(heads(xdtw[:, g * 512:(g + 1) * 512]), heads(xdt[:, c, g * 512:(g + 1) * 512]),
                                per_head(wend[:, c, hs], SD), ALU.mult).then_inc(sem("xdtw_ready"), 1)
                sample_state(2 * s)
                key, yv = ("y", c, g), ytok[:, c, g * 512:(g + 1) * 512]
                full(dve, key)
                if c == 0:
                    free(key, v.tensor_copy(yv, bank(key)))
                    full(dve, ("kv", 0, g))
                    free(("kv", 0, g), v.tensor_copy(hst[:, g, :], bank(("kv", 0, g))))
                else:
                    full(dve, ("yi", g))
                    free(("yi", g), v.tensor_tensor(heads(yv), heads(bank(("yi", g))), per_head(eac[:, hs], SD), ALU.mult), wait=True)
                    free(key, v.tensor_tensor(yv, yv, bank(key), ALU.add))
                    if g == 0:
                        dve.wait_ge(sem("etot_ready"), 1)
                    hv = heads(hst[:, g, :])
                    step(v.tensor_tensor(hv, hv, per_head(etot[:, 8 * g:8 * g + 8], SD), ALU.mult))
                    full(dve, ("kv", 1, g))
                    free(("kv", 1, g), v.tensor_tensor(hst[:, g, :], hst[:, g, :], bank(("kv", 1, g)), ALU.add))
                sample_state(2 * s + 1)
            sample_y(NB - 1)
            for t in range(KT):
                key = ("yT", t)
                full(dve, key)
                free(key, v.scalar_tensor_tensor(out=xc[:, t, 0:NP], in0=xc[:, t, 0:NP], scalar=Dcol[:, t:t + 1],
                                                 in1=bank(key)[:, 0:NP], op0=ALU.mult, op1=ALU.add), wait=(t == KT - 1))
            zy = zg[:, 0:KT, :]
            dve.wait_ge(sem("z_ready"), 1)
            step(v.tensor_tensor(zy, zy, xc[:, 0:KT, :], ALU.mult))
            v.tensor_tensor(sqb[:, :, :], zy, zy, ALU.mult).then_inc(sem("ysq_ready"), 1)
            for g in range(SG):
                taken(dve, ("yss", g))
                step(v.reciprocal(rs2[:, g, :], rs2[:, g, :]))
                for t in range(4 * g, 4 * g + 4):
                    ins = v.scalar_tensor_tensor(out=zg[:, t, :], in0=zg[:, t, :], scalar=gain("gnorm", t), in1=rs2[:, g, :],
                                                 op0=ALU.mult, op1=ALU.mult)
            step(ins)
            for i in range(8):
                kind = "q" if i < 4 else "k"
                full(dve, ("rot", i))
                v.tensor_tensor(rs2[:, 0, :], qk[:, i, :], const("cos" + kind), ALU.mult)
                free(("rot", i), v.tensor_tensor(rs2[:, 1, :], bank(("rot", i))[:, 0:T], const("sin" + kind), ALU.mult), wait=True)
                v.tensor_tensor(qk[:, i, :], rs2[:, 0, :], rs2[:, 1, :], ALU.add).then_inc(sem("rot_done"), 1)
                dve.wait_ge(sem("rot_done"), i + 1)
            for j in range(2):
                full(dve, ("vstok", j))
                free(("vstok", j), v.tensor_copy(vstok[0:NB, j * 512:(j + 1) * 512], bank(("vstok", j))[0:NB, :]))
            for c in range(NC):
                key = ("ktok", c)
                full(dve, key)
                free(key, v.tensor_tensor(heads(ktok[:, c, :]), heads(bank(key)), per_head(const("wk"), RK), ALU.mult))
            for c in range(NC):
                for j in range(2):
                    key = ("vtok", c, j)
                    full(dve, key)
                    free(key, v.tensor_copy(vtok[:, c, j * 512:(j + 1) * 512], bank(key)))

            def sample_o(b):
                for p in range(2):
                    full(dve, ("os", b, p))
                    free(("os", b, p), v.tensor_copy(oTt[:, p:RH:2, NP + b], bank(("os", b, p))[:, 0:4]), wait=(b == NB - 1))

            def sample_v(b):
                key = ("vb", b)
                full(dve, key)
                dve.wait_ge(sem("r_decayed"), b + 1)
                for hh in range(4):
                    hv = rb[:, b % 4, hh * RV:(hh + 1) * RV]
                    ins = v.scalar_tensor_tensor(out=hv, in0=bank(key)[:, hh * RV:(hh + 1) * RV], scalar=qk[:, 4 + hh, NP + b:NP + b + 1],
                                                 in1=hv, op0=ALU.mult, op1=ALU.add)
                free(key, ins)
                if b:
                    sample_o(b - 1)

            dve.wait_ge(sem("ssm_p_out"), 16)
            for c in range(NC):
                for p in range(2):
                    key = ("rs", c, p)
                    full(dve, key)
                    free(key, v.tensor_tensor(S[:, 2 * c + p, :], bank(key), const("dret")[:, p * 512:(p + 1) * 512], ALU.mult))
                sample_v(2 * c)
                for p in range(2):
                    key, ov = ("ro", c, p), otok[:, c, p * 512:(p + 1) * 512]
                    if c == 0:
                        full(dve, key)
                        ins = v.tensor_copy(ov, bank(key))
                    else:
                        full(dve, ("ri", p))
                        free(("ri", p), v.tensor_tensor(heads(ov, 4), heads(bank(("ri", p)), 4),
                                                        per_head(const("gq")[:, 4 * p:4 * p + 4], RV), ALU.mult), wait=True)
                        ins = v.tensor_tensor(ov, ov, bank(key), ALU.add)
                    free(key, ins, wait=(p == 1))
                dve.sem_inc(sem("o_rows"), 1)
                key = ("rkv", c)
                full(dve, key)
                rv = rst[:, 0, :]
                if c == 0:
                    free(key, v.tensor_copy(rv, bank(key)), wait=True)
                else:
                    for hh in range(4):
                        hv = rv[:, hh * RV:(hh + 1) * RV]
                        ins = v.scalar_tensor_tensor(out=hv, in0=hv, scalar=const("gchunk")[:, hh:hh + 1],
                                                     in1=bank(key)[:, hh * RV:(hh + 1) * RV], op0=ALU.mult, op1=ALU.add)
                    free(key, ins)
                sample_v(2 * c + 1)
            for b in range(4, NB):
                sample_v(b)
                if b < 4 + NC:
                    c = b - 4
                    dve.wait_ge(sem("o_root"), c + 1)
                    step(v.reciprocal(oms[:, c, :], oms[:, c, :]))
                    v.tensor_tensor(heads(otok[:, c, :]), heads(otok[:, c, :]), per_head(oms[:, c, :], RV), ALU.mult)\
                        .then_inc(sem("o_scaled"), 1)
            sample_o(NB - 1)
            os_ = oTt[:, :, NP:T]
            v.tensor_tensor(ogs, os_, os_, ALU.mult).then_inc(sem("osq_ready"), 1)
            dve.wait_ge(sem("g_ready"), 1)
            zs = zg[:, RH:2 * RH, NP:T]
            step(v.tensor_tensor(zs, zs, os_, ALU.mult))
            for h in range(RH):
                full(dve, ("oT", h))
                zo = zg[:, RH + h, 0:NP]
                free(("oT", h), v.tensor_tensor(zo, zo, bank(("oT", h))[:, 0:NP], ALU.mult))
            taken(dve, ("oss",))
            step(v.reciprocal(ogs, ogs))
            v.tensor_tensor(zs, zs, ogs, ALU.mult).then_inc(sem("mixed_ready"), 1)

            def memory_rows(l):
                for j in range(4):
                    key = ("mT", l, j)
                    full(dve, key)
                    free(key, v.tensor_copy(mT[:, 2 * j:2 * j + 2, :].rearrange("p t m -> p (t m)"), bank(key)), wait=(j == 3))
                norm(MEM_NORM[l], "mem", KT * l, mT[:, :, :], mT, memsq[:, :, :], width=ML)

            memory_rows(0)
            add_x("wout0")

            def cross(l):
                x_norm(CROSS_NORM[l], "cross", KT * l)
                if l:
                    dve.wait_ge(sem("odd_out"), 64)
                for t in range(KT):
                    full(dve, (f"xq{l}", t))
                    free((f"xq{l}", t), v.tensor_copy(qT[:, t, :], bank((f"xq{l}", t))[:, 0:T]))
                for j in range(2):
                    full(dve, ("qs", l, j))
                    free(("qs", l, j), v.tensor_copy(qstok[0:NB, j * 512:(j + 1) * 512], bank(("qs", l, j))[0:NB, :]))
                for lt in range(2):
                    for hp in range(2):
                        key = ("S", l, lt, hp)
                        full(dve, key)
                        c = 4 * lt + 2 * hp
                        step(v.tensor_reduce(nmx[:, c:c + 2], bank(key).rearrange("p (q m) -> p q m", q=2), AX, ALU.max))
                        v.tensor_scalar(nmx[:, c:c + 2], nmx[:, c:c + 2], -1.0 / 16, None, ALU.mult).then_inc(sem("mx_ready"), 1)
                for lt in range(2):
                    for hp in range(2):
                        key = ("S", l, lt, hp)
                        taken(dve, key)
                        c = 4 * lt + 2 * hp
                        step(v.reciprocal(rsum[:, c:c + 2], rsum[:, c:c + 2]))
                        for q in range(2):
                            ins = v.tensor_scalar(Pr[:, 2 * lt + hp, q, :], Pr[:, 2 * lt + hp, q, :], rsum[:, c + q:c + q + 1], None, ALU.mult)
                        ins.then_inc(sem("p_ready"), 1)
                for lt in range(2):
                    for hp in range(2):
                        key = ("PT", l, lt, hp)
                        full(dve, key)
                        for q in range(2):
                            ins = v.tensor_copy(PTt[:, 2 * hp + q, :, lt * P:(lt + 1) * P],
                                                bank(key)[:, q * 256:(q + 1) * 256].rearrange("p (m i) -> p m i", m=2))
                        free(key, ins)
                for b in range(NB):
                    rows = kv_in(dve, l, b)
                    for j in range(2):
                        key = ("qb", l, b, j)
                        full(dve, key)
                        for m in range(2):
                            for q in range(2):
                                h = 2 * j + q
                                kh = rows[:, m, h * 256:(h + 1) * 256]
                                ins = v.tensor_tensor_reduce(kh, kh, bank(key)[:, q * 256:(q + 1) * 256], 1.0, 0.0, ALU.mult, ALU.add,
                                                             sS[:, m, b * XH + h:b * XH + h + 1])
                        free(key, ins)
                key = ("sT", l)
                full(dve, key)
                step(v.tensor_reduce(nms, bank(key)[0:32, 0:ML], AX, ALU.max))
                v.tensor_scalar(nms, nms, -1.0 / 16, None, ALU.mult).then_inc(sem("smx_ready"), 1)
                taken(dve, key)
                step(v.reciprocal(rss, rss))
                v.tensor_scalar(Ps[0:32, :], Ps[0:32, :], rss, None, ALU.mult).then_inc(sem("ps_ready"), 1)
                full(dve, ("pT", l))
                free(("pT", l), v.tensor_copy(pTs[:, :, :].rearrange("p m i -> p (m i)"), bank(("pT", l))[:, 0:64]))
                full(dve, ("aos", l))
                free(("aos", l), v.tensor_copy(oT[:, :, NP:T], bank(("aos", l))[:, 0:64].rearrange("p (t b) -> p t b", t=KT)))
                add_x(f"xo{l}")

            cross(0)
            x_norm(3, "ffn", 0)
            dve.wait_ge(sem("kst"), 16)
            dve.wait_ge(sem("vst"), 16)
            for t in range(FT):
                full(dve, ("f3", t))
                taken(dve, ("f1", t))
                free(("f3", t), v.tensor_tensor(hid[:, t, :], sil[:, t % 2, :], bank(("f3", t))[:, 0:T], ALU.mult))
            memory_rows(1)
            add_x("f2")
            full(dve, ("ost", 0))
            v.memset(up[:, :, 0:PST], 0.0)
            v.memset(gp[:, :, 0:CK - 1], 0.0)
            for t in range(OT):
                ins = v.tensor_copy(us[:, t, :, 0:PST], bank(("ost", 0))[:, t * 120:(t + 1) * 120].rearrange("p (b s) -> p b s", s=PST))
            free(("ost", 0), ins)
            for j in (1, 2):
                key = ("ost", j)
                full(dve, key)
                for t in range(OT):
                    ins = v.tensor_copy(gs[:, t, 4 * j - 4:4 * j, 0:CK - 1],
                                        bank(key)[:, t * 120:(t + 1) * 120].rearrange("p (b s) -> p b s", s=CK - 1))
                free(key, ins)
            x_norm(ODD_NORM, "mix", KT)
            for t in range(8):
                key = ("win1", t)
                full(dve, key)
                if t < OT:
                    v.tensor_copy(us[:, t, :, PST], bank(key)[:, NP:T])
                    free(key, v.tensor_copy(up[:, t, PST:], bank(key)[:, 0:NP]), wait=True)
                else:
                    free(key, v.tensor_copy(ga[:, t - OT, :], bank(key)[:, 0:T]), wait=True)
            for t in range(OT):
                taken(dve, ("win1", 8 + t))
                v.tensor_tensor(gs[:, t, :, CK - 1], ga[:, t, NP:T], csq[:, t, NP:T], ALU.mult)
                v.tensor_tensor(gp[:, t, CK - 1:], ga[:, t, 0:NP], csq[:, t, 0:NP], ALU.mult).then_inc(sem("odd_raw"), 1)
            dve.wait_ge(sem("odd_raw"), 4)
            n_up = PST + NP
            for g, win in enumerate(WINDOWS):
                src, width, lo = up[:, g, :], 1, 0
                bufs = [w2t, w4t]
                while width < win:
                    dst = bufs[0]
                    step(v.tensor_tensor(dst[:, lo + width:n_up], src[:, lo + width:n_up], src[:, lo:n_up - width], ALU.add))
                    src, lo, width = dst, lo + width, 2 * width
                    bufs = bufs[::-1]
                u_ = up[:, g, PST:]
                step(v.scalar_tensor_tensor(out=pooled[:, g, 0:NP], in0=src[:, PST:], scalar=1.0 / win, in1=u_, op0=ALU.mult,
                                            op1=ALU.subtract))
                at = g * (PST + 1)
                step(v.tensor_tensor(prods[:, 0, 0:PST + 1], src[:, PST:2 * PST + 1], const("invcnt")[:, at:at + PST + 1], ALU.mult))
                step(v.tensor_tensor(pooled[:, g, 0:PST + 1], prods[:, 0, 0:PST + 1], u_[:, 0:PST + 1], ALU.subtract))
                step(v.tensor_reduce(prods[:, 1, 0:NB], us[:, g, :, PST + 1 - win:PST + 1], AX, ALU.add))
                v.scalar_tensor_tensor(out=pooled[:, g, NP:T], in0=prods[:, 1, 0:NB], scalar=1.0 / win, in1=us[:, g, :, PST],
                                       op0=ALU.mult, op1=ALU.subtract).then_inc(sem("pooled"), 1)
                dve.wait_ge(sem("pooled"), g + 1)
            for j, (key, dst, n) in enumerate(((("tail1",), tok1, 23), (("tail2",), tok2, 38))):
                full(dve, key)
                free(key, v.tensor_copy(dst[0:n, :], bank(key)[0:n, :]))
            for t in range(OT):
                if t == 2:
                    for g in range(OT):
                        key = ("pw", g)
                        full(dve, key)
                        free(key, v.tensor_scalar(mixo[:, g, :], bank(key)[:, 0:T], gain("pscale", g), None, ALU.mult))
                cw = par[:, COL["ccw"] + t:COL["ccw"] + 4 * CK:4]
                step(v.tensor_tensor(prods[:, :, :], gs[:, t, :, :], cw.unsqueeze(1).to_broadcast([P, NB, CK]), ALU.mult))
                step(v.tensor_reduce(mixo[:, OT + t, NP:T], prods[:, :, :], AX, ALU.add))
                step(v.tensor_scalar(mixo[:, OT + t, NP:T], mixo[:, OT + t, NP:T], gain("ccb", t), None, ALU.add))
                dve.wait_ge(sem("ctap0"), t + 1)
                for k in range(1, CK):
                    ins = v.scalar_tensor_tensor(out=mixo[:, OT + t, 0:NP], in0=gp[:, t, k:k + NP], scalar=gain("ccw", 4 * k + t),
                                                 in1=mixo[:, OT + t, 0:NP], op0=ALU.mult, op1=ALU.add)
                    if k < CK - 1:
                        step(ins)
                ins.then_inc(sem("conv_done"), 1)
                dve.wait_ge(sem("conv_done"), t + 1)
            full(dve, ("mu",))
            for t in range(OT):
                ins = v.scalar_tensor_tensor(out=mixo[:, OT + t, :], in0=bank(("mu",))[:, 0:T], scalar=-1.0 / 512, in1=mixo[:, OT + t, :],
                                             op0=ALU.mult, op1=ALU.add)
            free(("mu",), ins, wait=True)
            v.tensor_tensor(csq[:, :, :], mixo[:, OT:, :], mixo[:, OT:, :], ALU.mult).then_inc(sem("csq_ready"), 1)
            taken(dve, ("var",))
            step(v.reciprocal(rstd[:], rstd[:]))
            for t in range(OT):
                v.tensor_tensor(mixo[:, OT + t, :], mixo[:, OT + t, :], rstd[:], ALU.mult).then_inc(sem("cnorm"), 1)
            add_x("wout1")
            cross(1)

            x_norm(7, "ffn", KT)
            full(dve, ("logit",))
            step(v.memset(comb[:, 2, :], 0.0))
            step(v.memset(slot[:, 2, :], -1.0))
            for c in range(3):
                n = P if c < 2 else NB
                ins = v.tensor_copy(lg[0:n, c, :], bank(("logit",))[0:n, c * NE:(c + 1) * NE])
            free(("logit",), ins, wait=True)
            for c in range(3):
                n = P if c < 2 else NB
                step(v.max(mx[0:n, c, :], lg[0:n, c, :]))
                step(v.max_index(idx[0:n, c, :], mx[0:n, c, :], lg[0:n, c, :]))
                step(v.tensor_copy(idxf[0:n, c, :], idx[0:n, c, :]))
                v.tensor_tensor(gt[0:n, c, 0:1], mx[0:n, c, 1:2], mx[0:n, c, 0:1], ALU.subtract).then_inc(sem("gap_ready"), 1)
            for c in range(3):
                n = P if c < 2 else NB
                dve.wait_ge(sem("gap_exp"), c + 1)
                step(v.tensor_scalar(gt[0:n, c, 2:3], gt[0:n, c, 1:2], 1.0, None, ALU.add))
                step(v.reciprocal(gt[0:n, c, 2:3], gt[0:n, c, 2:3]))
                step(v.tensor_tensor(gt[0:n, c, 3:4], gt[0:n, c, 1:2], gt[0:n, c, 2:3], ALU.mult))
                iota = const("iota")[0:n, 0:NE]
                step(v.tensor_scalar(picked[0:n, c, :], iota, idxf[0:n, c, 0:1], None, ALU.is_equal))
                step(v.tensor_scalar(lg[0:n, c, :], iota, idxf[0:n, c, 1:2], None, ALU.is_equal))
                step(v.tensor_scalar(comb[0:n, c, :], picked[0:n, c, :], gt[0:n, c, 2:3], None, ALU.mult))
                step(v.scalar_tensor_tensor(out=comb[0:n, c, :], in0=lg[0:n, c, :], scalar=gt[0:n, c, 3:4], in1=comb[0:n, c, :],
                                            op0=ALU.mult, op1=ALU.add))
                step(v.tensor_tensor(picked[0:n, c, :], picked[0:n, c, :], lg[0:n, c, :], ALU.add))
            v.memset(ys[0:CAP, :], 0.0)
            v.memset(selT[0:CAP, 1, :], 0.0).then_inc(sem("picked_ready"), 1)
            full(dve, ("rank",))
            rank = bank(("rank",))
            for c in range(3):
                n = P if c < 2 else NB
                step(v.tensor_tensor(slot[0:n, c, :], rank[0:n, c * NE:(c + 1) * NE], picked[0:n, c, :], ALU.mult))
                step(v.tensor_scalar(slot[0:n, c, :], slot[0:n, c, :], -1.0, None, ALU.add))
            step(v.tensor_reduce(cnts[:, 0:1], rank[:, 3 * NE:4 * NE], AX, ALU.max))
            free(("rank",), v.tensor_scalar(cnts[:, 1:2], cnts[:, 0:1], float(CAP), float(NE // 2), ALU.is_gt, ALU.mult), wait=True)
            step(v.tensor_scalar(cnts[:, 2:3], cnts[:, 0:1], float(2 * CAP), float(NE // 2), ALU.is_gt, ALU.mult))
            step(v.scalar_tensor_tensor(out=cnts[:, 3:4], in0=cnts[:, 1:2], scalar=float(NE // 2), in1=cnts[:, 2:3],
                                        op0=ALU.add, op1=ALU.add))
            step(v.tensor_scalar(cnts[:, 2:3], cnts[:, 3:4], 2.0, -1.0, ALU.mult, ALU.add))
            v.tensor_copy(rounds[:, 0:1], cnts[:, 3:4])
            v.tensor_copy(rounds[:, 1:2], cnts[:, 2:3]).then_inc(sem("rounds_known"), 1)
            iota3 = const("iota").unsqueeze(1).to_broadcast([P, 3, CAP])

            def choose(e, link):
                at = slot[:, :, bass.ds(e, 1)] if not isinstance(e, int) else slot[:, :, e:e + 1]
                gate = comb[:, :, bass.ds(e, 1)] if not isinstance(e, int) else comb[:, :, e:e + 1]
                link(v.tensor_tensor(sel[:, :, :], iota3, at.to_broadcast([P, 3, CAP]), ALU.is_equal))
                link(v.tensor_scalar(at, at, -float(CAP), None, ALU.add))
                v.tensor_tensor(selg[:, :, :], sel[:, :, :], gate.to_broadcast([P, 3, CAP]), ALU.mult).then_inc(sem("sel_ready"), 1)

            choose(0, step)
            for c in range(3):
                n = P if c < 2 else NB
                for j in range(2):
                    key = ("htok", c, j)
                    full(dve, key)
                    free(key, v.tensor_copy(htok[0:n, c, j * 512:(j + 1) * 512], bank(key)[0:n, :]))
            full(dve, ("selT0",))
            free(("selT0",), v.tensor_copy(selT[0:CAP, 0, :], bank(("selT0",))[0:CAP, 0:T]))
            for j in range(2):
                key = ("gat0", j)
                full(dve, key)
                free(key, v.tensor_copy(hg[:, 0, 4 * j:4 * j + 4, :], bank(key)[:, 0:4 * CAP].rearrange("p (t s) -> p t s", t=4)))
            side_full = [sem("side_full6"), sem("side_full7")]
            side_taken = [sem("side_taken6"), sem("side_taken7")]
            for name in ("up_taken", "ys_ready", "side_taken6", "side_taken7"):
                dve.sem_inc(sem(name), 1)
            dve.wait_ge(sem("rounds_known"), 1)
            pairs = dve.value_load(rounds[0:1, 0:1], min_val=NE // 2, max_val=3 * NE // 2)

            def scatter_add(n):
                for t in range(KT):
                    b = t % 2
                    dve.wait_ge(side_full[b], n * (6, 5)[b] + (t // 2 + 1))
                    v.tensor_tensor(xT[:, t, :], xT[:, t, :], psum[:, 6 + b, 0:T], ALU.add).then_inc(side_taken[b], 1)

            with dve.Fori(0, pairs) as pair:
                for h in range(2):
                    n = pair * 2 + h
                    links = [0]

                    def link(ins):
                        links[0] += 1
                        ins.then_inc(sem("choose_chain"), 1)
                        dve.wait_ge(sem("choose_chain"), n * 2 + links[0])

                    dve.wait_ge(side_taken[0], n * 6 + 1)
                    choose((n + 1) & (NE - 1), link)
                    for f in range(ET):
                        dve.wait_ge(eu, n * (2 * ET) + (4 * (f // 2) + 2 + f % 2 + 1))
                        dve.wait_ge(sem("gate_taken"), n * ET + (f + 2))
                        v.tensor_tensor(ehid[:, f, :], esil[:, f % 2, :], psum[:, 2 + f % 2, 0:CAP], ALU.mult).then_inc(sem("up_taken"), 1)
                    scatter_add(n)
            scatter_add(dve.snap(pairs * 2))
            dve.wait_ge(side_taken[1], pairs * 10 + 5)
            norm(8, "final", 0, xT[:, :, :], hT, hT[:, :, :], root=sem("final_root"))
            for c in range(3):
                n = P if c < 2 else NB
                dve.wait_ge(sem("final_tok"), c + 1)
                v.tensor_copy(fin[0:n, c, :], psum[0:n, 1 + 2 * c:3 + 2 * c, :].rearrange("p a b -> p (a b)")).then_inc(sem("fin_tok"), 1)


_INS = ["x_prompt", "x_sample", "state_ssm", "state_ssm_conv", "state_ret", "state_pool", "state_conv",
        "cache_mem_k", "cache_mem_v", "mem_prompt", "norm_mix", "norm_cross", "norm_ffn", "norm_mem", "norm_final",
        "w_in_even", "ssd_conv_w", "ssd_conv_b", "ssd_dt_bias", "ssd_a_log", "ssd_d", "ssd_norm", "w_out_even",
        "ffn_w1", "ffn_w3", "ffn_w2", "w_in_odd", "pool_w", "pool_scale", "conv_w", "conv_b", "conv_norm_g",
        "conv_norm_b", "w_out_odd", "router_w", "router_b", "moe_w1", "moe_w3", "moe_w2",
        "xattn_q", "xattn_k", "xattn_v", "xattn_o"]
_OUTS = [(1, NP, DM), (NB, 1, DM), (2, 1, ML, XH, 256), (2, 1, ML, XH, 256),
         (1, 1, SH, SN, SD), (1, 1, SCONV - 1, 1536), (1, 1, RH, RK, RV), (1, 1, PST, 512), (1, 1, CK - 1, 512),
         (1, NB, SH, SN, SD), (1, NB, SCONV - 1, 1536), (1, NB, RH, RK, RV), (1, NB, PST, 512), (1, NB, CK - 1, 512)]


def kernel(**inputs):
    import numpy as _np
    import concourse.bacc as _bacc
    from concourse.bass_utils import run_bass_kernel_spmd as _run

    nc = _bacc.Bacc("TRN2", target_bir_lowering=False, num_devices=1)
    arrays, w = {}, {}
    for name in _INS:
        a = _np.ascontiguousarray(inputs[name])
        arrays[f"in_{name}_dram"] = a
        w[name] = nc.dram_tensor(f"in_{name}_dram", a.shape, F32, kind="ExternalInput").ap()
    arrays["in_consts_dram"] = CONST_ARRAY
    consts = nc.dram_tensor("in_consts_dram", CONST_ARRAY.shape, F32, kind="ExternalInput").ap()
    outs = [nc.dram_tensor(f"out_{i}_dram", shape, F32, kind="ExternalOutput").ap() for i, shape in enumerate(_OUTS)]
    trunk_kernel(nc, w, consts, outs)
    r = _run(nc, [arrays], core_ids=[0])
    return tuple(r.results[0][f"out_{i}_dram"] for i in range(len(_OUTS)))
```

```python
from contextlib import ExitStack

import numpy as np

import concourse.bass as bass
from concourse import mybir

F32 = mybir.dt.float32
U32 = mybir.dt.uint32
ALU = mybir.AluOpType
ACT = mybir.ActivationFunctionType
AX = mybir.AxisListType.X

P = 128
DM = 1024
KT = DM // P
NP = 256
NB = 8
T = NP + NB
NC = NP // P
EPS = 1e-6
SH, SD, SG, SN = 16, 64, 2, 128
RH, RK, RV = 8, 64, 128
XT = 12
SCONV = 4
FF = 2816
NE, FE = 8, 1792
CAP = 96
ML, XH = 256, 4
WINDOWS = (2, 4, 8, 16)
PST = max(WINDOWS) - 1
CK = 31
OT = 4
PAST = 2048
ROPE_BASE = 10000.0

RING = 11
TRUNK_RING = 6
SLOT_K, SLOT_N = 8, 256
SLOT = SLOT_K * SLOT_N
BANKS = 6
SUMS = 6
FT, ET = FF // P, FE // P
KV_SLOTS = RING - TRUNK_RING

PA = dict(mix=0, cross=16, ffn=32, mem=48, final=64, gnorm=72, scw=80)
PB = dict(scb=128, pscale=140, ccb=144, cng=148, cnb=152)
PC = dict(ccw=156)
COL = {**PA, **PB, **PC}
NPAR = 280

CONST = {}


def _add(name, a):
    CONST[name] = np.ascontiguousarray(a, np.float32)


def _constants():
    i = np.arange(P)
    _add("ident", np.eye(P))
    _add("ones", np.ones((P, P)))
    half = RK // 2
    rot = np.zeros((P, P))
    for d in range(P):
        if d % RK < half:
            rot[d + half, d] = -1.0
        else:
            rot[d - half, d] = 1.0
    _add("rot", rot)
    inv = np.float32(ROPE_BASE) ** (-np.arange(half, dtype=np.float32) / np.float32(half))
    pos = np.concatenate([np.arange(NP), np.full(NB, PAST)]).astype(np.float32)
    ang = (pos[None, :] * inv[i % half][:, None]).astype(np.float32)
    for n, s in (("q", 1.0), ("k", RK ** -0.5)):
        _add("cos" + n, np.cos(ang.astype(np.float64)) * s)
        _add("sin" + n, np.sin(ang.astype(np.float64)) * s)
    _add("causal", (i[None, :] >= i[:, None]) * 1.0)
    lg = np.log1p(-np.exp2(-5.0 - np.arange(RH)))
    d = i[None, :] - i[:, None]
    dec = np.where(d >= 0, np.exp(np.minimum(lg[:, None, None] * d, 0.0)), 0.0)
    order = [2 * hh + par for par in range(2) for hh in range(RH // 2)]
    _add("dret", dec[order].transpose(1, 0, 2).reshape(P, RH * P))
    _add("gq", np.exp(lg[order][None, :] * (i[:, None] + 1)))
    _add("wk", np.exp(lg[None, :] * (P - 1 - i[:, None])))
    par = i // RK
    hh = np.arange(RH // 2)
    _add("gchunk", np.exp(lg[2 * hh[None, :] + par[:, None]] * P))
    _add("gone", np.exp(lg[2 * hh[None, :] + par[:, None]]))
    _add("iota", np.tile(np.arange(CAP), (P, 1)))
    cnt = np.stack([1.0 / np.minimum(np.arange(PST + 1) + 1.0, w) for w in WINDOWS])
    _add("invcnt", np.tile(cnt.reshape(1, -1), (P, 1)))


_constants()
EVEN_CONST = ("rot", "cosq", "sinq", "cosk", "sink", "dret", "gq", "wk", "gchunk", "gone")
BASE_CONST = ("ident", "ones", "causal", "iota", "invcnt")
CONST_AT = {}
_off = 0
for _n in BASE_CONST + EVEN_CONST:
    CONST_AT[_n] = (_off, CONST[_n].shape[1])
    _off += CONST[_n].shape[1]
N_CONST = _off
N_BASE = sum(CONST[_n].shape[1] for _n in BASE_CONST)
CONST_ARRAY = np.concatenate([CONST[_n] for _n in BASE_CONST + EVEN_CONST], axis=1)


def weight_items(w):
    items = []

    def block(name, wm, n0, n, block_no, chunks):
        for kc, (k0, kn) in enumerate(chunks):
            items.append((name, block_no, kc, wm[k0 * P:(k0 + kn) * P, n0:n0 + n].rearrange("(t p) n -> p t n", p=P)))

    def whole(name, wm, n, chunks):
        for b in range(n // SLOT_N):
            block(name, wm, b * SLOT_N, SLOT_N, b, chunks)

    full = [(0, 8)]
    win = w["w_in_even"][0]
    cols = dict(z=0, xbc=1024, dt=2560, q=2576, k=3088, v=3600, g=4624)
    for name, nb in (("xbc", 6), ("dt", 1), ("q", 2), ("k", 2), ("v", 4), ("z", 4), ("g", 4)):
        for b in range(nb):
            n = SH if name == "dt" else SLOT_N
            block(name, win, cols[name] + b * SLOT_N, n, b, full)
    whole("wout0", w["w_out_even"][0], DM, [(0, 8), (8, 8)])

    whole("xk0", w["xattn_k"][0], DM, full)
    whole("xq0", w["xattn_q"][0], DM, full)
    whole("xv0", w["xattn_v"][0], DM, full)
    whole("xo0", w["xattn_o"][0], DM, full)
    for b in range(FF // SLOT_N):
        block("f1", w["ffn_w1"][0], b * SLOT_N, SLOT_N, b, full)
        block("f3", w["ffn_w3"][0], b * SLOT_N, SLOT_N, b, full)
    whole("f2", w["ffn_w2"][0], DM, [(0, 8), (8, 8), (16, 6)])
    whole("win1", w["w_in_odd"][0], 1536, full)
    whole("xk1", w["xattn_k"][1], DM, full)
    whole("xv1", w["xattn_v"][1], DM, full)
    whole("wout1", w["w_out_odd"][0], DM, full)
    whole("xq1", w["xattn_q"][1], DM, full)
    whole("xo1", w["xattn_o"][1], DM, full)
    return items


MEM_NORM, CROSS_NORM, FFN_NORM, ODD_NORM = (1, 4), (2, 6), (3, 7), 5


def memory_rows(l):
    return [("mT", l, j) for j in range(4)]


def psum_groups():
    g = [("xT", t) for t in range(KT)]

    def lin(name, n):
        return [(name, t) for t in range(n)]

    def lin_x(name, n):
        mem = {"wout0": [("ss", MEM_NORM[0])], "f2": [("ss", MEM_NORM[1])]}.get(name, [])
        return [(name, 0), (name, 1)] + mem + lin(name, KT)[2:] + [("ss", n)]

    g += [("ss", 0), ("params",), ("cst",)] + lin("xbc", 12) + [("dt", 0)] + lin("q", 4) + lin("k", 4)
    g += [("tail0", j) for j in range(3)] + lin("v", 8)
    g += [("dtT",), ("dbc",), ("Btok",)] + [("xtok", c, j) for c in range(NC) for j in range(2)] + [("CB",)]
    g += [("xstok", 0), ("xstok", 1), ("eab",), ("bc", 0, 0, 0), ("bc", 0, 0, 1)]
    for s in range(NC * SG):
        if s < 3:
            g += [("bc", (s + 1) // SG, (s + 1) % SG, j) for j in range(2)]
        g += [("xb", 2 * s, 0), ("xb", 2 * s, 1)]
        g += [("y", s // SG, s % SG)] + ([("yi", s % SG)] if s >= SG else []) + [("kv", s // SG, s % SG)]
        g += [("z", 2 * s), ("z", 2 * s + 1)]
        g += [("xb", 2 * s + 1, 0), ("xb", 2 * s + 1, 1)]
    g += [("yT", t) for t in range(KT)] + [("ysT",)]
    g += [("g", 0), ("g", 1), ("yss", 0), ("yss", 1)]
    g += [("rot", i) for i in range(8)]
    g += [("vstok", 0), ("vstok", 1), ("g", 2), ("g", 3)]
    g += [("ktok", c) for c in range(NC)] + [("vtok", c, j) for c in range(NC) for j in range(2)]
    for c in range(NC):
        g += [("rs", c, p) for p in range(2)]
        g += [("vb", 2 * c)]
        g += [("g", 4 + 2 * c), ("g", 5 + 2 * c)]
        g += [("ro", c, p) for p in range(2)]
        if c:
            g += [("ri", p) for p in range(2)]
        g += [("rkv", c)]
        g += [("vb", 2 * c + 1)]
    g += [("vb", b) for b in range(2 * NC, NB)]
    g += [("oT", h) for h in range(RH)] + [("osT",), ("oss",)]
    g += memory_rows(0)
    g += lin_x("wout0", CROSS_NORM[0])

    def mem_k(l):
        return [(f"xk{l}", b, m) for b in range(4) for m in range(2)] + [("KT", l, j) for j in range(4)]

    def mem_v(l):
        return [(f"xv{l}", b, m) for b in range(4) for m in range(2)]

    def cross(l):
        r = lin(f"xq{l}", KT)
        r += [("qs", l, 0), ("qs", l, 1)]
        r += [("S", l, lt, hp) for lt in range(2) for hp in range(2)]
        for b in range(NB):
            r += [("qb", l, b, j) for j in range(2)]
            if l == 0:
                r += [("xv0", b // 2, b % 2)]
        r += [("PT", l, lt, hp) for lt in range(2) for hp in range(2)]
        r += [("sT", l)] + [("ao", l, t) for t in range(KT)]
        r += [("pT", l), ("aoT", l)] + lin_x(f"xo{l}", FFN_NORM[l])
        return r

    g += mem_k(0) + cross(0)
    for b in range(FF // SLOT_N):
        g += [("f1", 2 * b), ("f1", 2 * b + 1), ("f3", 2 * b), ("f3", 2 * b + 1)]
    g += memory_rows(1)
    g += [("ost", j) for j in range(3)]
    g += lin_x("f2", ODD_NORM)
    g += lin("win1", 12) + [("tail1",), ("tail2",)]
    g += mem_k(1) + [("pw", i) for i in range(4)] + mem_v(1) + [("mu",), ("var",)]
    g += lin_x("wout1", CROSS_NORM[1])
    g += cross(1)
    g += [("logit",), ("rank",)] + [("htok", c, j) for c in range(3) for j in range(2)]
    g += [("selT0",), ("gat0", 0), ("gat0", 1)]
    return g


def trunk_kernel(nc, w, consts, outs):
    (y_p, y_s, mk_p, mv_p, ssm_p, ssmc_p, ret_p, pool_p, conv_p, ssm_s, ssmc_s, ret_s, pool_s, conv_s) = outs
    items = weight_items(w)
    item_at = {(n, b, kc): i for i, (n, b, kc, _) in enumerate(items)}
    groups = psum_groups()
    G = {k: i for i, k in enumerate(groups)}
    assert len(G) == len(groups)

    ctx = ExitStack()
    with ctx:
        sems = {}

        def sem(name):
            if name not in sems:
                sems[name] = ctx.enter_context(nc.semaphore(name))
            return sems[name]

        def sb(name, shape, dt=F32):
            return ctx.enter_context(nc.sbuf_tensor(name, shape, dt))

        ring = sb("ring", [P, RING, SLOT])
        xT = sb("xT", [P, KT, T])
        hT = sb("hT", [P, KT, T])
        par = sb("par", [P, NPAR])
        cbase = sb("cbase", [P, N_BASE])
        rstd = sb("rstd", [P, T])
        eps = sb("eps", [P, 1])
        small = sb("small", [P, 160])
        arena_n = 25160
        arena = sb("arena", [P, arena_n])
        psum = ctx.enter_context(nc.psum_tensor("psum", [P, SUMS + 2, 512], F32))
        bank_full = [sem(f"bank_full{b}") for b in range(BANKS)]
        bank_free = [sem(f"bank_free{b}") for b in range(BANKS)]
        slot_full = [sem(f"slot_full{s}") for s in range(RING)]
        chunk_used = sem("chunk_used")
        eu, ed, eh = sem("expert_up"), sem("expert_down"), sem("expert_half")
        base_full = [16 * sum(i % TRUNK_RING == s for i in range(len(items))) if s < TRUNK_RING else 0 for s in range(RING)]

        class Region:

            def __init__(self, at=0):
                self.at = at

            def take(self, *shape):
                n = int(np.prod(shape))
                v = view(self.at, *shape)
                self.at += n
                assert self.at <= arena_n, self.at
                return v

        def view(at, *shape):
            n = int(np.prod(shape))
            v = arena[:, at:at + n]
            if len(shape) == 2:
                v = v.rearrange("p (a b) -> p a b", a=shape[0])
            if len(shape) == 3:
                v = v.rearrange("p (a b c) -> p a b c", a=shape[0], b=shape[1])
            return v

        def const(name):
            at, n = CONST_AT[name]
            if name in BASE_CONST:
                return cbase[:, at:at + n]
            return E_const[:, at - N_BASE:at - N_BASE + n]

        X = ring[:, TRUNK_RING:, :].rearrange("p a b -> p (a b)")
        x_taken = [0]

        def take_x(*shape):
            n, at = int(np.prod(shape)), x_taken[0]
            x_taken[0] += n
            assert x_taken[0] <= (RING - TRUNK_RING) * SLOT
            v = X[:, at:at + n]
            if len(shape) == 2:
                v = v.rearrange("p (a b) -> p a b", a=shape[0])
            return v

        R = Region()
        E_const = R.take(N_CONST - N_BASE)
        zg = R.take(16, T)
        xr_at = R.at
        xr = R.take(XT, SCONV - 1 + NP)
        xrs = R.take(XT, NB, SCONV)
        xc = R.take(XT, T)
        qk = R.take(8, T)
        vT = R.take(RH, T)
        xdt = R.take(NC, DM)
        btok_at = R.at
        Btok = R.take(NC, SG * SN)
        SM = R.take(SG * NC, P)
        xdtw_at = R.at
        xdtw = R.take(DM)
        rs2 = view(R.at, 2, T)
        R.take(DM)
        hst = R.take(SG, 512)
        dtT = R.take(T)
        acT = R.take(T)
        ytok = view(xr_at, NC, DM)
        hb = take_x(3, DM)
        rb = take_x(4, 512)
        S = take_x(4, 512)
        otok = take_x(NC, DM)
        xstok = take_x(DM)
        sqb = view(xr_at, KT, T)
        dtmp = view(xdtw_at, 5, T)
        vstok = view(btok_at, DM)
        vtok = xdt
        ktok = view(xdtw_at, NC, 512)
        tailtok = xdt[:, :, :].rearrange("p a b -> p (a b)")[0:11, 0:1536]
        oTt = xc[:, 0:RH, :]
        rst = hst
        tailT0 = R.take(XT, 11)
        tk = R.take(2, 2, SH)
        tot = R.take(NC, SH)
        wend = R.take(NC, SH)
        eac = R.take(SH)
        etot = R.take(SH)
        eab = R.take(NB, SH)
        eaD = R.take(NB, SH)
        ea = R.take(NB)
        dtst = R.take(SH)
        oms = R.take(NC, RH)
        ogs = view(xdtw_at, RH, NB)
        junk = view(xdtw_at + 1024 + 2 * T, P)
        Zc = view(xdtw_at + 1024 + 2 * T + P, SG, NB * NB)
        Zq = xstok[:, 0:RH // 2 * NB * 2 * NB].rearrange("p (h c) -> p h c", h=RH // 2)
        ysr = xstok
        osr = vstok[:, 0:512]
        cst_keep = R.take(XT * NB * (SCONV - 1))
        Dcol = R.take(KT)
        stage_x = view(xr_at, 2, DM)
        stage_s = view(xr_at + 2 * DM, DM)
        stage_c = view(btok_at, 1536)
        R = Region()
        KTt = R.take(KT, ML)
        Vt = R.take(2, DM)
        Kt = R.take(2, DM)
        R.at = max(xr_at, (FT + 2) * T)
        memtok = R.take(2, DM)
        mT = R.take(KT, ML)
        odd_at = R.at + KT * ML
        memsq = view(R.at, KT, ML)
        Pr = R.take(4, 2, ML)
        PTt = R.take(XH, 2, NP)
        qT = R.take(KT, T)
        oT = R.take(KT, T)
        qstok = R.take(DM)
        sS = R.take(2, NB * XH)
        Ps = R.take(2 * P)
        Zp = R.take(2 * XH, NB * NB)
        aor = qstok
        kv = X[:, 0:KV_SLOTS * 2 * DM].rearrange("p (s m d) -> p s m d", s=KV_SLOTS, m=2)
        R = Region()
        hid = R.take(FT, T)
        sil = R.take(2, T)
        R = Region(odd_at)
        up = R.take(OT, PST + NP)
        us = R.take(OT, NB, PST + 1)
        gp = R.take(OT, CK - 1 + NP)
        gs = R.take(OT, NB, CK)
        ga = R.take(OT, T)
        mixo = R.take(2 * OT, T)
        w2t = R.take(PST + NP)
        w4t = R.take(PST + NP)
        pooled = R.take(OT, T)
        csq = R.take(OT, T)
        tl1 = R.take(OT, 23)
        tl2 = R.take(OT, 38)
        st_pool = R.take(512)
        st_conv = R.take(2, 512)
        tok1, tok2 = st_conv[:, 0, :], st_conv[:, 1, :]
        pw = R.take(OT, P)
        prods = R.take(NB, CK)
        R = Region()
        ehid = R.take(ET, CAP)
        esil = R.take(2, CAP)
        hg = R.take(2, KT, CAP)
        htok = R.take(3, DM)
        sel = R.take(3, CAP)
        selg = R.take(3, CAP)
        selT = R.take(2, T)
        ys = R.take(DM)
        rwt = R.take(KT, NE)
        rbt = R.take(NE)
        lg = R.take(3, NE)
        mx = R.take(3, NE)
        idxf = R.take(3, NE)
        comb = R.take(3, NE)
        picked = R.take(3, NE)
        slot = R.take(3, NE)
        gt = R.take(3, 4)
        cnts = R.take(4)
        fin = R.take(3, DM)
        idx = sb("idx", [P, 3, NE], U32)
        rounds = sb("rounds", [P, 2], mybir.dt.int32)

        a_log_t, dt_bias_t, D_row, ea_t = small[0:SH, 0:1], small[0:SH, 1:2], small[0:1, 2:2 + SH], small[0:SH, 20:21]
        nmx, rsum = small[:, 24:32], small[:, 32:40]
        nms, rss = small[0:32, 40:41], small[0:32, 41:42]
        zeros = small[:, 64:64 + 2 * NB]

        def bank(key):
            return psum[:, G[key] % BANKS, :]

        def full(eng, key):
            eng.wait_ge(bank_full[G[key] % BANKS], G[key] // BANKS + 1)

        def taken(eng, key):
            eng.wait_ge(bank_free[G[key] % BANKS], G[key] // BANKS + 1)

        def gain(name, t):
            return par[:, COL[name] + t:COL[name] + t + 1]

        def slot_left(eng, i):
            name, b, kc, _ = items[i]
            if (name, b, kc + 1) in item_at:
                eng.wait_ge(chunk_used, sum((n, bb, k + 1) in item_at for n, bb, k, _ in items[:i + 1]))
            elif (name, b, 1) in G:
                full(eng, (name, b, 1))
            else:
                full(eng, (name, b if name == "dt" else 2 * b + 1))

        def kv_in(eng, l, n):
            i = 2 * NB * l + n
            eng.wait_ge(sem(f"kv_in{i % KV_SLOTS}"), 16 * (i // KV_SLOTS + 1))
            return kv[:, i % KV_SLOTS, :, :]

        def even_stored(eng):
            for j in range(3):
                eng.wait_ge(sem(f"h_out{j}"), 16 * len(range(j, NB, 3)))
            for j in range(4):
                eng.wait_ge(sem(f"r_out{j}"), 32 * len(range(j, NB, 4)))
            eng.wait_ge(sem("tail0_out"), 32)

        last_in_slot = [max(i for i in range(len(items)) if i % TRUNK_RING == s) for s in range(TRUNK_RING)]
        block = ctx.enter_context(nc.Block())

        def slot_view(i, k, n):
            return ring[:, i % RING, 0:k * n].rearrange("p (k n) -> p k n", k=k)

        @block.sync
        def _(sp):
            sp.dma_start(cbase[:], consts[:, 0:N_BASE]).then_inc(sem("consts_in"), 16)
            for dst, src in ((stage_x[:, 0, :], w["x_prompt"][0, 0:P, :]), (stage_x[:, 1, :], w["x_prompt"][0, P:NP, :]),
                             (stage_s[0:NB, :], w["x_sample"].rearrange("b s d -> (b s) d"))):
                sp.dma_start(dst, src).then_inc(sem("x_in"), 16)
            prow = zg[:, 0:3, 0:P]

            def rows(name, src, at, n):
                g = 0 if at < 128 else (1 if at < 156 else 2)
                base = (0, 128, 156)[g]
                sp.dma_start(prow[at - base:at - base + n, g, :], src).then_inc(sem("params_in"), 16)

            def flat(a):
                return a.rearrange("l (t p) -> (l t) p", p=P)

            rows("mix", flat(w["norm_mix"]), PA["mix"], 16)
            rows("cross", flat(w["norm_cross"]), PA["cross"], 16)
            rows("ffn", flat(w["norm_ffn"]), PA["ffn"], 16)
            rows("mem", flat(w["norm_mem"]), PA["mem"], 16)
            rows("final", w["norm_final"].rearrange("(t p) -> t p", p=P), PA["final"], 8)
            rows("gnorm", flat(w["ssd_norm"]), PA["gnorm"], 8)
            rows("scw", w["ssd_conv_w"][0].rearrange("k (t p) -> (k t) p", p=P), PA["scw"], 48)
            rows("scb", flat(w["ssd_conv_b"]), PB["scb"], 12)
            rows("pscale", flat(w["pool_scale"]), PB["pscale"], 4)
            rows("ccb", flat(w["conv_b"]), PB["ccb"], 4)
            rows("cng", flat(w["conv_norm_g"]), PB["cng"], 4)
            rows("cnb", flat(w["conv_norm_b"]), PB["cnb"], 4)
            rows("ccw", w["conv_w"][0].rearrange("k (t p) -> (k t) p", p=P), PC["ccw"], 124)
            for i, (name, b, kc, src) in enumerate(items):
                if i >= TRUNK_RING:
                    slot_left(sp, i - TRUNK_RING)
                k, n = src.shape[1], src.shape[2]
                sp.dma_start(slot_view(i % TRUNK_RING, k, n), src).then_inc(slot_full[i % TRUNK_RING], 16)
            ups = [w[n][0].rearrange("e (t p) n -> p e t n", p=P) for n in ("moe_w1", "moe_w3")]
            down = w["moe_w2"][0].rearrange("e (t p) n -> p e t n", p=P)

            def expert_load(e, j):
                pick = slice(e, e + 1) if isinstance(e, int) else bass.ds(e, 1)
                if j < 14:
                    src, k = ups[j % 2][:, pick, :, (j // 2) * 256:(j // 2 + 1) * 256], 8
                else:
                    q = j - 14
                    src, k = down[:, pick, 7 * (q % 2):7 * (q % 2) + 7, (q // 2) * 256:(q // 2 + 1) * 256], 7
                sp.dma_start(slot_view(j, k, 256), src.rearrange("p e t n -> p (e t) n")).then_inc(slot_full[j % RING], 16)

            def expert_left(n, j):
                if j < 14:
                    sp.wait_ge(eu, n * (2 * ET) + 2 * (j + 1))
                else:
                    sp.wait_ge(eh if j % 2 == 0 else ed, n * 4 + ((j - 14) // 2 + 1))

            sp.wait_ge(sem("aos_done"), 2)
            for j in range(TRUNK_RING, RING):
                expert_load(0, j)
            for j in range(TRUNK_RING):
                slot_left(sp, last_in_slot[j])
                expert_load(0, j)
            sp.wait_ge(sem("rounds_known"), 1)
            steps = sp.value_load(rounds[0:1, 1:2], min_val=NE - 1, max_val=3 * NE - 1)
            with sp.Fori(0, steps) as n:
                e, e_next = n & (NE - 1), (n + 1) & (NE - 1)
                sp.wait_ge(eu, e + e_next + 1)
                for j in range(RING, 2 * RING):
                    if j != 14:
                        expert_left(n, j - RING + (j == 13))
                    expert_load(e, j)
                for j in range(RING):
                    expert_left(n, j + RING)
                    expert_load(e_next, j)
            for j in range(RING, 2 * RING):
                expert_left(steps, j - RING)
                expert_load(NE - 1, j)

        @block.gpsimd
        def _(pool):
            def load(dst, src, s):
                pool.dma_start(dst, src).then_inc(sem(s), 16)

            stored = [0]

            def store(dst, src):
                pool.dma_start(dst, src).then_inc(sem("stored"), 16)
                stored[0] += 16

            nc.gpsimd.memset(eps[:], EPS).then_inc(sem("eps_set"), 1)
            nc.gpsimd.memset(zeros, 0.0).then_inc(sem("zeros_set"), 1)
            load(stage_c[0:24, :], w["state_ssm_conv"][0].rearrange("b s c -> (b s) c"), "cst_in")
            load(a_log_t, w["ssd_a_log"].rearrange("l h -> h l"), "small_in")
            load(dt_bias_t, w["ssd_dt_bias"].rearrange("l h -> h l"), "small_in")
            load(D_row, w["ssd_d"], "small_in")
            load(E_const, consts[:, N_BASE:N_CONST], "econst_in")
            hsem = [sem(f"h_in{j}") for j in range(3)]
            ssm_v = w["state_ssm"][0].rearrange("b h k v -> b k h v")
            ssm_o = ssm_s[0].rearrange("b h k v -> b k h v")
            hdone = [sem(f"h_out{j}") for j in range(3)]
            rsem = [sem(f"r_in{j}") for j in range(4)]
            rdone = [sem(f"r_out{j}") for j in range(4)]
            ret_v = w["state_ret"][0].rearrange("b (c r) k v -> b r k c v", r=2)
            ret_o = ret_s[0].rearrange("b (c r) k v -> b r k c v", r=2)

            def hload(b):
                if b >= 3:
                    pool.wait_ge(hdone[b % 3], 16 * (b // 3))
                    pool.wait_ge(sem("ys_used"), b - 2)
                pool.dma_start(hb[:, b % 3, :].rearrange("p (h v) -> p h v", h=SH), ssm_v[b]).then_inc(hsem[b % 3], 16)

            def rload(b):
                if b >= 4:
                    pool.wait_ge(rdone[b % 4], 32 * (b // 4))
                    pool.wait_ge(sem("os_used"), b - 3)
                for r in range(2):
                    pool.dma_start(rb[64 * r:64 * r + 64, b % 4, :].rearrange("p (c v) -> p c v", v=RV), ret_v[b, r])\
                        .then_inc(rsem[b % 4], 16)

            for b in range(3):
                hload(b)
            for b in range(4):
                rload(b)
            store(ssmc_s[0, :, 0:SCONV - 2, :], w["state_ssm_conv"][0, :, 1:SCONV - 1, :])
            store(pool_s[0, :, 0:PST - 1, :], w["state_pool"][0, :, 1:PST, :])
            store(conv_s[0, :, 0:CK - 2, :], w["state_conv"][0, :, 1:CK - 1, :])
            taken(pool, ("xbc", XT - 1))
            nc.gpsimd.tensor_copy(tailT0[:, :, 0:3], xr[:, :, NP:NP + 3])
            nc.gpsimd.tensor_copy(tailT0[:, :, 3:11], xrs[:, :, :, SCONV - 1]).then_inc(sem("tail0_ready"), 1)
            taken(pool, ("tail0", 2))
            pool.dma_start(ssmc_p[0, 0], tailtok[0:3, :]).then_inc(sem("tail0_out"), 16)
            pool.dma_start(ssmc_s[0, :, SCONV - 2, :], tailtok[3:11, :]).then_inc(sem("tail0_out"), 16)

            taken(pool, ("eab",))
            for b in range(NB):
                pool.wait_ge(hsem[b % 3], 16 * (b // 3 + 1))
                hv = hb[:, b % 3, :].rearrange("p (h v) -> p h v", h=SH)
                nc.gpsimd.tensor_tensor(hv, hv, eab[:, b, :].unsqueeze(2).to_broadcast([P, SH, SD]), ALU.mult)\
                    .then_inc(sem("h_decayed"), 1)
                if b and b + 2 < NB:
                    hload(b + 2)
                taken(pool, ("xb", b, 1))
                pool.dma_start(ssm_o[b], hv).then_inc(hdone[b % 3], 16)
            for g in range(SG):
                taken(pool, ("kv", 1, g))
            pool.dma_start(ssm_p[0, 0].rearrange("h k v -> k h v"), hst[:, :, :].rearrange("p g (h v) -> p (g h) v", v=SD))\
                .then_inc(sem("ssm_p_out"), 16)

            def memload():
                load(memtok[:, 0, :], w["mem_prompt"][0, 0:P, :], "mem_in")
                load(memtok[:, 1, :], w["mem_prompt"][0, P:ML, :], "mem_in")

            full(pool, ("yss", 1))
            memload()
            for b in range(NB):
                pool.wait_ge(rsem[b % 4], 32 * (b // 4 + 1))
                rv = rb[:, b % 4, :].rearrange("p (c v) -> p c v", v=RV)
                nc.gpsimd.tensor_tensor(rv, rv, const("gone").unsqueeze(2).to_broadcast([P, RH // 2, RV]), ALU.mult)\
                    .then_inc(sem("r_decayed"), 1)
                if b and b + 3 < NB:
                    rload(b + 3)
                taken(pool, ("vb", b))
                for r in range(2):
                    pool.dma_start(ret_o[b, r], rb[64 * r:64 * r + 64, b % 4, :].rearrange("p (c v) -> p c v", v=RV))\
                        .then_inc(rdone[b % 4], 16)
                if b == 3:
                    taken(pool, ("rkv", 1))
                    ret_po = ret_p[0, 0].rearrange("(c r) k v -> r k c v", r=2)
                    for r in range(2):
                        pool.dma_start(ret_po[r], rst[64 * r:64 * r + 64, 0, :].rearrange("p (c v) -> p c v", v=RV))\
                            .then_inc(sem("ret_p_out"), 16)
            even_stored(pool)
            pool.wait_ge(sem("ret_p_out"), 32)
            caches = [w["cache_mem_k"], w["cache_mem_v"]]

            def kvload(l, n):
                i = 2 * NB * l + n
                src = caches[n // NB][l, n % NB].rearrange("(m p) h d -> p m (h d)", p=P)
                pool.dma_start(kv[:, i % KV_SLOTS, :, :], src).then_inc(sem(f"kv_in{i % KV_SLOTS}"), 16)

            def memory_k_out(l):
                taken(pool, (f"xk{l}", 3, 1))
                pool.dma_start(mk_p[l, 0].rearrange("(m p) h d -> p m (h d)", p=P), Kt[:, :, :]).then_inc(sem("kst"), 16)

            def more_kv(l):
                for n in range(KV_SLOTS, 2 * NB):
                    old = n - KV_SLOTS
                    if old == NB:
                        taken(pool, (f"xv{l}", 3, 1))
                        pool.dma_start(mv_p[l, 0].rearrange("(m p) h d -> p m (h d)", p=P), Vt[:, :, :]).then_inc(sem("vst"), 16)
                    if old < NB:
                        taken(pool, ("qb", l, old, 1))
                    else:
                        pool.wait_ge(sem("v_used"), (NB - 1) * l + old - NB + 1)
                    kvload(l, n)

            pool.wait_ge(sem("mixed_ready"), 1)
            for n in range(KV_SLOTS):
                kvload(0, n)
            memory_k_out(0)
            more_kv(0)
            taken(pool, ("xo0", KT - 1))
            memload()
            for n in range(KV_SLOTS):
                kvload(1, n)
            load(st_pool[0:120, :], w["state_pool"][0].rearrange("b s c -> (b s) c"), "ost_in")
            for j in range(2):
                load(st_conv[0:120, j, :], w["state_conv"][0, 4 * j:4 * j + 4].rearrange("b s c -> (b s) c"), "ost_in")
            load(pw[:, :, :], w["pool_w"][0].rearrange("g c d -> c g d"), "pw_in")
            pool.wait_ge(sem("odd_raw"), 4)
            nc.gpsimd.tensor_copy(tl1[:, :, 0:15], up[:, :, NP:NP + 15])
            nc.gpsimd.tensor_copy(tl1[:, :, 15:23], us[:, :, :, PST])
            nc.gpsimd.tensor_copy(tl2[:, :, 0:30], gp[:, :, NP:NP + 30])
            nc.gpsimd.tensor_copy(tl2[:, :, 30:38], gs[:, :, :, CK - 1]).then_inc(sem("tail1_ready"), 1)
            taken(pool, ("tail2",))
            for dst, src in ((pool_p[0, 0], tok1[0:15, :]), (pool_s[0, :, PST - 1, :], tok1[15:23, :]),
                             (conv_p[0, 0], tok2[0:30, :]), (conv_s[0, :, CK - 2, :], tok2[30:38, :])):
                pool.dma_start(dst, src).then_inc(sem("odd_out"), 16)
            memory_k_out(1)
            more_kv(1)
            taken(pool, ("xo1", KT - 1))
            pool.wait_ge(sem("kst"), 32)
            pool.wait_ge(sem("vst"), 32)
            load(rwt[:, :, :], w["router_w"][0].rearrange("(t p) e -> p t e", p=P), "router_in")
            load(rbt[0:1, :], w["router_b"], "router_in")
            pool.wait_ge(sem("fin_tok"), 3)
            for c in range(NC):
                store(y_p[0, c * P:(c + 1) * P, :], fin[:, c, :])
            store(y_s.rearrange("b s d -> (b s) d"), fin[0:NB, 2, :])
            pool.wait_ge(sem("stored"), stored[0])

        @block.tensor
        def _(pe):
            mm, tr = nc.tensor.matmul, nc.tensor.transpose
            ident, ones = const("ident"), const("ones")
            made = [0]

            def begin(key):
                g = G[key]
                assert g == made[0], (key, g, made[0])
                made[0] += 1
                if g >= BANKS:
                    pe.wait_ge(bank_free[g % BANKS], g // BANKS)
                return psum[:, g % BANKS, :]

            def end(key, ins):
                ins.then_inc(bank_full[G[key] % BANKS], 1)

            def arrived(i):
                pe.wait_ge(slot_full[i % TRUNK_RING], 16 * (i // TRUNK_RING + 1))

            def linear(name, nb, chunks, rhs, width=256, tiles=2, first=0, ready=None, norm=None, memory=None):
                for b in range(first, first + nb):
                    outs_ = [begin((name, tiles * b + m)) for m in range(tiles)]
                    base = 0
                    for kc, kn in enumerate(chunks):
                        i = item_at[(name, b, kc)]
                        arrived(i)
                        wv = slot_view(i % TRUNK_RING, kn, width)
                        mw = min(P, width)
                        for m in range(tiles):
                            for k in range(kn):
                                if ready is not None and b == first and m == 0:
                                    pe.wait_ge(sem("h_ready"), KT * ready + k + 1)
                                ins = mm(outs_[m][0:mw, 0:T], wv[:, k, m * mw:(m + 1) * mw], rhs(base + k),
                                         start=(base + k == 0), stop=(kc == len(chunks) - 1 and k == kn - 1),
                                         skip_group_check=True)
                            if kc == len(chunks) - 1 and m < tiles - 1:
                                end((name, tiles * b + m), ins)
                        if kc < len(chunks) - 1:
                            ins.then_inc(chunk_used, 1)
                        base += kn
                    end((name, tiles * b + tiles - 1), ins)
                    if b == 0 and memory is not None:
                        square_sum(MEM_NORM[memory], memsq[:, 0, :], ML)
                if norm is not None:
                    square_sum(norm, hT[:, 0, :], T)

            def square_sum(n, src, width):
                o = begin(("ss", n))
                pe.wait_ge(sem("sq_ready"), n + 1)
                end(("ss", n), mm(o[:, 0:width], ones, src, start=True, stop=True))

            def sumsq(key, src, n, width):
                o = begin(key)
                for k in range(n):
                    ins = mm(o[:, 0:width], ones, src(k), start=(k == 0), stop=(k == n - 1))
                end(key, ins)

            pe.wait_ge(sem("consts_in"), 16)
            pe.wait_ge(sem("x_in"), 48)
            for t in range(KT):
                o = begin(("xT", t))
                for c in range(NC):
                    tr(o[:, c * P:(c + 1) * P], stage_x[:, c, t * P:(t + 1) * P], ident)
                end(("xT", t), tr(o[:, NP:T], stage_s[0:NB, t * P:(t + 1) * P], ident[0:NB, 0:NB]))
            square_sum(0, hT[:, 0, :], T)

            pe.wait_ge(sem("params_in"), 16 * 13)
            prow = zg[:, 0:3, 0:P]
            o = begin(("params",))
            for g, (at, n) in enumerate(((0, 128), (128, 28), (156, 124))):
                ins = tr(o[:, at:at + n], prow[0:n, g, :], ident[0:n, 0:n])
            end(("params",), ins)
            pe.wait_ge(sem("cst_in"), 16)
            o = begin(("cst",))
            for t in range(XT):
                ins = tr(o[:, 24 * t:24 * t + 24], stage_c[0:24, t * P:(t + 1) * P], ident[0:24, 0:24])
            end(("cst",), ins)

            def h_in(k):
                return hT[:, k, :]

            linear("xbc", 6, [8], h_in, ready=0)
            linear("dt", 1, [8], h_in, width=SH, tiles=1)
            linear("q", 2, [8], h_in)
            linear("k", 2, [8], h_in)
            pe.wait_ge(sem("tail0_ready"), 1)
            for j in range(3):
                o = begin(("tail0", j))
                for t in range(4):
                    ins = tr(o[0:11, t * P:(t + 1) * P], tailT0[:, 4 * j + t, :], ident)
                end(("tail0", j), ins)
            linear("v", 4, [8], h_in)

            pe.wait_ge(sem("dt_ready"), 1)
            o = begin(("dtT",))
            for n, src in enumerate((dtT, acT)):
                for c in range(NC):
                    tr(o[:, (2 * n + c) * SH:(2 * n + c + 1) * SH], src[0:SH, c * P:(c + 1) * P], ident[0:SH, 0:SH])
            end(("dtT",), tr(o[0:NB, 4 * SH:5 * SH], dtT[0:SH, NP:T], ident[0:SH, 0:SH]))
            pe.wait_ge(sem("small_in"), 48)
            o = begin(("dbc",))
            end(("dbc",), mm(o[:, 0:SH], ones[0:1, :], D_row, start=True, stop=True))
            pe.wait_ge(sem("xc_ready"), XT)
            o = begin(("Btok",))
            for c in range(NC):
                for g in range(SG):
                    ins = tr(o[:, (2 * c + g) * P:(2 * c + g + 1) * P], xc[:, 8 + g, c * P:(c + 1) * P], ident)
            end(("Btok",), ins)
            for c in range(NC):
                for j in range(2):
                    o = begin(("xtok", c, j))
                    for t in range(4):
                        ins = tr(o[:, t * P:(t + 1) * P], xc[:, 4 * j + t, c * P:(c + 1) * P], ident)
                    end(("xtok", c, j), ins)
            o = begin(("CB",))
            for g in range(SG):
                for c in range(NC):
                    ins = mm(o[:, (2 * g + c) * P:(2 * g + c + 1) * P], xc[:, 8 + g, c * P:(c + 1) * P],
                             xc[:, 10 + g, c * P:(c + 1) * P], start=True, stop=True)
            end(("CB",), ins)
            for j in range(2):
                o = begin(("xstok", j))
                for t in range(4):
                    ins = tr(o[0:NB, t * P:(t + 1) * P], xc[:, 4 * j + t, NP:T], ident)
                end(("xstok", j), ins)
            pe.wait_ge(sem("ead_ready"), 1)
            o = begin(("eab",))
            end(("eab",), mm(o[:, 0:NB * SH], ones[0:SH, :], eaD[0:SH, :, :].rearrange("p b h -> p (b h)"), start=True, stop=True))

            def decay_rows(s):
                c, g = s // SG, s % SG
                for j in range(2):
                    o = begin(("bc", c, g, j))
                    for q in range(4):
                        h = 8 * g + 4 * j + q
                        ins = mm(o[:, q * P:(q + 1) * P], ident[0:SH, h:h + 1].to_broadcast([SH, P]),
                                 acT[0:SH, c * P:(c + 1) * P], start=True, stop=True)
                    end(("bc", c, g, j), ins)

            def sample_y(b):
                taken(pe, ("xb", b, 1))
                if b == 0:
                    pe.wait_ge(sem("c_spread"), 1)
                for g in range(SG):
                    ins = mm(psum[0:NB, SUMS + g, :], Zc[:, g, b * NB:(b + 1) * NB], hb[:, b % 3, g * 512:(g + 1) * 512],
                             start=(b == 0), stop=(b == NB - 1), skip_group_check=True)
                ins.then_inc(sem("ys_used"), 1)

            def rows_turned(o, rows, n, count):
                pe.wait_ge(sem("sums_out"), count)
                for t in range(rows.shape[1] // P):
                    ins = tr(o[:, t * n:(t + 1) * n], rows[0:n, t * P:(t + 1) * P], ident[0:n, 0:n])
                return ins

            def sample_x(b):
                if b == 0:
                    taken(pe, ("xstok", 0))
                    taken(pe, ("xstok", 1))
                for g in range(SG):
                    o = begin(("xb", b, g))
                    end(("xb", b, g), mm(o, ident[0:NB, b:b + 1].to_broadcast([NB, P]), xstok[0:NB, g * 512:(g + 1) * 512],
                                         start=True, stop=True))
                if b:
                    sample_y(b - 1)

            decay_rows(0)
            for s in range(NC * SG):
                c, g = s // SG, s % SG
                if s < NC * SG - 1:
                    decay_rows(s + 1)
                sample_x(2 * s)
                o = begin(("y", c, g))
                taken(pe, ("xtok", c, g))
                for j in range(2):
                    pe.wait_ge(sem("s_ready"), 2 * s + j + 1)
                    for q in range(4):
                        hl = 4 * j + q
                        ins = mm(o[:, hl * SD:(hl + 1) * SD], S[:, 2 * (s % 2) + j, q * P:(q + 1) * P],
                                 xdt[:, c, (8 * g + hl) * SD:(8 * g + hl + 1) * SD], start=True, stop=True)
                end(("y", c, g), ins)
                if c:
                    o = begin(("yi", g))
                    taken(pe, ("kv", 0, g))
                    end(("yi", g), mm(o, xc[:, 10 + g, P:NP], hst[:, g, :], start=True, stop=True))
                o = begin(("kv", c, g))
                pe.wait_ge(sem("xdtw_ready"), s + 1)
                if s == 0:
                    taken(pe, ("Btok",))
                end(("kv", c, g), mm(o, Btok[:, c, g * P:(g + 1) * P], xdtw[:, g * 512:(g + 1) * 512], start=True, stop=True))
                linear("z", 1, [8], h_in, first=s)
                sample_x(2 * s + 1)
            sample_y(NB - 1)
            for c in range(NC):
                for g in range(SG):
                    taken(pe, ("y", c, g))
            for t in range(KT):
                o = begin(("yT", t))
                for c in range(NC):
                    ins = tr(o[:, c * P:(c + 1) * P], ytok[:, c, t * P:(t + 1) * P], ident)
                end(("yT", t), ins)
            o = begin(("ysT",))
            end(("ysT",), rows_turned(o, ysr, NB, 1))
            linear("g", 1, [8], h_in, first=0)
            pe.wait_ge(sem("ysq_ready"), 1)
            for g in range(SG):
                sumsq(("yss", g), lambda k: sqb[:, 4 * g + k, :], 4, T)

            pe.wait_ge(sem("econst_in"), 16)
            for i in range(8):
                o = begin(("rot", i))
                taken(pe, (("q", i) if i < 4 else ("k", i - 4)))
                end(("rot", i), mm(o[:, 0:T], const("rot"), qk[:, i, :], start=True, stop=True))
            for t in range(RH):
                taken(pe, ("v", t))
            for j in range(2):
                o = begin(("vstok", j))
                for t in range(4):
                    ins = tr(o[0:NB, t * P:(t + 1) * P], vT[:, 4 * j + t, NP:T], ident)
                end(("vstok", j), ins)
            linear("g", 1, [8], h_in, first=1)
            pe.wait_ge(sem("rot_done"), 8)
            for c in range(NC):
                o = begin(("ktok", c))
                for t in range(4):
                    ins = tr(o[:, t * P:(t + 1) * P], qk[:, 4 + t, c * P:(c + 1) * P], ident)
                end(("ktok", c), ins)
            for c in range(NC):
                for j in range(2):
                    o = begin(("vtok", c, j))
                    for t in range(4):
                        ins = tr(o[:, t * P:(t + 1) * P], vT[:, 4 * j + t, c * P:(c + 1) * P], ident)
                    end(("vtok", c, j), ins)

            def clear_sums(n, bank_no):
                mm(psum[0:n, SUMS + bank_no, :], zeros[:, 0:n], cbase[:, 0:512], start=True, stop=False, skip_group_check=True)

            def sample_o(b):
                taken(pe, ("vb", b))
                if b == 0:
                    pe.wait_ge(sem("q_spread"), 1)
                    pe.wait_ge(sem("zeros_set"), 1)
                    clear_sums(2 * NB, 0)
                for hh in range(RH // 2):
                    ins = mm(psum[0:2 * NB, SUMS, hh * RV:(hh + 1) * RV], Zq[:, hh, b * 2 * NB:(b + 1) * 2 * NB],
                             rb[:, b % 4, hh * RV:(hh + 1) * RV], start=False, stop=(b == NB - 1), skip_group_check=True)
                ins.then_inc(sem("os_used"), 1)

            vs4 = vstok[0:NB, :].rearrange("p (c r v) -> p c r v", r=2, v=RV)

            def sample_v(b):
                if b == 0:
                    taken(pe, ("vstok", 0))
                    taken(pe, ("vstok", 1))
                o = begin(("vb", b))
                for p in range(2):
                    ins = mm(o[64 * p:64 * p + 64, :], ident[0:NB, b:b + 1].to_broadcast([NB, 64]), vs4[:, :, p, :],
                             start=True, stop=True)
                end(("vb", b), ins)
                if b:
                    sample_o(b - 1)

            for c in range(NC):
                for p in range(2):
                    o = begin(("rs", c, p))
                    for hh in range(4):
                        ins = mm(o[:, hh * P:(hh + 1) * P], qk[64 * p:64 * p + 64, 4 + hh, c * P:(c + 1) * P],
                                 qk[64 * p:64 * p + 64, hh, c * P:(c + 1) * P], start=True, stop=True)
                    end(("rs", c, p), ins)
                sample_v(2 * c)
                linear("g", 1, [8], h_in, first=2 + c)
                for j in range(2):
                    taken(pe, ("vtok", c, j))
                for p in range(2):
                    o = begin(("ro", c, p))
                    taken(pe, ("rs", c, p))
                    for hh in range(4):
                        h = 2 * hh + p
                        ins = mm(o[:, hh * P:(hh + 1) * P], S[:, 2 * c + p, hh * P:(hh + 1) * P], vtok[:, c, h * RV:(h + 1) * RV],
                                 start=True, stop=True)
                    end(("ro", c, p), ins)
                if c:
                    taken(pe, ("rkv", 0))
                    for p in range(2):
                        o = begin(("ri", p))
                        for hh in range(4):
                            ins = mm(o[:, hh * P:(hh + 1) * P], qk[64 * p:64 * p + 64, hh, P:NP],
                                     rst[64 * p:64 * p + 64, 0, hh * P:(hh + 1) * P], start=True, stop=True)
                        end(("ri", p), ins)
                o = begin(("rkv", c))
                taken(pe, ("ktok", c))
                for hh in range(4):
                    for p in range(2):
                        h = 2 * hh + p
                        ins = mm(o[64 * p:64 * p + 64, hh * P:(hh + 1) * P], ktok[:, c, h * RK:(h + 1) * RK],
                                 vtok[:, c, h * RV:(h + 1) * RV], start=True, stop=True)
                end(("rkv", c), ins)
                sample_v(2 * c + 1)
            for b in range(4, NB):
                sample_v(b)
            sample_o(NB - 1)
            pe.wait_ge(sem("o_scaled"), NC)
            for h in range(RH):
                o = begin(("oT", h))
                at = ((h % 2) * 4 + h // 2) * P
                for c in range(NC):
                    ins = tr(o[:, c * P:(c + 1) * P], otok[:, c, at:at + P], ident)
                end(("oT", h), ins)
            o = begin(("osT",))
            end(("osT",), rows_turned(o, osr, 2 * NB, 2))
            o = begin(("oss",))
            pe.wait_ge(sem("osq_ready"), 1)
            end(("oss",), mm(o[:, 0:RH * NB], ones, ogs.rearrange("p h b -> p (h b)"), start=True, stop=True))

            def memory_rows(l):
                pe.wait_ge(sem("mem_in"), 32 * (l + 1))
                for j in range(4):
                    o = begin(("mT", l, j))
                    for t in range(2):
                        for m in range(2):
                            ins = tr(o[:, (2 * t + m) * P:(2 * t + m + 1) * P], memtok[:, m, (2 * j + t) * P:(2 * j + t + 1) * P], ident)
                    end(("mT", l, j), ins)

            def tokmajor(name, parts=range(8)):
                for part in parts:
                    b, m = part // 2, part % 2
                    i = item_at[(name, b, 0)]
                    arrived(i)
                    wv = slot_view(i % TRUNK_RING, 8, 256)
                    o = begin((name, b, m))
                    for k in range(KT):
                        ins = mm(o[:, 0:256], mT[:, k, m * P:(m + 1) * P], wv[:, k, :], start=(k == 0), stop=(k == KT - 1))
                    end((name, b, m), ins)

            def memory_k(l):
                pe.wait_ge(sem("h_ready"), KT * (MEM_NORM[l] + 1))
                tokmajor(f"xk{l}")
                taken(pe, (f"xk{l}", 3, 1))
                for j in range(4):
                    o = begin(("KT", l, j))
                    for t in range(2):
                        for m in range(2):
                            ins = tr(o[:, (2 * t + m) * P:(2 * t + m + 1) * P], Kt[:, m, (2 * j + t) * P:(2 * j + t + 1) * P], ident)
                    end(("KT", l, j), ins)

            memory_rows(0)
            pe.wait_ge(sem("mixed_ready"), 1)
            linear("wout0", 4, [8, 8], lambda k: zg[:, k, :], norm=CROSS_NORM[0], memory=0)

            def cross(l):
                linear(f"xq{l}", 4, [8], h_in, ready=CROSS_NORM[l])
                taken(pe, (f"xq{l}", KT - 1))
                for j in range(2):
                    o = begin(("qs", l, j))
                    for t in range(4):
                        ins = tr(o[0:NB, t * P:(t + 1) * P], qT[:, 4 * j + t, NP:T], ident)
                    end(("qs", l, j), ins)
                for j in range(4):
                    taken(pe, ("KT", l, j))
                for lt in range(2):
                    for hp in range(2):
                        o = begin(("S", l, lt, hp))
                        for q in range(2):
                            h = 2 * hp + q
                            for d in range(2):
                                ins = mm(o[:, q * ML:(q + 1) * ML], qT[:, 2 * h + d, lt * P:(lt + 1) * P], KTt[:, 2 * h + d, :],
                                         start=(d == 0), stop=(d == 1))
                        end(("S", l, lt, hp), ins)
                taken(pe, ("qs", l, 0))
                taken(pe, ("qs", l, 1))
                for b in range(NB):
                    for j in range(2):
                        o = begin(("qb", l, b, j))
                        end(("qb", l, b, j), mm(o, ident[0:NB, b:b + 1].to_broadcast([NB, P]), qstok[0:NB, j * 512:(j + 1) * 512],
                                                start=True, stop=True))
                    if l == 0:
                        tokmajor("xv0", [b])
                n = 0
                for lt in range(2):
                    for hp in range(2):
                        o = begin(("PT", l, lt, hp))
                        n += 1
                        pe.wait_ge(sem("p_ready"), 4 * l + n)
                        for q in range(2):
                            for m in range(2):
                                ins = tr(o[:, (2 * q + m) * P:(2 * q + m + 1) * P], Pr[:, 2 * lt + hp, q, m * P:(m + 1) * P], ident)
                        end(("PT", l, lt, hp), ins)
                o = begin(("sT", l))
                taken(pe, ("qb", l, NB - 1, 1))
                for m in range(2):
                    ins = tr(o[0:32, m * P:(m + 1) * P], sS[:, m, :], ident)
                end(("sT", l), ins)
                taken(pe, (f"xv{l}", 3, 1))
                for lt in range(2):
                    for hp in range(2):
                        taken(pe, ("PT", l, lt, hp))
                for t in range(KT):
                    o = begin(("ao", l, t))
                    for m in range(2):
                        ins = mm(o[:, 0:NP], Vt[:, m, t * P:(t + 1) * P], PTt[:, t // 2, m, :], start=(m == 0), stop=(m == 1))
                    end(("ao", l, t), ins)
                o = begin(("pT", l))
                pe.wait_ge(sem("ps_ready"), l + 1)
                for m in range(2):
                    ins = tr(o[:, m * 32:(m + 1) * 32], Ps[0:32, m * P:(m + 1) * P], ident[0:32, 0:32])
                end(("pT", l), ins)
                clear_sums(NB, 0)
                clear_sums(NB, 1)
                taken(pe, ("pT", l))
                for b in range(NB):
                    rows = kv_in(pe, l, NB + b)
                    for h in range(XH):
                        for m in range(2):
                            ins = mm(psum[0:NB, SUMS + h // 2, (h % 2) * 256:(h % 2 + 1) * 256], Zp[:, m * XH + h, b * NB:(b + 1) * NB],
                                     rows[:, m, h * 256:(h + 1) * 256], start=False, stop=(b == NB - 1 and m == 1),
                                     skip_group_check=True)
                    ins.then_inc(sem("v_used") if b < NB - 1 else sem("aos_done"), 1)
                o = begin(("aoT", l))
                end(("aoT", l), rows_turned(o, aor, NB, 3 + l))
                taken(pe, ("aoT", l))
                for t in range(KT):
                    taken(pe, ("ao", l, t))
                linear(f"xo{l}", 4, [8], lambda k: oT[:, k, :], norm=FFN_NORM[l])

            memory_k(0)
            cross(0)
            for b in range(FF // SLOT_N):
                for name in ("f1", "f3"):
                    i = item_at[(name, b, 0)]
                    arrived(i)
                    wv = slot_view(i % TRUNK_RING, 8, 256)
                    for m in range(2):
                        o = begin((name, 2 * b + m))
                        for k in range(KT):
                            if b == 0 and name == "f1" and m == 0:
                                pe.wait_ge(sem("h_ready"), KT * FFN_NORM[0] + k + 1)
                            ins = mm(o[:, 0:T], wv[:, k, m * P:(m + 1) * P], hT[:, k, :], start=(k == 0), stop=(k == KT - 1))
                        end((name, 2 * b + m), ins)
            memory_rows(1)
            for t in range(FT):
                taken(pe, ("f3", t))
            pe.wait_ge(sem("ost_in"), 48)
            for j in range(3):
                o = begin(("ost", j))
                src = st_pool if j == 0 else st_conv[:, j - 1, :]
                for t in range(4):
                    ins = tr(o[:, t * 120:(t + 1) * 120], src[0:120, t * P:(t + 1) * P], ident[0:120, 0:120])
                end(("ost", j), ins)
            linear("f2", 4, [8, 8, 6], lambda k: hid[:, k, :], norm=ODD_NORM, memory=1)

            linear("win1", 6, [8], h_in, ready=ODD_NORM)
            pe.wait_ge(sem("tail1_ready"), 1)
            for key, src, n in ((("tail1",), tl1, 23), (("tail2",), tl2, 38)):
                o = begin(key)
                for t in range(4):
                    ins = tr(o[0:n, t * P:(t + 1) * P], src[:, t, :], ident)
                end(key, ins)
            memory_k(1)
            pe.wait_ge(sem("pw_in"), 16)
            pe.wait_ge(sem("pooled"), 4)
            for g in range(OT):
                o = begin(("pw", g))
                end(("pw", g), mm(o[:, 0:T], pw[:, g, :], pooled[:, g, :], start=True, stop=True))
            tokmajor("xv1")
            pe.wait_ge(sem("conv_taps"), OT * (CK - 1))
            sumsq(("mu",), lambda k: mixo[:, OT + k, :], OT, T)
            pe.wait_ge(sem("csq_ready"), 1)
            sumsq(("var",), lambda k: csq[:, k, :], OT, T)
            pe.wait_ge(sem("conv_act"), 4)
            for g in range(OT):
                taken(pe, ("pw", g))
            linear("wout1", 4, [8], lambda k: mixo[:, k, :], norm=CROSS_NORM[1])
            cross(1)

            pe.wait_ge(sem("h_ready"), KT * (FFN_NORM[1] + 1))
            pe.wait_ge(sem("router_in"), 32)
            o = begin(("logit",))
            for c in range(3):
                n = P if c < 2 else NB
                for k in range(KT):
                    mm(o[0:n, c * NE:(c + 1) * NE], hT[:, k, c * P:c * P + n], rwt[:, k, :], start=(k == 0), stop=False)
                ins = mm(o[0:n, c * NE:(c + 1) * NE], ones[0:1, 0:n], rbt[0:1, :], start=False, stop=True)
            end(("logit",), ins)
            o = begin(("rank",))
            pe.wait_ge(sem("picked_ready"), 1)
            for c in range(3):
                n = P if c < 2 else NB
                for b in range(c):
                    mm(o[0:n, c * NE:(c + 1) * NE], ones[:, 0:n], picked[:, b, :], start=(b == 0), stop=False)
                mm(o[0:n, c * NE:(c + 1) * NE], const("causal")[0:n, 0:n], picked[0:n, c, :], start=(c == 0), stop=True)
            for c in range(3):
                n = P if c < 2 else NB
                ins = mm(o[:, 3 * NE:4 * NE], ones[0:n, :], picked[0:n, c, :], start=(c == 0), stop=(c == 2))
            end(("rank",), ins)
            for c in range(3):
                n = P if c < 2 else NB
                for j in range(2):
                    o = begin(("htok", c, j))
                    for t in range(4):
                        ins = tr(o[0:n, t * P:(t + 1) * P], hT[:, 4 * j + t, c * P:c * P + n], ident)
                    end(("htok", c, j), ins)

            def turn_gates(o):
                for c in range(3):
                    n = P if c < 2 else NB
                    ins = tr(o[0:CAP, c * P:c * P + n], selg[0:n, c, :], ident[0:n, 0:n])
                return ins

            def gather(o, j):
                for t in range(4):
                    for c in range(3):
                        n = P if c < 2 else NB
                        ins = mm(o[:, t * CAP:(t + 1) * CAP], htok[0:n, c, (4 * j + t) * P:(4 * j + t + 1) * P], sel[0:n, c, :],
                                 start=(c == 0), stop=(c == 2))
                return ins

            o = begin(("selT0",))
            pe.wait_ge(sem("sel_ready"), 1)
            end(("selT0",), turn_gates(o))
            taken(pe, ("htok", 2, 1))
            for j in range(2):
                o = begin(("gat0", j))
                end(("gat0", j), gather(o, j))
            for j in range(2):
                taken(pe, ("gat0", j))
            taken(pe, ("selT0",))
            pe.wait_ge(sem("rounds_known"), 1)
            pairs = pe.value_load(rounds[0:1, 0:1], min_val=NE // 2, max_val=3 * NE // 2)
            side_full = [sem("side_full6"), sem("side_full7")]
            side_taken = [sem("side_taken6"), sem("side_taken7")]
            PER = (6, 5)

            def side(n, b, k):
                pe.wait_ge(side_taken[b], n * PER[b] + (k + 1))
                return psum[:, 6 + b, :]

            def scatter(n, h):
                pe.wait_ge(sem("ys_ready"), n * 2 + 1)
                for t in range(KT):
                    o = side(n, t % 2, t // 2)
                    mm(o[:, 0:T], ys[0:CAP, t * P:(t + 1) * P], selT[0:CAP, 1 - h, :], start=True, stop=True)\
                        .then_inc(side_full[t % 2], 1)

            with pe.Fori(0, pairs) as pair:
                for h in range(2):
                    n = pair * 2 + h
                    for j in range(ET // 2):
                        for g in range(2):
                            it = 2 * j + g
                            s, r = it % RING, it // RING
                            pe.wait_ge(slot_full[s], n * 32 + (base_full[s] + 16 * (r + 1)))
                            wv = slot_view(s, 8, 256)
                            for m in range(2):
                                pe.wait_ge(sem("gate_taken" if g == 0 else "up_taken"), n * ET + (max(2 * j + m - 1, 0) + 1))
                                for k in range(KT):
                                    ins = mm(psum[:, 2 * g + m, 0:CAP], wv[:, k, m * P:(m + 1) * P], hg[:, h, k, :],
                                             start=(k == 0), stop=(k == KT - 1))
                                ins.then_inc(eu, 1)
                    scatter(n, h)
                    o = side(n, 0, 4)
                    pe.wait_ge(sem("sel_ready"), n + 2)
                    turn_gates(o).then_inc(side_full[0], 1)
                    gather(side(n, 1, 4), 0).then_inc(side_full[1], 1)
                    gather(side(n, 0, 5), 1).then_inc(side_full[0], 1)
                    pe.wait_ge(sem("up_taken"), n * ET + (ET + 1))
                    pe.wait_ge(sem("ys_ready"), n * 2 + 1)
                    for d in range(4):
                        for kc in range(2):
                            it = 14 + 2 * d + kc
                            s, r = it % RING, it // RING
                            pe.wait_ge(slot_full[s], n * 32 + (base_full[s] + 16 * (r + 1)))
                            wv = slot_view(s, 7, 256)
                            for k in range(7):
                                ins = mm(psum[0:CAP, 4 + d // 2, (d % 2) * 256:(d % 2 + 1) * 256], ehid[:, 7 * kc + k, :], wv[:, k, :],
                                         start=(kc == 0 and k == 0), stop=(kc == 1 and k == 6))
                            ins.then_inc(eh if kc == 0 else ed, 1)
                    pe.wait_ge(sem("gate_taken"), n * ET + (ET + 1))
                    pe.wait_ge(side_taken[0], n * PER[0] + 7)
                    pe.wait_ge(side_taken[1], n * PER[1] + 6)
            scatter(pe.snap(pairs * 2), 0)
            pe.wait_ge(sem("sq_ready"), 9)
            mm(psum[:, 0, 0:T], ones, hT[:, 0, :], start=True, stop=True).then_inc(sem("final_ss"), 1)
            pe.wait_ge(sem("h_ready"), KT * 9)
            for c in range(3):
                n = P if c < 2 else NB
                for j in range(2):
                    for t in range(4):
                        ins = tr(psum[0:n, 1 + 2 * c + j, t * P:(t + 1) * P], hT[:, 4 * j + t, c * P:c * P + n], ident)
                ins.then_inc(sem("final_tok"), 1)


        @block.scalar
        def _(act):
            af = nc.scalar.activation

            def free(key, ins):
                ins.then_inc(bank_free[G[key] % BANKS], 1)

            act.wait_ge(sem("eps_set"), 1)

            def norm(n, width=T):
                full(act, ("ss", n))
                free(("ss", n), af(rstd[:, 0:width], bank(("ss", n))[:, 0:width], ACT.Sqrt, scale=1.0 / DM, bias=eps[:, 0:1]))

            norm(0)
            taken(act, ("params",))
            for t in range(XT):
                taken(act, ("xbc", t))
                af(xc[:, t, 0:NP], xr[:, t, 0:NP], ACT.Identity, scale=gain("scw", t), bias=gain("scb", t))\
                    .then_inc(sem("tap0"), 1)

            def gate_out(name, t):
                for i in (t, t + 1):
                    full(act, (name, i))
                    free((name, i), af(zg[:, (0 if name == "z" else 8) + i, :], bank((name, i))[:, 0:T], ACT.Copy))

            act.wait_ge(sem("conv0"), 1)
            for t in range(XT):
                af(xc[:, t, :], xc[:, t, :], ACT.Silu).then_inc(sem("xc_ready"), 1)
            for j in range(3):
                full(act, ("tail0", j))
                free(("tail0", j), af(tailtok[:, j * 512:(j + 1) * 512], bank(("tail0", j))[0:11, :], ACT.Copy))
            act.wait_ge(sem("u_ready"), 1)
            act.wait_ge(sem("small_in"), 48)
            af(ea_t, a_log_t, ACT.Exp)
            af(dtmp[0:SH, 2, :], dtmp[0:SH, 1, :], ACT.Exp).then_inc(sem("e_ready"), 1)
            act.wait_ge(sem("w_ready"), 1)
            af(dtmp[0:SH, 4, :], dtmp[0:SH, 3, :], ACT.Ln).then_inc(sem("ln_ready"), 1)
            act.wait_ge(sem("dt_ready"), 1)
            af(ea[0:SH, :], acT[0:SH, NP:T], ACT.Exp).then_inc(sem("ea_ready"), 1)
            taken(act, ("dtT",))
            af(eac, tk[:, 1, 1, :], ACT.Exp).then_inc(sem("eac_ready"), 1)

            def decays(s):
                c, g = s // SG, s % SG
                for j in range(2):
                    act.wait_ge(sem("diff_ready"), 2 * s + j + 1)
                    sv = S[:, 2 * (s % 2) + j, :]
                    af(sv, sv, ACT.Exp).then_inc(sem("decay_ready"), 1)
                act.wait_ge(sem("wdiff_ready"), s + 1)
                w8 = wend[:, c, 8 * g:8 * g + 8]
                af(w8, w8, ACT.Exp).then_inc(sem("wend_ready"), 1)

            decays(0)
            for s in range(NC * SG):
                if s < NC * SG - 1:
                    decays(s + 1)
                if s == NC * SG - 2:
                    af(etot, tot[:, 1, :], ACT.Exp).then_inc(sem("etot_ready"), 1)
                gate_out("z", 2 * s)

            def sums_out(dst, n, banks):
                src = psum[0:n, SUMS:SUMS + banks, :].rearrange("p a b -> p (a b)")
                af(dst[0:n, :], src, ACT.Copy).then_inc(sem("sums_out"), 1)

            act.wait_ge(sem("ys_used"), NB)
            sums_out(ysr, NB, 2)
            taken(act, ("z", KT - 1))
            af(zg[:, 0:KT, :], zg[:, 0:KT, :], ACT.Silu).then_inc(sem("z_ready"), 1)
            gate_out("g", 0)
            for g in range(SG):
                full(act, ("yss", g))
                free(("yss", g), af(rs2[:, g, :], bank(("yss", g))[:, 0:T], ACT.Sqrt, scale=1.0 / 512, bias=eps[:, 0:1]))
            gate_out("g", 2)
            for c in range(NC):
                gate_out("g", 4 + 2 * c)
                if c:
                    taken(act, ("g", RH - 1))
                    af(zg[:, KT:, :], zg[:, KT:, :], ACT.Silu).then_inc(sem("g_ready"), 1)
                act.wait_ge(sem("o_rows"), c + 1)
                for h in range(RH):
                    af(junk, otok[:, c, h * P:(h + 1) * P], ACT.Square, accum_out=oms[:, c, h:h + 1]).then_inc(sem("o_squared"), 1)
                    act.wait_ge(sem("o_squared"), RH * c + h + 1)
                af(oms[:, c, :], oms[:, c, :], ACT.Sqrt, scale=1.0 / RV, bias=eps[:, 0:1]).then_inc(sem("o_root"), 1)
            act.wait_ge(sem("os_used"), NB)
            sums_out(osr, 2 * NB, 1)
            full(act, ("oss",))
            free(("oss",), af(ogs.rearrange("p h b -> p (h b)"), bank(("oss",))[:, 0:RH * NB], ACT.Sqrt, scale=1.0 / RV, bias=eps[:, 0:1]))

            def memory_out(name, dst, parts=range(8)):
                for part in parts:
                    b, m = part // 2, part % 2
                    full(act, (name, b, m))
                    free((name, b, m), af(dst[:, m, b * 256:(b + 1) * 256], bank((name, b, m))[:, 0:256], ACT.Copy))

            def memory_k(l):
                memory_out(f"xk{l}", Kt)
                for j in range(4):
                    key = ("KT", l, j)
                    full(act, key)
                    free(key, af(KTt[:, 2 * j:2 * j + 2, :].rearrange("p t m -> p (t m)"), bank(key), ACT.Copy))

            def cross(l):
                if l:
                    norm(CROSS_NORM[1])
                n = 0
                for lt in range(2):
                    for hp in range(2):
                        key = ("S", l, lt, hp)
                        n += 1
                        act.wait_ge(sem("mx_ready"), 4 * l + n)
                        for q in range(2):
                            c = 4 * lt + 2 * hp + q
                            ins = af(Pr[:, 2 * lt + hp, q, :], bank(key)[:, q * ML:(q + 1) * ML], ACT.Exp, scale=1.0 / 16,
                                     bias=nmx[:, c:c + 1], accum_out=rsum[:, c:c + 1])
                        free(key, ins)
                if l == 0:
                    memory_out("xv0", Vt)
                act.wait_ge(sem("smx_ready"), l + 1)
                free(("sT", l), af(Ps[0:32, :], bank(("sT", l))[0:32, 0:ML], ACT.Exp, scale=1.0 / 16, bias=nms, accum_out=rss))
                for t in range(KT):
                    key = ("ao", l, t)
                    full(act, key)
                    free(key, af(oT[:, t, 0:NP], bank(key)[:, 0:NP], ACT.Copy))
                act.wait_ge(sem("aos_done"), l + 1)
                sums_out(aor, NB, 2)

            norm(MEM_NORM[0], ML)
            norm(CROSS_NORM[0])
            memory_k(0)
            cross(0)
            norm(3)
            for t in range(FT):
                if t >= 2:
                    taken(act, ("f3", t - 2))
                full(act, ("f1", t))
                free(("f1", t), af(sil[:, t % 2, :], bank(("f1", t))[:, 0:T], ACT.Silu))
            norm(MEM_NORM[1], ML)
            norm(ODD_NORM)
            for t in range(OT):
                key = ("win1", 8 + t)
                full(act, key)
                free(key, af(csq[:, t, :], bank(key)[:, 0:T], ACT.Sigmoid))
            for t in range(OT):
                act.wait_ge(sem("odd_raw"), t + 1)
                af(mixo[:, OT + t, 0:NP], gp[:, t, 0:NP], ACT.Identity, scale=gain("ccw", t), bias=gain("ccb", t))\
                    .then_inc(sem("ctap0"), 1)
            for key, dst, n in ((("tail1",), tok1, 23), (("tail2",), tok2, 38)):
                full(act, key)
                free(key, af(dst[0:n, :], bank(key)[0:n, :], ACT.Copy))
            memory_k(1)
            for g in range(OT):
                key = ("pw", g)
                full(act, key)
                free(key, af(mixo[:, g, :], bank(key)[:, 0:T], ACT.Copy, scale=gain("pscale", g)))
            memory_out("xv1", Vt)
            full(act, ("var",))
            free(("var",), af(rstd[:], bank(("var",))[:, 0:T], ACT.Sqrt, scale=1.0 / 512, bias=eps[:, 0:1]))
            for t in range(OT):
                act.wait_ge(sem("cnorm"), t + 1)
                af(mixo[:, OT + t, :], mixo[:, OT + t, :], ACT.Silu, scale=gain("cng", t), bias=gain("cnb", t))\
                    .then_inc(sem("conv_act"), 1)
            cross(1)
            norm(7)
            act.wait_ge(sem("gap_ready"), 1)
            af(gt[:, :, 1:2], gt[:, :, 0:1], ACT.Exp).then_inc(sem("gap_exp"), 1)
            act.sem_inc(sem("gate_taken"), 1)
            act.wait_ge(sem("rounds_known"), 1)
            pairs = act.value_load(rounds[0:1, 0:1], min_val=NE // 2, max_val=3 * NE // 2)
            side_full = [sem("side_full6"), sem("side_full7")]
            side_taken = [sem("side_taken6"), sem("side_taken7")]
            with act.Fori(0, pairs) as pair:
                for h in range(2):
                    n = pair * 2 + h
                    for f in range(ET):
                        act.wait_ge(eu, n * (2 * ET) + (4 * (f // 2) + f % 2 + 1))
                        act.wait_ge(sem("up_taken"), n * ET + (max(f - 1, 0) + 1))
                        af(esil[:, f % 2, :], psum[:, f % 2, 0:CAP], ACT.Silu).then_inc(sem("gate_taken"), 1)
                    act.wait_ge(side_full[0], n * 6 + 5)
                    af(selT[0:CAP, 1 - h, :], psum[0:CAP, 6, 0:T], ACT.Copy).then_inc(side_taken[0], 1)
                    act.wait_ge(side_full[1], n * 5 + 5)
                    af(hg[:, 1 - h, 0:4, :], psum[:, 7, 0:4 * CAP].rearrange("p (t s) -> p t s", t=4), ACT.Copy).then_inc(side_taken[1], 1)
                    act.wait_ge(side_full[0], n * 6 + 6)
                    af(hg[:, 1 - h, 4:8, :], psum[:, 6, 0:4 * CAP].rearrange("p (t s) -> p t s", t=4), ACT.Copy).then_inc(side_taken[0], 1)
                    for j in range(2):
                        act.wait_ge(ed, n * 4 + (2 * j + 2))
                        af(ys[0:CAP, j * 512:(j + 1) * 512], psum[0:CAP, 4 + j, :], ACT.Copy).then_inc(sem("ys_ready"), 1)
            act.wait_ge(sem("final_ss"), 1)
            af(rstd[:], psum[:, 0, 0:T], ACT.Sqrt, scale=1.0 / DM, bias=eps[:, 0:1]).then_inc(sem("final_root"), 1)

        @block.vector
        def _(dve):
            v = nc.vector
            chain = [0]

            def step(ins):
                chain[0] += 1
                ins.then_inc(sem("dve_chain"), 1)
                dve.wait_ge(sem("dve_chain"), chain[0])

            def free(key, ins, wait=False):
                ins.then_inc(bank_free[G[key] % BANKS], 1)
                if wait:
                    taken(dve, key)

            def square(x, sq, t):
                step(v.tensor_tensor(sq[:, t, :], x[:, t, :], x[:, t, :], ALU.mult))
                if 0 < t < KT - 1:
                    step(v.tensor_tensor(sq[:, 0, :], sq[:, 0, :], sq[:, t, :], ALU.add))
                elif t:
                    v.tensor_tensor(sq[:, 0, :], sq[:, 0, :], sq[:, t, :], ALU.add).then_inc(sem("sq_ready"), 1)

            def norm(n, name, t0, x, h, width=T, root=None):
                if root is None:
                    taken(dve, ("ss", n))
                else:
                    dve.wait_ge(root, 1)
                step(v.reciprocal(rstd[:, 0:width], rstd[:, 0:width]))
                for t in range(KT):
                    v.scalar_tensor_tensor(out=h[:, t, :], in0=x[:, t, :], scalar=gain(name, t0 + t), in1=rstd[:, 0:width],
                                           op0=ALU.mult, op1=ALU.mult).then_inc(sem("h_ready"), 1)

            def x_norm(n, name, t0):
                norm(n, name, t0, xT, hT)

            def add_x(name):
                for t in range(KT):
                    full(dve, (name, t))
                    free((name, t), v.tensor_tensor(xT[:, t, :], xT[:, t, :], bank((name, t))[:, 0:T], ALU.add), wait=True)
                    square(xT, hT, t)

            for t in range(KT):
                full(dve, ("xT", t))
                free(("xT", t), v.tensor_copy(xT[:, t, :], bank(("xT", t))[:, 0:T]), wait=True)
                square(xT, hT, t)
            full(dve, ("params",))
            free(("params",), v.tensor_copy(par[:], bank(("params",))[:, 0:NPAR]), wait=True)
            full(dve, ("cst",))
            free(("cst",), v.tensor_copy(cst_keep, bank(("cst",))[:, 0:24 * XT]))
            x_norm(0, "mix", 0)
            step(v.memset(xr[:, :, 0:SCONV - 1], 0.0))
            v.tensor_copy(xrs[:, :, :, 0:SCONV - 1], cst_keep.rearrange("p (t b s) -> p t b s", t=XT, s=SCONV - 1))
            for t in range(XT):
                full(dve, ("xbc", t))
                v.tensor_copy(xrs[:, t, :, SCONV - 1], bank(("xbc", t))[:, NP:T])
                free(("xbc", t), v.tensor_copy(xr[:, t, SCONV - 1:], bank(("xbc", t))[:, 0:NP]), wait=True)
            full(dve, ("dt", 0))
            dve.wait_ge(sem("small_in"), 48)
            u, na, ex, wv, ln = (dtmp[0:SH, i, :] for i in range(5))
            free(("dt", 0), v.tensor_scalar(u, bank(("dt", 0))[0:SH, 0:T], dt_bias_t, None, ALU.add), wait=True)
            v.scalar_tensor_tensor(out=na, in0=u, scalar=-1.0, in1=u, op0=ALU.mult, op1=ALU.min).then_inc(sem("u_ready"), 1)
            for k in range(1, SCONV):
                for t in range(XT):
                    if k == 1:
                        dve.wait_ge(sem("tap0"), t + 1)
                    else:
                        dve.wait_ge(sem("taps"), XT * (k - 2) + t + 1)
                    v.scalar_tensor_tensor(out=xc[:, t, 0:NP], in0=xr[:, t, k:k + NP], scalar=gain("scw", k * XT + t),
                                           in1=xc[:, t, 0:NP], op0=ALU.mult, op1=ALU.add).then_inc(sem("taps"), 1)
            sx = xc[:, :, NP:T]
            wk_ = lambda k: par[:, COL["scw"] + k * XT:COL["scw"] + (k + 1) * XT].unsqueeze(2).to_broadcast([P, XT, NB])
            bias_ = par[:, COL["scb"]:COL["scb"] + XT].unsqueeze(2).to_broadcast([P, XT, NB])
            tmp = cst_keep[:, 0:XT * NB].rearrange("p (t b) -> p t b", t=XT)
            step(v.tensor_tensor(sx, xrs[:, :, :, 0], wk_(0), ALU.mult))
            step(v.tensor_tensor(sx, sx, bias_, ALU.add))
            for k in range(1, SCONV):
                step(v.tensor_tensor(tmp, xrs[:, :, :, k], wk_(k), ALU.mult))
                if k < SCONV - 1:
                    step(v.tensor_tensor(sx, sx, tmp, ALU.add))
            v.tensor_tensor(sx, sx, tmp, ALU.add).then_inc(sem("conv0"), 1)
            for name, at in (("q", 0), ("k", 4)):
                for t in range(4):
                    full(dve, (name, t))
                    free((name, t), v.tensor_copy(qk[:, at + t, :], bank((name, t))[:, 0:T]))
            dve.wait_ge(sem("e_ready"), 1)
            v.tensor_scalar(wv, ex, 1.0, None, ALU.add).then_inc(sem("w_ready"), 1)
            dve.wait_ge(sem("w_ready"), 1)
            step(v.tensor_scalar(na, wv, -1.0, None, ALU.add))
            dve.wait_ge(sem("ln_ready"), 1)
            step(v.tensor_scalar(wv, na, 0.0, None, ALU.is_equal))
            step(v.tensor_tensor(na, na, wv, ALU.add))
            step(v.reciprocal(na, na))
            step(v.tensor_tensor(ln, ln, na, ALU.mult))
            step(v.tensor_tensor(ln, ln, wv, ALU.add))
            step(v.tensor_tensor(ln, ln, ex, ALU.mult))
            step(v.scalar_tensor_tensor(out=dtT[0:SH, :], in0=u, scalar=0.0, in1=ln, op0=ALU.max, op1=ALU.add))
            step(v.tensor_scalar(na, dtT[0:SH, :], ea_t, -1.0, ALU.mult, ALU.mult))
            for c in range(NC):
                v.tensor_tensor_scan(acT[0:SH, c * P:(c + 1) * P], const("ones")[0:SH, :], na[:, c * P:(c + 1) * P], 0.0,
                                     ALU.mult, ALU.add)
            v.tensor_copy(acT[0:SH, NP:T], na[:, NP:T]).then_inc(sem("dt_ready"), 1)
            for t in range(RH):
                full(dve, ("v", t))
                free(("v", t), v.tensor_copy(vT[:, t, :], bank(("v", t))[:, 0:T]))
            full(dve, ("dtT",))
            v.tensor_copy(tk[:, :, :, :].rearrange("p a c h -> p (a c h)"), bank(("dtT",))[:, 0:4 * SH])
            free(("dtT",), v.tensor_copy(dtst[0:NB, :], bank(("dtT",))[0:NB, 4 * SH:5 * SH]), wait=True)
            full(dve, ("dbc",))
            db = bank(("dbc",))
            v.tensor_copy(Dcol[0:64, :], db[0:64, 0:SH:2])
            free(("dbc",), v.tensor_copy(Dcol[64:P, :], db[64:P, 1:SH:2]), wait=True)
            full(dve, ("Btok",))
            free(("Btok",), v.tensor_copy(Btok[:, :, :].rearrange("p c n -> p (c n)"), bank(("Btok",))))

            def heads(ap, n=8):
                return ap.rearrange("p (h v) -> p h v", h=n)

            def per_head(ap, width):
                return ap.unsqueeze(2).to_broadcast([ap.shape[0], ap.shape[1], width])

            dve.wait_ge(sem("tail0_out"), 32)
            for c in range(NC):
                for j in range(2):
                    key = ("xtok", c, j)
                    full(dve, key)
                    free(key, v.tensor_tensor(heads(xdt[:, c, j * 512:(j + 1) * 512]), heads(bank(key)),
                                              per_head(tk[:, 0, c, 8 * j:8 * j + 8], SD), ALU.mult), wait=True)
            full(dve, ("CB",))
            dve.wait_ge(sem("econst_in"), 16)
            free(("CB",), v.tensor_tensor(SM[:, :, :], bank(("CB",)).rearrange("p (a i) -> p a i", i=P),
                                          const("causal").unsqueeze(1).to_broadcast([P, SG * NC, P]), ALU.mult), wait=True)
            for j in range(2):
                key = ("xstok", j)
                full(dve, key)
                free(key, v.tensor_tensor(heads(xstok[0:NB, j * 512:(j + 1) * 512]), heads(bank(key)[0:NB, :]),
                                          per_head(dtst[0:NB, 8 * j:8 * j + 8], SD), ALU.mult))
            dve.wait_ge(sem("ea_ready"), 1)
            idn = const("ident")[0:SH, 0:SH].unsqueeze(1).to_broadcast([SH, NB, SH])
            v.tensor_tensor(eaD[0:SH, :, :], idn, ea[0:SH, :].unsqueeze(2).to_broadcast([SH, NB, SH]), ALU.mult)\
                .then_inc(sem("ead_ready"), 1)
            full(dve, ("eab",))
            free(("eab",), v.tensor_copy(eab[:, :, :].rearrange("p b h -> p (b h)"), bank(("eab",))[:, 0:NB * SH]))
            step(v.memset(Zc[:, :, :], 0.0))
            v.tensor_copy(Zc[:, :, 0:NB * NB:NB + 1], xc[:, 10:10 + SG, NP:T]).then_inc(sem("c_spread"), 1)
            dve.wait_ge(sem("eac_ready"), 1)

            def decay_logs(s):
                c, g = s // SG, s % SG
                for j in range(2):
                    key = ("bc", c, g, j)
                    full(dve, key)
                    h0 = 8 * g + 4 * j
                    for q in range(4):
                        ins = v.tensor_scalar(S[:, 2 * (s % 2) + j, q * P:(q + 1) * P], bank(key)[:, q * P:(q + 1) * P],
                                              tk[:, 1, c, h0 + q:h0 + q + 1], 0.0, ALU.subtract, ALU.min)
                    ins.then_inc(sem("diff_ready"), 1)
                    free(key, v.tensor_copy(tot[:, c, h0:h0 + 4], bank(key)[:, P - 1:512:P]), wait=(j == 1))
                hs = slice(8 * g, 8 * g + 8)
                v.tensor_tensor(wend[:, c, hs], tot[:, c, hs], tk[:, 1, c, hs], ALU.subtract).then_inc(sem("wdiff_ready"), 1)

            def sample_state(b):
                dve.wait_ge(sem("h_decayed"), b + 1)
                for g in range(SG):
                    key = ("xb", b, g)
                    full(dve, key)
                    hv = hb[:, b % 3, g * 512:(g + 1) * 512]
                    free(key, v.scalar_tensor_tensor(out=hv, in0=bank(key), scalar=xc[:, 8 + g, NP + b:NP + b + 1], in1=hv,
                                                     op0=ALU.mult, op1=ALU.add))

            decay_logs(0)
            for s in range(NC * SG):
                c, g = s // SG, s % SG
                hs = slice(8 * g, 8 * g + 8)
                if s < NC * SG - 1:
                    decay_logs(s + 1)
                for j in range(2):
                    dve.wait_ge(sem("decay_ready"), 2 * s + j + 1)
                    sv = S[:, 2 * (s % 2) + j, :].rearrange("p (q i) -> p q i", q=4)
                    v.tensor_tensor(sv, sv, SM[:, 2 * g + c, :].unsqueeze(1).to_broadcast([P, 4, P]), ALU.mult)\
                        .then_inc(sem("s_ready"), 1)
                dve.wait_ge(sem("wend_ready"), s + 1)
                v.tensor_tensor(heads(xdtw[:, g * 512:(g + 1) * 512]), heads(xdt[:, c, g * 512:(g + 1) * 512]),
                                per_head(wend[:, c, hs], SD), ALU.mult).then_inc(sem("xdtw_ready"), 1)
                sample_state(2 * s)
                key, yv = ("y", c, g), ytok[:, c, g * 512:(g + 1) * 512]
                full(dve, key)
                if c == 0:
                    free(key, v.tensor_copy(yv, bank(key)))
                    full(dve, ("kv", 0, g))
                    free(("kv", 0, g), v.tensor_copy(hst[:, g, :], bank(("kv", 0, g))))
                else:
                    full(dve, ("yi", g))
                    free(("yi", g), v.tensor_tensor(heads(yv), heads(bank(("yi", g))), per_head(eac[:, hs], SD), ALU.mult), wait=True)
                    free(key, v.tensor_tensor(yv, yv, bank(key), ALU.add))
                    if g == 0:
                        dve.wait_ge(sem("etot_ready"), 1)
                    hv = heads(hst[:, g, :])
                    step(v.tensor_tensor(hv, hv, per_head(etot[:, 8 * g:8 * g + 8], SD), ALU.mult))
                    full(dve, ("kv", 1, g))
                    free(("kv", 1, g), v.tensor_tensor(hst[:, g, :], hst[:, g, :], bank(("kv", 1, g)), ALU.add))
                sample_state(2 * s + 1)
            for t in range(KT):
                key = ("yT", t)
                full(dve, key)
                free(key, v.scalar_tensor_tensor(out=xc[:, t, 0:NP], in0=xc[:, t, 0:NP], scalar=Dcol[:, t:t + 1],
                                                 in1=bank(key)[:, 0:NP], op0=ALU.mult, op1=ALU.add), wait=(t == KT - 1))
            full(dve, ("ysT",))
            xs, dx = xc[:, 0:KT, NP:T], cst_keep[:, 0:KT * NB].rearrange("p (t b) -> p t b", t=KT)
            step(v.tensor_tensor(dx, xs, Dcol.unsqueeze(2).to_broadcast([P, KT, NB]), ALU.mult))
            free(("ysT",), v.tensor_tensor(xs, dx, bank(("ysT",))[:, 0:KT * NB].rearrange("p (t b) -> p t b", t=KT), ALU.add), wait=True)
            zy = zg[:, 0:KT, :]
            dve.wait_ge(sem("z_ready"), 1)
            step(v.tensor_tensor(zy, zy, xc[:, 0:KT, :], ALU.mult))
            v.tensor_tensor(sqb[:, :, :], zy, zy, ALU.mult).then_inc(sem("ysq_ready"), 1)
            for g in range(SG):
                taken(dve, ("yss", g))
                step(v.reciprocal(rs2[:, g, :], rs2[:, g, :]))
                for t in range(4 * g, 4 * g + 4):
                    ins = v.scalar_tensor_tensor(out=zg[:, t, :], in0=zg[:, t, :], scalar=gain("gnorm", t), in1=rs2[:, g, :],
                                                 op0=ALU.mult, op1=ALU.mult)
            step(ins)
            for i in range(8):
                kind = "q" if i < 4 else "k"
                full(dve, ("rot", i))
                v.tensor_tensor(rs2[:, 0, :], qk[:, i, :], const("cos" + kind), ALU.mult)
                free(("rot", i), v.tensor_tensor(rs2[:, 1, :], bank(("rot", i))[:, 0:T], const("sin" + kind), ALU.mult), wait=True)
                v.tensor_tensor(qk[:, i, :], rs2[:, 0, :], rs2[:, 1, :], ALU.add).then_inc(sem("rot_done"), 1)
                dve.wait_ge(sem("rot_done"), i + 1)
            for j in range(2):
                full(dve, ("vstok", j))
                free(("vstok", j), v.tensor_copy(vstok[0:NB, j * 512:(j + 1) * 512], bank(("vstok", j))[0:NB, :]))
            for c in range(NC):
                key = ("ktok", c)
                full(dve, key)
                free(key, v.tensor_tensor(heads(ktok[:, c, :]), heads(bank(key)), per_head(const("wk"), RK), ALU.mult))
            for c in range(NC):
                for j in range(2):
                    key = ("vtok", c, j)
                    full(dve, key)
                    free(key, v.tensor_copy(vtok[:, c, j * 512:(j + 1) * 512], bank(key)))

            def sample_v(b):
                key = ("vb", b)
                full(dve, key)
                dve.wait_ge(sem("r_decayed"), b + 1)
                for hh in range(4):
                    hv = rb[:, b % 4, hh * RV:(hh + 1) * RV]
                    ins = v.scalar_tensor_tensor(out=hv, in0=bank(key)[:, hh * RV:(hh + 1) * RV], scalar=qk[:, 4 + hh, NP + b:NP + b + 1],
                                                 in1=hv, op0=ALU.mult, op1=ALU.add)
                free(key, ins)

            step(v.memset(Zq[:, :, :], 0.0))
            v.tensor_copy(Zq[0:64, :, 0:NB * 2 * NB:2 * NB + 1], qk[0:64, 0:4, NP:T])
            v.tensor_copy(Zq[64:P, :, NB:NB * 2 * NB:2 * NB + 1], qk[64:P, 0:4, NP:T]).then_inc(sem("q_spread"), 1)
            dve.wait_ge(sem("ssm_p_out"), 16)
            for c in range(NC):
                for p in range(2):
                    key = ("rs", c, p)
                    full(dve, key)
                    free(key, v.tensor_tensor(S[:, 2 * c + p, :], bank(key), const("dret")[:, p * 512:(p + 1) * 512], ALU.mult))
                sample_v(2 * c)
                for p in range(2):
                    key, ov = ("ro", c, p), otok[:, c, p * 512:(p + 1) * 512]
                    if c == 0:
                        full(dve, key)
                        ins = v.tensor_copy(ov, bank(key))
                    else:
                        full(dve, ("ri", p))
                        free(("ri", p), v.tensor_tensor(heads(ov, 4), heads(bank(("ri", p)), 4),
                                                        per_head(const("gq")[:, 4 * p:4 * p + 4], RV), ALU.mult), wait=True)
                        ins = v.tensor_tensor(ov, ov, bank(key), ALU.add)
                    free(key, ins, wait=(p == 1))
                dve.sem_inc(sem("o_rows"), 1)
                key = ("rkv", c)
                full(dve, key)
                rv = rst[:, 0, :]
                if c == 0:
                    free(key, v.tensor_copy(rv, bank(key)), wait=True)
                else:
                    for hh in range(4):
                        hv = rv[:, hh * RV:(hh + 1) * RV]
                        ins = v.scalar_tensor_tensor(out=hv, in0=hv, scalar=const("gchunk")[:, hh:hh + 1],
                                                     in1=bank(key)[:, hh * RV:(hh + 1) * RV], op0=ALU.mult, op1=ALU.add)
                    free(key, ins)
                sample_v(2 * c + 1)
            for b in range(4, NB):
                sample_v(b)
                if b < 4 + NC:
                    c = b - 4
                    dve.wait_ge(sem("o_root"), c + 1)
                    step(v.reciprocal(oms[:, c, :], oms[:, c, :]))
                    v.tensor_tensor(heads(otok[:, c, :]), heads(otok[:, c, :]), per_head(oms[:, c, :], RV), ALU.mult)\
                        .then_inc(sem("o_scaled"), 1)
            dve.wait_ge(sem("g_ready"), 1)
            for h in range(RH):
                full(dve, ("oT", h))
                zo = zg[:, RH + h, 0:NP]
                free(("oT", h), v.tensor_tensor(zo, zo, bank(("oT", h))[:, 0:NP], ALU.mult))
            full(dve, ("osT",))
            os_, zs = oTt[:, :, NP:T], zg[:, RH:2 * RH, NP:T]
            free(("osT",), v.tensor_copy(os_, bank(("osT",))[:, 0:RH * NB].rearrange("p (h b) -> p h b", h=RH)), wait=True)
            v.tensor_tensor(ogs, os_, os_, ALU.mult).then_inc(sem("osq_ready"), 1)
            step(v.tensor_tensor(zs, zs, os_, ALU.mult))
            taken(dve, ("oss",))
            step(v.reciprocal(ogs, ogs))
            v.tensor_tensor(zs, zs, ogs, ALU.mult).then_inc(sem("mixed_ready"), 1)

            def memory_rows(l):
                for j in range(4):
                    key = ("mT", l, j)
                    full(dve, key)
                    free(key, v.tensor_copy(mT[:, 2 * j:2 * j + 2, :].rearrange("p t m -> p (t m)"), bank(key)), wait=True)
                    square(mT, memsq, 2 * j)
                    square(mT, memsq, 2 * j + 1)

            def memory_norm(l):
                norm(MEM_NORM[l], "mem", KT * l, mT, mT, width=ML)

            memory_rows(0)
            memory_norm(0)
            add_x("wout0")

            def cross(l):
                x_norm(CROSS_NORM[l], "cross", KT * l)
                if l:
                    dve.wait_ge(sem("odd_out"), 64)
                step(v.memset(Zp[:, :, :], 0.0))
                for t in range(KT):
                    full(dve, (f"xq{l}", t))
                    free((f"xq{l}", t), v.tensor_copy(qT[:, t, :], bank((f"xq{l}", t))[:, 0:T]))
                for j in range(2):
                    full(dve, ("qs", l, j))
                    free(("qs", l, j), v.tensor_copy(qstok[0:NB, j * 512:(j + 1) * 512], bank(("qs", l, j))[0:NB, :]))
                for lt in range(2):
                    for hp in range(2):
                        key = ("S", l, lt, hp)
                        full(dve, key)
                        c = 4 * lt + 2 * hp
                        step(v.tensor_reduce(nmx[:, c:c + 2], bank(key).rearrange("p (q m) -> p q m", q=2), AX, ALU.max))
                        v.tensor_scalar(nmx[:, c:c + 2], nmx[:, c:c + 2], -1.0 / 16, None, ALU.mult).then_inc(sem("mx_ready"), 1)
                for b in range(NB):
                    if b == NB // 2:
                        for lt in range(2):
                            for hp in range(2):
                                key = ("S", l, lt, hp)
                                taken(dve, key)
                                c = 4 * lt + 2 * hp
                                step(v.reciprocal(rsum[:, c:c + 2], rsum[:, c:c + 2]))
                                for q in range(2):
                                    ins = v.tensor_scalar(Pr[:, 2 * lt + hp, q, :], Pr[:, 2 * lt + hp, q, :], rsum[:, c + q:c + q + 1], None, ALU.mult)
                                ins.then_inc(sem("p_ready"), 1)
                    rows = kv_in(dve, l, b)
                    for j in range(2):
                        key = ("qb", l, b, j)
                        full(dve, key)
                        for m in range(2):
                            for q in range(2):
                                h = 2 * j + q
                                kh = rows[:, m, h * 256:(h + 1) * 256]
                                ins = v.tensor_tensor_reduce(kh, kh, bank(key)[:, q * 256:(q + 1) * 256], 1.0, 0.0, ALU.mult, ALU.add,
                                                             sS[:, m, b * XH + h:b * XH + h + 1])
                        free(key, ins)
                for lt in range(2):
                    for hp in range(2):
                        key = ("PT", l, lt, hp)
                        full(dve, key)
                        for q in range(2):
                            ins = v.tensor_copy(PTt[:, 2 * hp + q, :, lt * P:(lt + 1) * P],
                                                bank(key)[:, q * 256:(q + 1) * 256].rearrange("p (m i) -> p m i", m=2))
                        free(key, ins)
                key = ("sT", l)
                full(dve, key)
                step(v.tensor_reduce(nms, bank(key)[0:32, 0:ML], AX, ALU.max))
                v.tensor_scalar(nms, nms, -1.0 / 16, None, ALU.mult).then_inc(sem("smx_ready"), 1)
                taken(dve, key)
                step(v.reciprocal(rss, rss))
                v.tensor_scalar(Ps[0:32, :], Ps[0:32, :], rss, None, ALU.mult).then_inc(sem("ps_ready"), 1)
                full(dve, ("pT", l))
                for m in range(2):
                    ins = v.tensor_copy(Zp[:, m * XH:(m + 1) * XH, 0:NB * NB:NB + 1],
                                        bank(("pT", l))[:, m * 32:(m + 1) * 32].rearrange("p (b h) -> p h b", h=XH))
                free(("pT", l), ins)
                full(dve, ("aoT", l))
                free(("aoT", l), v.tensor_copy(oT[:, :, NP:T], bank(("aoT", l))[:, 0:KT * NB].rearrange("p (t b) -> p t b", t=KT)))
                add_x(f"xo{l}")

            cross(0)
            x_norm(FFN_NORM[0], "ffn", 0)
            dve.wait_ge(sem("kst"), 16)
            dve.wait_ge(sem("vst"), 16)
            for t in range(FT):
                full(dve, ("f3", t))
                taken(dve, ("f1", t))
                free(("f3", t), v.tensor_tensor(hid[:, t, :], sil[:, t % 2, :], bank(("f3", t))[:, 0:T], ALU.mult))
            memory_rows(1)
            full(dve, ("ost", 0))
            v.memset(up[:, :, 0:PST], 0.0)
            v.memset(gp[:, :, 0:CK - 1], 0.0)
            for t in range(OT):
                ins = v.tensor_copy(us[:, t, :, 0:PST], bank(("ost", 0))[:, t * 120:(t + 1) * 120].rearrange("p (b s) -> p b s", s=PST))
            free(("ost", 0), ins)
            for j in (1, 2):
                key = ("ost", j)
                full(dve, key)
                for t in range(OT):
                    ins = v.tensor_copy(gs[:, t, 4 * j - 4:4 * j, 0:CK - 1],
                                        bank(key)[:, t * 120:(t + 1) * 120].rearrange("p (b s) -> p b s", s=CK - 1))
                free(key, ins)
            memory_norm(1)
            add_x("f2")
            x_norm(ODD_NORM, "mix", KT)
            for t in range(8):
                key = ("win1", t)
                full(dve, key)
                if t < OT:
                    v.tensor_copy(us[:, t, :, PST], bank(key)[:, NP:T])
                    free(key, v.tensor_copy(up[:, t, PST:], bank(key)[:, 0:NP]), wait=True)
                else:
                    free(key, v.tensor_copy(ga[:, t - OT, :], bank(key)[:, 0:T]), wait=True)
            for t in range(OT):
                taken(dve, ("win1", 8 + t))
                v.tensor_tensor(gs[:, t, :, CK - 1], ga[:, t, NP:T], csq[:, t, NP:T], ALU.mult)
                v.tensor_tensor(gp[:, t, CK - 1:], ga[:, t, 0:NP], csq[:, t, 0:NP], ALU.mult).then_inc(sem("odd_raw"), 1)
            dve.wait_ge(sem("odd_raw"), 4)
            n_up = PST + NP
            for g, win in enumerate(WINDOWS):
                src, width, lo = up[:, g, :], 1, 0
                bufs = [w2t, w4t]
                while width < win:
                    dst = bufs[0]
                    step(v.tensor_tensor(dst[:, lo + width:n_up], src[:, lo + width:n_up], src[:, lo:n_up - width], ALU.add))
                    src, lo, width = dst, lo + width, 2 * width
                    bufs = bufs[::-1]
                u_ = up[:, g, PST:]
                step(v.scalar_tensor_tensor(out=pooled[:, g, 0:NP], in0=src[:, PST:], scalar=1.0 / win, in1=u_, op0=ALU.mult,
                                            op1=ALU.subtract))
                at = g * (PST + 1)
                step(v.tensor_tensor(prods[:, 0, 0:PST + 1], src[:, PST:2 * PST + 1], const("invcnt")[:, at:at + PST + 1], ALU.mult))
                step(v.tensor_tensor(pooled[:, g, 0:PST + 1], prods[:, 0, 0:PST + 1], u_[:, 0:PST + 1], ALU.subtract))
                step(v.tensor_reduce(prods[:, 1, 0:NB], us[:, g, :, PST + 1 - win:PST + 1], AX, ALU.add))
                v.scalar_tensor_tensor(out=pooled[:, g, NP:T], in0=prods[:, 1, 0:NB], scalar=1.0 / win, in1=us[:, g, :, PST],
                                       op0=ALU.mult, op1=ALU.subtract).then_inc(sem("pooled"), 1)
                dve.wait_ge(sem("pooled"), g + 1)
            for t in range(OT):
                cw = par[:, COL["ccw"] + t:COL["ccw"] + 4 * CK:4]
                step(v.tensor_tensor(prods[:, :, :], gs[:, t, :, :], cw.unsqueeze(1).to_broadcast([P, NB, CK]), ALU.mult))
                step(v.tensor_reduce(mixo[:, OT + t, NP:T], prods[:, :, :], AX, ALU.add))
                step(v.tensor_scalar(mixo[:, OT + t, NP:T], mixo[:, OT + t, NP:T], gain("ccb", t), None, ALU.add))
            for k in range(1, CK):
                for t in range(OT):
                    if k == 1:
                        dve.wait_ge(sem("ctap0"), t + 1)
                    else:
                        dve.wait_ge(sem("conv_taps"), OT * (k - 2) + t + 1)
                    v.scalar_tensor_tensor(out=mixo[:, OT + t, 0:NP], in0=gp[:, t, k:k + NP], scalar=gain("ccw", 4 * k + t),
                                           in1=mixo[:, OT + t, 0:NP], op0=ALU.mult, op1=ALU.add).then_inc(sem("conv_taps"), 1)
            dve.wait_ge(sem("conv_taps"), OT * (CK - 1))
            full(dve, ("mu",))
            for t in range(OT):
                ins = v.scalar_tensor_tensor(out=mixo[:, OT + t, :], in0=bank(("mu",))[:, 0:T], scalar=-1.0 / 512, in1=mixo[:, OT + t, :],
                                             op0=ALU.mult, op1=ALU.add)
            free(("mu",), ins, wait=True)
            v.tensor_tensor(csq[:, :, :], mixo[:, OT:, :], mixo[:, OT:, :], ALU.mult).then_inc(sem("csq_ready"), 1)
            taken(dve, ("var",))
            step(v.reciprocal(rstd[:], rstd[:]))
            for t in range(OT):
                v.tensor_tensor(mixo[:, OT + t, :], mixo[:, OT + t, :], rstd[:], ALU.mult).then_inc(sem("cnorm"), 1)
            add_x("wout1")
            cross(1)

            x_norm(FFN_NORM[1], "ffn", KT)
            v.memset(mx[:, 2, :], 0.0)
            v.memset(idxf[:, 2, :], 0.0)
            step(v.memset(slot[:, 2, :], -1.0))
            full(dve, ("logit",))
            for c in range(3):
                n = P if c < 2 else NB
                ins = v.tensor_copy(lg[0:n, c, :], bank(("logit",))[0:n, c * NE:(c + 1) * NE])
            free(("logit",), ins, wait=True)
            for c in range(3):
                n = P if c < 2 else NB
                step(v.max(mx[0:n, c, :], lg[0:n, c, :]))
                step(v.max_index(idx[0:n, c, :], mx[0:n, c, :], lg[0:n, c, :]))
                step(v.tensor_copy(idxf[0:n, c, :], idx[0:n, c, :]))
            v.tensor_tensor(gt[:, :, 0:1], mx[:, :, 1:2], mx[:, :, 0:1], ALU.subtract).then_inc(sem("gap_ready"), 1)
            iota8 = const("iota")[:, 0:NE].unsqueeze(1).to_broadcast([P, 3, NE])

            def each(ap):
                return ap.to_broadcast([P, 3, NE])

            v.tensor_tensor(picked[:, :, :], iota8, each(idxf[:, :, 0:1]), ALU.is_equal)
            v.tensor_tensor(lg[:, :, :], iota8, each(idxf[:, :, 1:2]), ALU.is_equal)
            dve.wait_ge(sem("gap_exp"), 1)
            step(v.tensor_scalar(gt[:, :, 2:3], gt[:, :, 1:2], 1.0, None, ALU.add))
            step(v.reciprocal(gt[:, :, 2:3], gt[:, :, 2:3]))
            step(v.tensor_tensor(gt[:, :, 3:4], gt[:, :, 1:2], gt[:, :, 2:3], ALU.mult))
            v.tensor_tensor(comb[:, :, :], picked[:, :, :], each(gt[:, :, 2:3]), ALU.mult)
            step(v.tensor_tensor(picked[:, :, :], picked[:, :, :], lg[:, :, :], ALU.add))
            step(v.tensor_tensor(lg[:, :, :], lg[:, :, :], each(gt[:, :, 3:4]), ALU.mult))
            step(v.tensor_tensor(comb[:, :, :], comb[:, :, :], lg[:, :, :], ALU.add))
            v.memset(ys[0:CAP, :], 0.0)
            v.memset(selT[0:CAP, 1, :], 0.0).then_inc(sem("picked_ready"), 1)
            full(dve, ("rank",))
            rank = bank(("rank",))
            for c in range(3):
                n = P if c < 2 else NB
                step(v.tensor_tensor(slot[0:n, c, :], rank[0:n, c * NE:(c + 1) * NE], picked[0:n, c, :], ALU.mult))
                step(v.tensor_scalar(slot[0:n, c, :], slot[0:n, c, :], -1.0, None, ALU.add))
            step(v.tensor_reduce(cnts[:, 0:1], rank[:, 3 * NE:4 * NE], AX, ALU.max))
            free(("rank",), v.tensor_scalar(cnts[:, 1:2], cnts[:, 0:1], float(CAP), float(NE // 2), ALU.is_gt, ALU.mult), wait=True)
            step(v.tensor_scalar(cnts[:, 2:3], cnts[:, 0:1], float(2 * CAP), float(NE // 2), ALU.is_gt, ALU.mult))
            step(v.scalar_tensor_tensor(out=cnts[:, 3:4], in0=cnts[:, 1:2], scalar=float(NE // 2), in1=cnts[:, 2:3],
                                        op0=ALU.add, op1=ALU.add))
            step(v.tensor_scalar(cnts[:, 2:3], cnts[:, 3:4], 2.0, -1.0, ALU.mult, ALU.add))
            v.tensor_copy(rounds[:, 0:1], cnts[:, 3:4])
            v.tensor_copy(rounds[:, 1:2], cnts[:, 2:3]).then_inc(sem("rounds_known"), 1)
            iota3 = const("iota").unsqueeze(1).to_broadcast([P, 3, CAP])

            def choose(e, link):
                at = slot[:, :, bass.ds(e, 1)] if not isinstance(e, int) else slot[:, :, e:e + 1]
                gate = comb[:, :, bass.ds(e, 1)] if not isinstance(e, int) else comb[:, :, e:e + 1]
                link(v.tensor_tensor(sel[:, :, :], iota3, at.to_broadcast([P, 3, CAP]), ALU.is_equal))
                link(v.tensor_scalar(at, at, -float(CAP), None, ALU.add))
                v.tensor_tensor(selg[:, :, :], sel[:, :, :], gate.to_broadcast([P, 3, CAP]), ALU.mult).then_inc(sem("sel_ready"), 1)

            choose(0, step)
            for c in range(3):
                n = P if c < 2 else NB
                for j in range(2):
                    key = ("htok", c, j)
                    full(dve, key)
                    free(key, v.tensor_copy(htok[0:n, c, j * 512:(j + 1) * 512], bank(key)[0:n, :]))
            full(dve, ("selT0",))
            free(("selT0",), v.tensor_copy(selT[0:CAP, 0, :], bank(("selT0",))[0:CAP, 0:T]))
            for j in range(2):
                key = ("gat0", j)
                full(dve, key)
                free(key, v.tensor_copy(hg[:, 0, 4 * j:4 * j + 4, :], bank(key)[:, 0:4 * CAP].rearrange("p (t s) -> p t s", t=4)))
            side_full = [sem("side_full6"), sem("side_full7")]
            side_taken = [sem("side_taken6"), sem("side_taken7")]
            for name in ("up_taken", "ys_ready", "side_taken6", "side_taken7"):
                dve.sem_inc(sem(name), 1)
            dve.wait_ge(sem("rounds_known"), 1)
            pairs = dve.value_load(rounds[0:1, 0:1], min_val=NE // 2, max_val=3 * NE // 2)

            def scatter_add(n):
                for t in range(KT):
                    b = t % 2
                    dve.wait_ge(side_full[b], n * (6, 5)[b] + (t // 2 + 1))
                    v.tensor_tensor(xT[:, t, :], xT[:, t, :], psum[:, 6 + b, 0:T], ALU.add).then_inc(side_taken[b], 1)

            with dve.Fori(0, pairs) as pair:
                for h in range(2):
                    n = pair * 2 + h
                    links = [0]

                    def link(ins):
                        links[0] += 1
                        ins.then_inc(sem("choose_chain"), 1)
                        dve.wait_ge(sem("choose_chain"), n * 2 + links[0])

                    dve.wait_ge(side_taken[0], n * 6 + 1)
                    choose((n + 1) & (NE - 1), link)
                    for f in range(ET):
                        dve.wait_ge(eu, n * (2 * ET) + (4 * (f // 2) + 2 + f % 2 + 1))
                        dve.wait_ge(sem("gate_taken"), n * ET + (f + 2))
                        v.tensor_tensor(ehid[:, f, :], esil[:, f % 2, :], psum[:, 2 + f % 2, 0:CAP], ALU.mult).then_inc(sem("up_taken"), 1)
                    scatter_add(n)
            scatter_add(dve.snap(pairs * 2))
            dve.wait_ge(side_taken[1], pairs * 10 + 5)
            step(v.tensor_tensor(hT[:, :, :], xT[:, :, :], xT[:, :, :], ALU.mult))
            step(v.tensor_tensor(hT[:, 0:4, :], hT[:, 0:4, :], hT[:, 4:8, :], ALU.add))
            step(v.tensor_tensor(hT[:, 0:2, :], hT[:, 0:2, :], hT[:, 2:4, :], ALU.add))
            v.tensor_tensor(hT[:, 0, :], hT[:, 0, :], hT[:, 1, :], ALU.add).then_inc(sem("sq_ready"), 1)
            norm(8, "final", 0, xT, hT, root=sem("final_root"))
            for c in range(3):
                n = P if c < 2 else NB
                dve.wait_ge(sem("final_tok"), c + 1)
                v.tensor_copy(fin[0:n, c, :], psum[0:n, 1 + 2 * c:3 + 2 * c, :].rearrange("p a b -> p (a b)")).then_inc(sem("fin_tok"), 1)


_INS = ["x_prompt", "x_sample", "state_ssm", "state_ssm_conv", "state_ret", "state_pool", "state_conv",
        "cache_mem_k", "cache_mem_v", "mem_prompt", "norm_mix", "norm_cross", "norm_ffn", "norm_mem", "norm_final",
        "w_in_even", "ssd_conv_w", "ssd_conv_b", "ssd_dt_bias", "ssd_a_log", "ssd_d", "ssd_norm", "w_out_even",
        "ffn_w1", "ffn_w3", "ffn_w2", "w_in_odd", "pool_w", "pool_scale", "conv_w", "conv_b", "conv_norm_g",
        "conv_norm_b", "w_out_odd", "router_w", "router_b", "moe_w1", "moe_w3", "moe_w2",
        "xattn_q", "xattn_k", "xattn_v", "xattn_o"]
_OUTS = [(1, NP, DM), (NB, 1, DM), (2, 1, ML, XH, 256), (2, 1, ML, XH, 256),
         (1, 1, SH, SN, SD), (1, 1, SCONV - 1, 1536), (1, 1, RH, RK, RV), (1, 1, PST, 512), (1, 1, CK - 1, 512),
         (1, NB, SH, SN, SD), (1, NB, SCONV - 1, 1536), (1, NB, RH, RK, RV), (1, NB, PST, 512), (1, NB, CK - 1, 512)]


def kernel(**inputs):
    import numpy as _np
    import concourse.bacc as _bacc
    from concourse.bass_utils import run_bass_kernel_spmd as _run

    nc = _bacc.Bacc("TRN2", target_bir_lowering=False, num_devices=1)
    arrays, w = {}, {}
    for name in _INS:
        a = _np.ascontiguousarray(inputs[name])
        arrays[f"in_{name}_dram"] = a
        w[name] = nc.dram_tensor(f"in_{name}_dram", a.shape, F32, kind="ExternalInput").ap()
    arrays["in_consts_dram"] = CONST_ARRAY
    consts = nc.dram_tensor("in_consts_dram", CONST_ARRAY.shape, F32, kind="ExternalInput").ap()
    outs = [nc.dram_tensor(f"out_{i}_dram", shape, F32, kind="ExternalOutput").ap() for i, shape in enumerate(_OUTS)]
    trunk_kernel(nc, w, consts, outs)
    r = _run(nc, [arrays], core_ids=[0])
    return tuple(r.results[0][f"out_{i}_dram"] for i in range(len(_OUTS)))
```
